# Optimizing a Trainium2 kernel written in Bass

```python
import math
import jax
import jax.numpy as jnp
from jax import lax
import numpy as np

D_MODEL = 1024
BATCH = 1
SEQ = 512
DEPTH = 2
DEC_BATCH = 8
DEC_SEQ = 1
PAST_LEN = 4096
PAGE_SIZE = 128

N_EVEN = (DEPTH + 1) // 2
N_ODD = DEPTH // 2

POOL_WINDOWS = (2, 4, 8, 16)
POOL_GROUPS = len(POOL_WINDOWS)
POOL_WIDTH = D_MODEL // 2
POOL_GW = POOL_WIDTH // POOL_GROUPS
POOL_BUF = max(POOL_WINDOWS) - 1

MLSTM_HEADS = 4
MLSTM_WIDTH = D_MODEL // 2
MLSTM_HEAD_DIM = MLSTM_WIDTH // MLSTM_HEADS
MLSTM_CHUNK = 128

MIX_WIDTH = POOL_WIDTH + MLSTM_WIDTH
IN_AB = POOL_WIDTH + 4 * MLSTM_WIDTH + 2 * MLSTM_HEADS

S5_GROUP_WIDTH = 16
S5_GROUPS = D_MODEL // S5_GROUP_WIDTH
S5_STATE = 64
S5_CHUNK = 128
S5_DT_MIN = 1e-3
S5_DT_MAX = 1e-1

MOE_GROUPS = 4
MOE_EXPERTS_PER_GROUP = 8
MOE_EXPERTS = MOE_GROUPS * MOE_EXPERTS_PER_GROUP
MOE_TOP_K = 2
MOE_HIDDEN = 256

RMS_EPS = 1e-6

kernel_name = 'hybrid_pool_mlstm_s5_hmoe_step'

def _rmsnorm(x, g):
    xf = x.astype(jnp.float32)
    y = xf * lax.rsqrt(jnp.mean(xf * xf, axis=-1, keepdims=True) + RMS_EPS) * g.astype(jnp.float32)
    return y.astype(x.dtype)

def _chunk_len(t, c):
    return c if t % c == 0 else t

def _pool_mixer(u, buf, pos, pool_w, pool_scale):
    t = u.shape[1]
    uf = u.astype(jnp.float32)
    ext = jnp.concatenate([buf.astype(jnp.float32), uf], axis=1)
    cs = jnp.cumsum(ext, axis=1)
    cs = jnp.concatenate([jnp.zeros_like(cs[:, :1]), cs], axis=1)
    means = []
    for g, w in enumerate(POOL_WINDOWS):
        c0 = g * POOL_GW
        hi = cs[:, POOL_BUF + 1:, c0:c0 + POOL_GW]
        lo = cs[:, POOL_BUF + 1 - w:POOL_BUF + 1 - w + t, c0:c0 + POOL_GW]
        cnt = jnp.minimum(w, pos + 1).astype(jnp.float32)
        means.append((hi - lo) / cnt[None, :, None])
    d = jnp.concatenate(means, axis=-1) - uf
    d = d.reshape(d.shape[:2] + (POOL_GROUPS, POOL_GW))
    y = jnp.einsum('btgc,gcd->btgd', d, pool_w.astype(jnp.float32)).reshape(uf.shape)
    return y * pool_scale.astype(jnp.float32), ext[:, -POOL_BUF:]

def _mlstm_chunk(carry, inp):
    c, n, m = carry
    q, k, v, li, lf = inp
    ln = q.shape[2]
    bcum = jnp.cumsum(lf, axis=-1)
    causal = jnp.tril(jnp.ones((ln, ln), dtype=bool))
    dmat = jnp.where(causal, bcum[..., :, None] - bcum[..., None, :] + li[..., None, :], -jnp.inf)
    inter = bcum + m[..., None]
    m_row = jnp.maximum(inter, jnp.max(dmat, axis=-1))
    w_intra = jnp.exp(dmat - m_row[..., None])
    w_inter = jnp.exp(inter - m_row)
    s = jnp.einsum('bhld,bhsd->bhls', q, k) * w_intra
    num = jnp.einsum('bhls,bhsd->bhld', s, v) + w_inter[..., None] * jnp.einsum('bhvk,bhlk->bhlv', c, q)
    den = jnp.sum(s, axis=-1) + w_inter * jnp.einsum('bhk,bhlk->bhl', n, q)
    h = num / jnp.maximum(jnp.abs(den), jnp.exp(-m_row))[..., None]
    b_end = bcum[..., -1]
    g = b_end[..., None] - bcum + li
    m_new = jnp.maximum(b_end + m, jnp.max(g, axis=-1))
    wg = jnp.exp(g - m_new[..., None])
    decay = jnp.exp(b_end + m - m_new)
    c_new = decay[..., None, None] * c + jnp.einsum('bhsv,bhsk->bhvk', v * wg[..., None], k)
    n_new = decay[..., None] * n + jnp.einsum('bhs,bhsk->bhk', wg, k)
    return (c_new, n_new, m_new), h

def _mlstm_mixer(q, k, v, o_pre, i_pre, f_pre, c0, n0, m0):
    b, t, _ = q.shape
    f32 = jnp.float32

    def heads(a):
        return a.astype(f32).reshape(b, t, MLSTM_HEADS, MLSTM_HEAD_DIM).transpose(0, 2, 1, 3)

    qh, kh, vh = heads(q), heads(k) * (MLSTM_HEAD_DIM ** -0.5), heads(v)
    li = i_pre.astype(f32).transpose(0, 2, 1)
    lf = jax.nn.log_sigmoid(f_pre.astype(f32)).transpose(0, 2, 1)
    ln = _chunk_len(t, MLSTM_CHUNK)
    nc = t // ln

    def chunks(a):
        return jnp.moveaxis(a.reshape(a.shape[:2] + (nc, ln) + a.shape[3:]), 2, 0)

    (c1, n1, m1), hs = lax.scan(
        _mlstm_chunk, (c0.astype(f32), n0.astype(f32), m0.astype(f32)),
        (chunks(qh), chunks(kh), chunks(vh), chunks(li), chunks(lf)))
    hs = jnp.moveaxis(hs, 0, 2).reshape(b, MLSTM_HEADS, t, MLSTM_HEAD_DIM)
    hs = hs.transpose(0, 2, 1, 3).reshape(b, t, MLSTM_WIDTH)
    return hs * jax.nn.sigmoid(o_pre.astype(f32)), c1, n1, m1

def _linear_combine(e1, e2):
    a1, b1 = e1
    a2, b2 = e2
    return a1 * a2, a2 * b1 + b2

def _s5_scan(u, h_re, h_im, lam_re, lam_im, log_step, b_re, b_im, c_re, c_im, d_skip):
    b, t, _ = u.shape
    f32 = jnp.float32
    uf = u.astype(f32).reshape(b, t, S5_GROUPS, S5_GROUP_WIDTH)
    lam = lax.complex(lam_re.astype(f32), lam_im.astype(f32))
    dt = jnp.exp(log_step.astype(f32))[:, None]
    lam_bar = jnp.exp(lam * dt)
    b_bar = ((lam_bar - 1.0) / lam)[..., None] * lax.complex(b_re.astype(f32), b_im.astype(f32))
    c_c = lax.complex(c_re.astype(f32), c_im.astype(f32))
    d_g = d_skip.astype(f32).reshape(S5_GROUPS, S5_GROUP_WIDTH)
    ln = _chunk_len(t, S5_CHUNK)
    nc = t // ln
    u_chunks = jnp.moveaxis(uf.reshape(b, nc, ln, S5_GROUPS, S5_GROUP_WIDTH), 1, 0)

    def body(h, u_blk):
        bu = jnp.einsum('blgc,gpc->blgp', u_blk.astype(jnp.complex64), b_bar)
        bu = bu.at[:, 0].add(lam_bar * h)
        a = jnp.broadcast_to(lam_bar, bu.shape)
        _, hs = lax.associative_scan(_linear_combine, (a, bu), axis=1)
        y = jnp.real(jnp.einsum('blgp,gcp->blgc', hs, c_c)) + d_g * u_blk
        return hs[:, -1], y

    h0 = lax.complex(h_re.astype(f32), h_im.astype(f32))
    h_last, ys = lax.scan(body, h0, u_chunks)
    y = jnp.moveaxis(ys, 0, 1).reshape(b, t, D_MODEL)
    return y, jnp.real(h_last), jnp.imag(h_last)

def _hmoe(h, w_group, b_group, w_expert, b_expert, w_gate, w_up, w_down):
    bsz, t, d = h.shape
    f32 = jnp.float32
    x = h.reshape(bsz * t, d)
    xf = x.astype(f32)
    g_logits = xf @ w_group.astype(f32) + b_group.astype(f32)
    g_prob = jax.nn.softmax(g_logits, axis=-1)
    g_sel = jnp.argmax(g_logits, axis=-1)
    g_w = jnp.take_along_axis(g_prob, g_sel[:, None], axis=-1)
    e_logits = (xf @ w_expert.astype(f32) + b_expert.astype(f32)).reshape(-1, MOE_GROUPS, MOE_EXPERTS_PER_GROUP)
    e_in = jnp.take_along_axis(e_logits, g_sel[:, None, None], axis=1)[:, 0]
    top_v, top_i = lax.top_k(e_in, MOE_TOP_K)
    top_w = jax.nn.softmax(top_v, axis=-1) * g_w
    eid = g_sel[:, None] * MOE_EXPERTS_PER_GROUP + top_i
    combine = jnp.sum(jax.nn.one_hot(eid, MOE_EXPERTS, dtype=f32) * top_w[..., None], axis=1)
    y = jnp.zeros((bsz * t, d), f32)
    for g in range(MOE_GROUPS):
        sl = slice(g * MOE_EXPERTS_PER_GROUP, (g + 1) * MOE_EXPERTS_PER_GROUP)
        hg = jnp.einsum('nd,edf->nef', x, w_gate[sl])
        hu = jnp.einsum('nd,edf->nef', x, w_up[sl])
        act = (jax.nn.silu(hg.astype(f32)) * hu.astype(f32)) * combine[:, sl, None]
        y = y + jnp.einsum('nef,efd->nd', act.astype(x.dtype), w_down[sl]).astype(f32)
    return y.reshape(bsz, t, d).astype(h.dtype)

def _trunk(x, pos, pool_st, mc_st, mn_st, mm_st, re_st, im_st, w):
    pools, mcs, mns, mms, res, ims = [], [], [], [], [], []
    o1 = POOL_WIDTH
    o2 = o1 + MLSTM_WIDTH
    o3 = o2 + MLSTM_WIDTH
    o4 = o3 + MLSTM_WIDTH
    o5 = o4 + MLSTM_WIDTH
    for l in range(DEPTH):
        h = _rmsnorm(x, w['norm_mix'][l])
        if l % 2 == 0:
            e = l // 2
            z = h @ w['w_in_ab'][e]
            gates = z[..., o5:].astype(jnp.float32) + w['b_gates'][e].astype(jnp.float32)
            pool_out, pb = _pool_mixer(z[..., :o1], pool_st[e], pos, w['pool_w'][e], w['pool_scale'][e])
            ml_out, c1, n1, m1 = _mlstm_mixer(z[..., o1:o2], z[..., o2:o3], z[..., o3:o4], z[..., o4:o5],
                                              gates[..., :MLSTM_HEADS], gates[..., MLSTM_HEADS:],
                                              mc_st[e], mn_st[e], mm_st[e])
            mix = jnp.concatenate([pool_out, ml_out], axis=-1).astype(x.dtype) @ w['w_out_ab'][e]
            pools.append(pb)
            mcs.append(c1)
            mns.append(n1)
            mms.append(m1)
        else:
            o = l // 2
            y, r, i = _s5_scan(h, re_st[o], im_st[o], w['s5_lam_re'][o], w['s5_lam_im'][o], w['s5_log_step'][o],
                               w['s5_b_re'][o], w['s5_b_im'][o], w['s5_c_re'][o], w['s5_c_im'][o], w['s5_d'][o])
            ag = jax.nn.gelu(y).astype(x.dtype) @ w['w_glu'][o]
            mix = ag[..., :D_MODEL] * jax.nn.sigmoid(ag[..., D_MODEL:])
            res.append(r)
            ims.append(i)
        x = x + mix.astype(x.dtype)
        x = x + _hmoe(_rmsnorm(x, w['norm_ffn'][l]), w['moe_w_group'][l], w['moe_b_group'][l],
                      w['moe_w_expert'][l], w['moe_b_expert'][l], w['moe_w_gate'][l],
                      w['moe_w_up'][l], w['moe_w_down'][l])
    return (_rmsnorm(x, w['norm_final']), jnp.stack(pools), jnp.stack(mcs), jnp.stack(mns),
            jnp.stack(mms), jnp.stack(res), jnp.stack(ims))

def setup_inputs(seed: int = 0) -> dict:
    key = jax.random.key(seed)
    ks = list(jax.random.split(key, 40))
    f32 = jnp.float32
    nrm = lambda shape, scale: scale * jax.random.normal(ks.pop(), shape, f32)
    H = MLSTM_HEADS
    b_gates = jnp.concatenate([nrm((N_EVEN, H), 0.1),
                               jnp.linspace(3.0, 6.0, H, dtype=f32)[None] + nrm((N_EVEN, H), 0.1)], axis=-1)
    lam_re = -0.5 + nrm((N_ODD, S5_GROUPS, S5_STATE), 0.01)
    lam_im = jnp.pi * jnp.arange(S5_STATE, dtype=f32)[None, None] + nrm((N_ODD, S5_GROUPS, S5_STATE), 0.01)
    log_step = jax.random.uniform(ks.pop(), (N_ODD, S5_GROUPS), f32,
                                  minval=math.log(S5_DT_MIN), maxval=math.log(S5_DT_MAX))
    return {
        'x_prompt': nrm((BATCH, SEQ, D_MODEL), 1.0),
        'x_sample': nrm((DEC_BATCH, DEC_SEQ, D_MODEL), 1.0),
        'state_pool': nrm((N_EVEN, DEC_BATCH, POOL_BUF, POOL_WIDTH), 1.0),
        'state_mlstm_c': nrm((N_EVEN, DEC_BATCH, H, MLSTM_HEAD_DIM, MLSTM_HEAD_DIM), 0.1),
        'state_mlstm_n': nrm((N_EVEN, DEC_BATCH, H, MLSTM_HEAD_DIM), 0.1),
        'state_mlstm_m': nrm((N_EVEN, DEC_BATCH, H), 1.0),
        'state_s5_re': nrm((N_ODD, DEC_BATCH, S5_GROUPS, S5_STATE), 0.1),
        'state_s5_im': nrm((N_ODD, DEC_BATCH, S5_GROUPS, S5_STATE), 0.1),
        'norm_mix': 1.0 + nrm((DEPTH, D_MODEL), 0.02),
        'norm_ffn': 1.0 + nrm((DEPTH, D_MODEL), 0.02),
        'norm_final': 1.0 + nrm((D_MODEL,), 0.02),
        'w_in_ab': nrm((N_EVEN, D_MODEL, IN_AB), D_MODEL ** -0.5),
        'b_gates': b_gates,
        'pool_w': nrm((N_EVEN, POOL_GROUPS, POOL_GW, POOL_GW), POOL_GW ** -0.5),
        'pool_scale': 1.0 + nrm((N_EVEN, POOL_WIDTH), 0.02),
        'w_out_ab': nrm((N_EVEN, MIX_WIDTH, D_MODEL), MIX_WIDTH ** -0.5),
        's5_lam_re': lam_re,
        's5_lam_im': lam_im,
        's5_log_step': log_step,
        's5_b_re': nrm((N_ODD, S5_GROUPS, S5_STATE, S5_GROUP_WIDTH), (2 * S5_GROUP_WIDTH) ** -0.5),
        's5_b_im': nrm((N_ODD, S5_GROUPS, S5_STATE, S5_GROUP_WIDTH), (2 * S5_GROUP_WIDTH) ** -0.5),
        's5_c_re': nrm((N_ODD, S5_GROUPS, S5_GROUP_WIDTH, S5_STATE), (S5_STATE / 4) ** -0.5),
        's5_c_im': nrm((N_ODD, S5_GROUPS, S5_GROUP_WIDTH, S5_STATE), (S5_STATE / 4) ** -0.5),
        's5_d': nrm((N_ODD, D_MODEL), 0.5),
        'w_glu': nrm((N_ODD, D_MODEL, 2 * D_MODEL), D_MODEL ** -0.5),
        'moe_w_group': nrm((DEPTH, D_MODEL, MOE_GROUPS), D_MODEL ** -0.5),
        'moe_b_group': nrm((DEPTH, MOE_GROUPS), 0.01),
        'moe_w_expert': nrm((DEPTH, D_MODEL, MOE_EXPERTS), D_MODEL ** -0.5),
        'moe_b_expert': nrm((DEPTH, MOE_EXPERTS), 0.01),
        'moe_w_gate': nrm((DEPTH, MOE_EXPERTS, D_MODEL, MOE_HIDDEN), D_MODEL ** -0.5),
        'moe_w_up': nrm((DEPTH, MOE_EXPERTS, D_MODEL, MOE_HIDDEN), D_MODEL ** -0.5),
        'moe_w_down': nrm((DEPTH, MOE_EXPERTS, MOE_HIDDEN, D_MODEL), MOE_HIDDEN ** -0.5),
    }

def reference(x_prompt, x_sample, state_pool, state_mlstm_c, state_mlstm_n, state_mlstm_m,
              state_s5_re, state_s5_im, norm_mix, norm_ffn, norm_final, w_in_ab, b_gates, pool_w,
              pool_scale, w_out_ab, s5_lam_re, s5_lam_im, s5_log_step, s5_b_re, s5_b_im, s5_c_re,
              s5_c_im, s5_d, w_glu, moe_w_group, moe_b_group, moe_w_expert, moe_b_expert,
              moe_w_gate, moe_w_up, moe_w_down):
    w = dict(norm_mix=norm_mix, norm_ffn=norm_ffn, norm_final=norm_final, w_in_ab=w_in_ab,
             b_gates=b_gates, pool_w=pool_w, pool_scale=pool_scale, w_out_ab=w_out_ab,
             s5_lam_re=s5_lam_re, s5_lam_im=s5_lam_im, s5_log_step=s5_log_step, s5_b_re=s5_b_re,
             s5_b_im=s5_b_im, s5_c_re=s5_c_re, s5_c_im=s5_c_im, s5_d=s5_d, w_glu=w_glu,
             moe_w_group=moe_w_group, moe_b_group=moe_b_group, moe_w_expert=moe_w_expert,
             moe_b_expert=moe_b_expert, moe_w_gate=moe_w_gate, moe_w_up=moe_w_up, moe_w_down=moe_w_down)
    f32 = jnp.float32
    bp, tp = x_prompt.shape[0], x_prompt.shape[1]
    ts = x_sample.shape[1]
    pos_p = jnp.arange(tp, dtype=jnp.int32)
    pos_s = PAST_LEN + jnp.arange(ts, dtype=jnp.int32)
    z_pool = jnp.zeros((N_EVEN, bp, POOL_BUF, POOL_WIDTH), f32)
    z_c = jnp.zeros((N_EVEN, bp, MLSTM_HEADS, MLSTM_HEAD_DIM, MLSTM_HEAD_DIM), f32)
    z_n = jnp.zeros((N_EVEN, bp, MLSTM_HEADS, MLSTM_HEAD_DIM), f32)
    z_m = jnp.zeros((N_EVEN, bp, MLSTM_HEADS), f32)
    z_s5 = jnp.zeros((N_ODD, bp, S5_GROUPS, S5_STATE), f32)
    y_prompt, pool_p, c_p, n_p, m_p, re_p, im_p = _trunk(x_prompt, pos_p, z_pool, z_c, z_n, z_m, z_s5, z_s5, w)
    y_sample, pool_s, c_s, n_s, m_s, re_s, im_s = _trunk(x_sample, pos_s, state_pool, state_mlstm_c,
                                                         state_mlstm_n, state_mlstm_m, state_s5_re,
                                                         state_s5_im, w)
    return (y_prompt, y_sample, pool_p, c_p, n_p, m_p, re_p, im_p, pool_s, c_s, n_s, m_s, re_s, im_s)


_drawn_inputs = setup_inputs


def setup_inputs(seed=0):
    import zlib

    import numpy as np

    out = dict(_drawn_inputs(seed))
    spreads = {}
    factors = {'norm_final': 2.829, 's5_lam_re': 4.011, 'moe_b_group': 3.569, 'moe_b_expert': 3.498}
    for name, (base, spread) in spreads.items():
        noise = np.random.default_rng([zlib.crc32(name.encode()), seed]).standard_normal(out[name].shape)
        drawn = base * np.exp(spread * noise) if base else spread * noise
        out[name] = jnp.asarray(drawn.astype(out[name].dtype))
    for name, factor in factors.items():
        out[name] = (out[name] * factor).astype(out[name].dtype)
    return out
```

```python
from contextlib import ExitStack
from math import pi

import numpy as np

import concourse.bass as bass
from concourse import mybir

F32 = mybir.dt.float32
I32 = mybir.dt.int32
ALU = mybir.AluOpType
ACT = mybir.ActivationFunctionType
AX = mybir.AxisListType.X

P = 128
D = 1024
KC = D // P
SEQ = 512
NS = 8
NT = SEQ + NS
TILES = SEQ // P
ROWS = [P] * TILES + [NS]
HALF = NT // 2
H = 4
GU = 64
PAIRS = GU // 2
CW = 16
L = P // CW
NCH = SEQ // L
UC = NS + NCH + NS
SC = NCH + NS
E = 32
CAP = 64
ROUNDS = -(-NT // CAP)
EPS = 1e-6
NORM = {0: 0, 1: 1, 3: 2, 4: 3}
BIG = 1e30
KSCALE = float(P) ** -0.5
KROW = 2 * P - CW
KZERO = KROW - P

CONST = {}
_at = 0
for _name, _n in [("ident", P), ("before", P), ("ones", P), ("causal", P), ("window", 4 * NS),
                  ("iota", P), ("eio", E), ("reve", E), ("revg", 4), ("tokid", 5), ("valid", 5),
                  ("half", 1), ("ramp", 4 * CW), ("head", 4 * P), ("keep", SEQ), ("diag", CW)]:
    CONST[_name] = (_at, _n)
    _at += _n
CONSTS = _at


def constants():
    c = np.zeros((P, CONSTS), np.float32)

    def put(name, a):
        at, n = CONST[name]
        c[:a.shape[0], at:at + n] = a.reshape(a.shape[0], n)

    p = np.arange(P)
    put("ident", np.eye(P, dtype=np.float32))
    put("before", (p[:, None] < p[None, :]).astype(np.float32))
    put("ones", np.ones((P, P), np.float32))
    put("causal", np.where(p[:, None] <= p[None, :], 0.0, -BIG).astype(np.float32))
    w = np.zeros((120, 4, NS), np.float32)
    for g in range(4):
        for n in range(NS):
            w[n * 15 + 15 - (2 ** (g + 1) - 1):n * 15 + 15, g, n] = 1.0
    put("window", w)
    put("iota", np.tile(np.arange(CAP, dtype=np.float32), (P, 2)))
    put("eio", np.tile(np.arange(E, dtype=np.float32), (P, 1)))
    put("reve", np.tile(E - np.arange(E, dtype=np.float32), (P, 1)))
    put("revg", np.tile(4 - np.arange(4, dtype=np.float32), (P, 1)))
    put("tokid", (np.arange(5)[None, :] * P + p[:, None] + 1).astype(np.float32))
    v = np.ones((P, 5), np.float32)
    v[NS:, 4] = 0
    put("valid", v)
    put("half", (p[:, None] >= CAP).astype(np.float32) - 2.0)
    t = np.arange(CW)
    put("ramp", np.tile(np.stack([1.0 / np.minimum(2 ** (g + 1), t + 1) for g in range(4)])[None],
                        (P, 1, 1)).astype(np.float32))
    h = np.zeros((4, 4, P), np.float32)
    for i in range(4):
        h[i, i] = 1.0
    put("head", h)
    k = np.ones((4, SEQ), np.float32)
    k[:, ::P] = 0
    put("keep", k)
    put("diag", (p[:, None] % CW == t[None, :]).astype(np.float32))
    return c


X_AT = 0
CONST_AT = X_AT + 5 * D
GB_AT = CONST_AT + CONSTS + CONSTS % 2
WR_AT = GB_AT + D
SMALL_AT = WR_AT + 2 * (KC * 36 + 36)
STAGE_AT = SMALL_AT + 2198
ARENA = 207 * 256


class PsumRing:

    def __init__(self, jobs, full, freed):
        self.jobs, self.full, self.freed = jobs, full, freed
        self.at = {name: n for n, (name, _) in enumerate(jobs)}
        assert len(self.at) == len(jobs)
        seen, self.count = {}, []
        for _, eng in jobs:
            seen[eng] = seen.get(eng, 0) + 1
            self.count.append(seen[eng])

    def slot(self, *name):
        return self.at[name] % 4

    def wait_free(self, pe, *name):
        n = self.at[name]
        if n >= 4:
            self.wait_emptied(pe, *self.jobs[n - 4][0])

    def wait_full(self, eng, *name):
        eng.wait_ge(self.full, self.at[name] + 1)

    def wait_emptied(self, eng, *name):
        n = self.at[name]
        eng.wait_ge(self.freed[self.jobs[n][1]], self.count[n])


def jobs_of_kernel():
    j = []
    for i in range(5):
        j.append((("ht", i), "act" if i % 2 else "dve"))
    j.append((("gates",), "dve"))
    for n in range(12):
        j.append((("z", n), "act"))
    j += [(("cols",), "dve"), (("sg",), "dve")]
    j += [(("bc", h), "dve") for h in range(H)]
    j += [(("st",), "dve")]
    for c in range(TILES):
        j += [(("kt", c), "dve"), (("s", c), "dve"), (("kv", c), "dve")]
    j += [(("z", n), "act") for n in range(12, 20)]
    j += [(("ws",), "dve")]
    for c in range(TILES):
        j += [(("num", c), "dve"), (("hT", c), "dve")]
    j += [(("pw", g), "act") for g in range(4)]
    j += [(("wo", i), "dve") for i in range(5)]

    def router(l):
        return [((k, l, i), e) for i in range(5) for k, e in (("tr", "act"), ("lg", "dve"))] + [(("pos", l), "dve")]
    j += router(0)
    j += [(("k",), "dve")]
    j += [(("mt", q), "act") for q in range(8)]
    j += [(("u", q), "act" if q % 2 else "dve") for q in range(8)]
    j += [(("zs", q), "dve") for q in range(8)]
    j += [(("y", q), "act" if q % 2 else "dve") for q in range(8)]
    j += [(("yT", q), "act") for q in range(8)]
    j += [(("gl", i, ch), "dve") for i in range(5) for ch in range(2)]
    j += router(1)
    return j


def bass_hybrid_step(nc, T):
    ctx = ExitStack()
    with ctx:
        sems = {}

        def sem(name):
            if name not in sems:
                sems[name] = ctx.enter_context(nc.semaphore(name))
            return sems[name]

        arena = ctx.enter_context(nc.sbuf_tensor("arena", [P, ARENA], F32))
        idx_list = ctx.enter_context(nc.sbuf_tensor("idx_list", [P, E], I32))
        idx_now = ctx.enter_context(nc.sbuf_tensor("idx_now", [P, 2], I32))
        idx_back = ctx.enter_context(nc.sbuf_tensor("idx_back", [P, 10], I32))
        most = ctx.enter_context(nc.sbuf_tensor("most", [P, 2], I32))
        ps = ctx.enter_context(nc.psum_tensor("ps", [P, 8, 512], F32))

        def place(at, *shape, parts=P, base=0):
            n = int(np.prod(shape))
            assert at + n <= ARENA
            a = arena[base:base + parts, at:at + n]
            if len(shape) == 2:
                a = a.rearrange("p (a b) -> p a b", a=shape[0])
            if len(shape) == 3:
                a = a.rearrange("p (a b c) -> p a b c", a=shape[0], b=shape[1])
            if len(shape) == 4:
                a = a.rearrange("p (a b c d) -> p a b c d", a=shape[0], b=shape[1], c=shape[2])
            return a

        def const(name, parts=P):
            at, n = CONST[name]
            return arena[0:parts, CONST_AT + at:CONST_AT + at + n]

        def spread(a, n):
            a = a.unsqueeze(len(a.shape))
            return a.broadcast_to(tuple(a.shape[:-1]) + (n,))

        def spread_mid(a, n):
            a = a.unsqueeze(1)
            return a.broadcast_to((a.shape[0], n) + tuple(a.shape[2:]))

        ident, before, ones, causal = const("ident"), const("before"), const("ones"), const("causal")

        X = place(X_AT, 5, D)
        GB = place(GB_AT, D)
        WR = [place(WR_AT + l * (KC * 36 + 36), KC, 36) for l in range(2)]
        BR = [place(WR_AT + l * (KC * 36 + 36) + KC * 36, 36) for l in range(2)]

        small_at = [SMALL_AT]

        def small(*shape, parts=P):
            at = small_at[0]
            small_at[0] += int(np.prod(shape))
            assert small_at[0] <= STAGE_AT
            return place(at, *shape, parts=parts)

        ss, var, root, rstd = small(5), small(5), small(5), small(5)
        LG = small(5, 36)
        gmax, gtop, gsum, gw = small(5), small(5), small(5), small(5)
        og, gexp, gneg = small(5, 4), small(5, 4), small(5, 4)
        me, hit = small(5, E), small(5, E)
        oh = [small(5, E), small(5, E)]
        OH, PRE, POS = small(5, E), small(5, E), small(5, E)
        both = small(E)
        m1, m2, etop, dexp, dsum = small(5), small(5), small(5), small(5), small(5)
        pw_ = [small(5), small(5)]
        RK, EID, QR = small(2, 5), small(2, 5), small(2, 5)
        cntmax = small(1)
        m0s, SG, SM = small(H, parts=NS), small(8, parts=NS), small(12, parts=NS)
        gcol, dec = small(16), small(16)
        ecol = small(16)
        den, dab, rden = small(H), small(H), small(H)
        vs, us, sos = small(H, NS), small(H, NS), small(H, NS)
        rs = small(NS * H)
        bg, mrun = small(2, parts=H), small(TILES + 1, parts=H)
        pscale = small(H)
        sden = small(3 * H, parts=NS)
        ssk = small(L, parts=UC)

        A = STAGE_AT

        def slot(*name):
            s = ring.slot(*name)
            return ps[:, 2 * s:2 * s + 2, :]

        def slot_flat(*name):
            return slot(*name).rearrange("p b n -> p (b n)")

        ring = PsumRing(jobs_of_kernel(), sem("psum_full"),
                        {"dve": sem("psum_emptied_by_dve"), "act": sem("psum_emptied_by_act")})

        def take(eng, *name):
            ring.wait_full(eng, *name)

        def give(eng, ins, *name):
            who = ring.jobs[ring.at[name]][1]
            ins.then_inc(ring.freed[who], 1)
            ring.wait_emptied(eng, *name)

        HH = place(A, 5, D)
        KB = place(A, NS * H, P)
        HT = place(A + 5120, KC, NT)
        WIN = [place(A + 9280 + 2048 * b, KC, 256) for b in range(2)]
        WG8 = place(A + 40000, KC, 8)
        WOUT = place(A + 5120, KC, D)
        Zk, Zq, Zv, Zo = (place(A + 13376 + 2080 * n, H, NT) for n in range(4))
        MIX = place(A + 13376, KC, NT)
        HM = place(A + 17536, 2, H, P)
        UE = place(A + 21696, H, 528)
        W = place(A + 23808, H, TILES, P)
        KT = place(A + 25856, TILES, H, P)
        DT = place(A + 25856, H, NT)
        V1 = place(A + 27936, TILES, H, 130)
        QT = place(A + 30016, H, SEQ)
        CN = place(A + 32064, TILES, H, 129)
        TU = [place(A + 34128 + 528 * b, 528) for b in range(2)]
        rows = [place(A + 35184 + NT * n, NT, parts=H) for n in range(8)]
        li, lf, bc_, ar, mr, wi, er, tr_ = rows
        CS = place(A + 35184, NS * H, P)
        PW = place(A + 39344, H, P)
        PB = place(A + 34128, SEQ, parts=120)
        ks = place(A + 40500, H, P, parts=NS)
        n0s = place(A + 41012, H, P, parts=NS)
        qs = place(A + 1536, H, P, parts=NS)
        DB = place(A + 41524, NS * H)

        WGU = [place(A + 4096 * b, KC, 512) for b in range(2)]
        WD = [place(A + 8192 + 2048 * b, 2, D) for b in range(2)]
        XG = [place(A + 12288 + 512 * b, 512) for b in range(2)]
        XT = [place(A + 13312 + 512 * b, 4, P) for b in range(2)]
        SIL = [place(A + 14336 + P * b, P) for b in range(2)]
        ACTB = [place(A + 14592 + P * b, P) for b in range(2)]
        AT = [place(A + 14848 + P * b, P) for b in range(2)]
        YE = [place(A + 15104 + 512 * b, 512) for b in range(2)]
        OHR = place(A + 16128, 10, P)
        YG = place(A + 17408, 10, D)
        HB = place(A + 27648, 5, D)
        HTB = [place(A + 32768 + 1024 * b, KC, P) for b in range(2)]

        HC = place(A + 27648, 5, D)
        U = place(A, GU, UC)
        XK = place(A + 5120, L, D, parts=UC)
        RR, RI = place(A + 5120, PAIRS, NCH), place(A + 7168, PAIRS, NCH)
        HR, HI = place(A + 9216, PAIRS, SC), place(A + 11520, PAIRS, SC)
        CIN = [place(A + 5120 + 512 * n, PAIRS, CW) for n in range(4)]
        BD = [place(A + 7168 + 1024 * n, PAIRS, 2 * CW) for n in range(2)]
        KS = place(A + 9216, KC, P)
        T1, T2 = place(A + 10240, PAIRS, CW), place(A + 10752, PAIRS, CW)
        KZ = place(A + 11264, KC, KZERO)
        DSK = place(A + 12160, KC)
        VR, VI = place(A + 13824, PAIRS, L, CW), place(A + 17920, PAIRS, L, CW)
        TC, TS = place(A + 13824, PAIRS, NCH), place(A + 15872, PAIRS, NCH)
        R8, TMP = place(A + 17920, PAIRS, NCH), place(A + 19968, PAIRS, NCH)
        XR = [place(A + 19968 + 1024 * b, D, parts=UC) for b in range(2)]
        YK = place(A + 13824, L, D)
        M = place(A + 22016, PAIRS, 2, P)
        TT = place(A + 22016, GU, P)
        GR, GI = place(A + 30208, PAIRS, L + 1, CW), place(A + 34816, PAIRS, L + 1, CW)
        PWR, PWI = place(A + 39424, L + 1, PAIRS), place(A + 39424 + 288, L + 1, PAIRS)
        BBR, BBI = place(A + 40000, PAIRS, CW), place(A + 40512, PAIRS, CW)
        sp_ = [place(A + 41024 + 32 * n, PAIRS) for n in range(20)]
        H0R, H0I = place(A + 41632, PAIRS * NS), place(A + 41888, PAIRS * NS)
        SHR, SHI, SHT = (place(A + 40000 + 256 * n, PAIRS, NS) for n in range(3))
        HEND = place(A + 39424, 2, PAIRS)
        YT = place(A, KC, NT)
        WGL = [place(A + 22016 + 8192 * ch, KC, D) for ch in range(2)]
        SIG = [place(A + 5120 + 512 * b, 512) for b in range(2)]
        GT = [place(A + 6144 + 512 * b, 512) for b in range(2)]

        def y_views(q, b):
            return (YK[0:SC, :, q * P:(q + 1) * P].rearrange("p l (j b c) -> p b j l c", b=2, c=CW)[:, b],
                    slot("y", q)[0:SC, b, :].rearrange("p (j l c) -> p j l c", j=4, l=L))

        hd, yd, kp = T["hd"], T["yd"], T["kp"]
        sdk, sdq, sdd = T["sdk"], T["sdq"], T["sdd"]
        hd_halves = hd.rearrange("t (h c) -> (t h) c", h=2)
        yd_rows = yd.rearrange("j t c -> (j t) c")

        block = ctx.enter_context(nc.Block())

        def tile_rows(a, i):
            return a[0:ROWS[i], i, :]

        @block.sync
        def _(sp):
            def load(dst, src, name):
                sp.dma_start(dst, src).then_inc(sem(name), 16)

            load(place(CONST_AT, CONSTS), T["const"], "consts")
            for i in range(TILES):
                load(X[:, i, :], T["x_prompt"][i * P:(i + 1) * P, :], f"x_in_{i}")
            sp.wait_ge(sem("x_cleared"), 1)
            load(X[0:NS, TILES, :], T["x_sample"], f"x_in_{TILES}")
            load(GB, T["norms"][0], "norm_in")
            load(WG8, T["w_gate8"], "w_gates_in")
            load(bg, T["b_gates"], "small_in")
            load(m0s, T["m0"], "small_in")
            load(pscale, T["pool_scale"], "small_in")
            for l in range(2):
                load(WR[l], T["w_router"][l], "small_in")
                load(BR[l], T["b_router"][l], "small_in")
            load(PW, T["pool_w"], "pool_in")
            load(PB, T["pool_rows"], "pool_in")
            load(n0s, T["n0"], "n0_in")
            for n in range(10):
                if n >= 2:
                    ring.wait_full(sp, "z", 2 * (n - 2) + 1)
                load(WIN[n % 2], T["w_in"][n], f"w_in_{n % 2}")
            sp.dma_start(T["pool_s"], T["pool_buf"]).then_inc(sem("stored"), 16)
            sp.wait_ge(sem("rows_dead"), 1)
            load(CS, T["c0"], "c0_in")
            ring.wait_full(sp, "z", 19)
            load(WOUT, T["w_out"], "w_out_in")
            sp.wait_ge(sem("ks_ready"), 1)
            sp.dma_start(sdk, ks.rearrange("p h k -> p (h k)")).then_inc(sem("sd_out"), 16)
            sp.dma_start(sdd, SM[:, 0:H]).then_inc(sem("sd_out"), 16)
            sp.dma_start(sdq, qs.rearrange("p h k -> p (h k)")).then_inc(sem("sd_out"), 16)
            sp.dma_start(T["n_s"], n0s.rearrange("p h k -> p (h k)")).then_inc(sem("stored"), 16)
            sp.dma_start(T["m_s"], sden[:, 0:H]).then_inc(sem("stored"), 16)
            sp.wait_ge(sem("sd_out"), 48)
            load(KB, sdk.rearrange("n (h k) -> (n h) k", h=H).partition_broadcast(P), "kb_in")
            load(DB, sdd.rearrange("n h -> (n h)").partition_broadcast(P), "kb_in")
            sp.wait_ge(sem("kb_used"), 1)
            load(KB, sdq.rearrange("n (h k) -> (n h) k", h=H).partition_broadcast(P), "qb_in")
            sp.wait_ge(sem("cs_ready"), 1)
            sp.dma_start(T["c_s"], CS).then_inc(sem("stored"), 16)
            sp.wait_ge(sem("us_ready"), 1)
            sp.dma_start(T["pool_p"], UE[:, :, 528 - 15:528]).then_inc(sem("stored"), 16)
            sp.dma_start(T["pool_us"], us).then_inc(sem("stored"), 16)
            sp.wait_ge(sem("cn_ready"), 1)
            sp.dma_start(T["cn_p"], CN[:, TILES - 1]).then_inc(sem("stored"), 16)
            sp.dma_start(T["m_p"], mrun[:, TILES:TILES + 1]).then_inc(sem("stored"), 16)

            def experts(l):
                def turns(r):
                    with sp.Fori(0, E // 2) as k:
                        t = k + 16 * r
                        for s in range(2):
                            sp.wait_ge(sem(f"gu_done_{l}"), 2 * t + 2)
                            e = 2 * k + s
                            sp.dma_start(WGU[s], T["w_gu"][l][bass.ds(e, 1)].rearrange("e p k n -> p (e k) n")
                                         ).then_inc(sem(f"wgu_in_{l}_{s}"), 16)
                        for s in range(2):
                            sp.wait_ge(sem(f"down_done_{l}"), 2 * t + 2)
                            e = 2 * k + s
                            sp.dma_start(WD[s], T["w_down"][l][bass.ds(e, 1)].rearrange("e p k n -> p (e k) n")
                                         ).then_inc(sem(f"wd_in_{l}_{s}"), 16)
                turns(0)
                sp.wait_ge(sem("most_ready"), l + 1)
                n = sp.value_load(most[0:1, l:l + 1], min_val=0, max_val=NT)
                with sp.Fori(1, ROUNDS) as r:
                    with sp.If(n > r * CAP):
                        turns(r)

            sp.wait_ge(sem("x_mixed"), 1)
            load(GB, T["norms"][1], "norm_in")
            experts(0)
            sp.wait_ge(sem("x_moe"), 1)
            load(GB, T["norms"][2], "norm_in")
            for n in range(4):
                load(CIN[n], T["s5_cb"][n], "s5_in")
            load(sp_[0], T["s5_ls"], "s5_in")
            load(sp_[1], T["s5_lr"], "s5_in")
            load(sp_[2], T["s5_li"], "s5_in")
            load(DSK, T["s5_d"], "s5_in")
            load(H0R, T["s5_h0r"], "s5_in")
            load(H0I, T["s5_h0i"], "s5_in")
            sp.wait_ge(sem("taps_ready"), 1)
            kv = kp.rearrange("(b p) n -> p b n", p=P)
            sp.dma_start(kv[:, :, KZERO:KROW], KS).then_inc(sem("taps_out"), 16)
            sp.dma_start(kv[:, :, 0:KZERO], KZ).then_inc(sem("taps_out"), 16)
            sp.wait_ge(sem("taps_out"), 32)
            sp.wait_ge(sem("x1_out"), 80)
            sp.wait_ge(sem("xk_cleared"), 1)
            load(XK[NS:NS + NCH], hd[0:SEQ, :].rearrange("(k l) c -> k l c", l=L), "xk_in")
            load(XK[0:NS, L - 1, :], hd[SEQ:NT, :], "xk_in")
            load(XK[NS + NCH:UC, 0, :], hd[SEQ:NT, :], "xk_in")
            ring.wait_full(sp, "zs", 7)
            kg = kp.rearrange("(g c) n -> c g n", c=CW)
            for s in range(L):
                load(TT[CW * s:CW * s + CW], kg[:, :, KZERO - CW * s:KZERO - CW * s + P], "taps_in")
            sp.wait_ge(sem("s5_end"), 1)
            sp.dma_start(T["s5_p"], HEND).then_inc(sem("stored"), 16)
            sp.dma_start(T["s5_sr"], SHR).then_inc(sem("stored"), 16)
            sp.dma_start(T["s5_si"], SHI).then_inc(sem("stored"), 16)
            ring.wait_full(sp, "y", 7)
            for ch in range(2):
                load(WGL[ch], T["w_glu"][ch], f"w_glu_in_{ch}")
            sp.wait_ge(sem("x_mixed"), 2)
            load(GB, T["norms"][3], "norm_in")
            experts(1)
            sp.wait_ge(sem("x_moe"), 2)
            load(GB, T["norms"][4], "norm_in")
            for i in range(5):
                sp.wait_ge(sem("h_4"), i + 1)
                sp.dma_start(T["y"][i * P:i * P + ROWS[i], :], tile_rows(HC, i)).then_inc(sem("stored"), 16)
            sp.wait_ge(sem("stored"), 16 * (1 + 2 + 1 + 2 + 2 + 3 + 5))

        @block.tensor
        def _(pe):
            def full(mm):
                mm.then_inc(ring.full, 1)

            def transposes(name, pieces):
                ring.wait_free(pe, *name)
                for out, in_ in pieces:
                    k = in_.shape[0]
                    mm = pe.transpose(out, in_, ident[0:k, 0:k])
                full(mm)

            for l in range(2):
                for name in ("gu_done", "down_done", "xt_done"):
                    pe.sem_inc(sem(f"{name}_{l}"), 2)
            pe.wait_ge(sem("consts"), 16)
            for i in range(5):
                n = ROWS[i]
                pe.wait_ge(sem("h_0"), i + 1)
                o = slot("ht", i)
                transposes(("ht", i), [(o[:, kc // 4, (kc % 4) * P:(kc % 4) * P + n], HH[0:n, i, kc * P:(kc + 1) * P])
                                       for kc in range(KC)])
            pe.wait_ge(sem("w_gates_in"), 16)
            for i in range(5):
                ring.wait_emptied(pe, "ht", i)
            ring.wait_free(pe, "gates")
            o = slot("gates")
            for b in range(2):
                for kc in range(KC):
                    for q in range(2):
                        mm = pe.matmul(o[32 * q:32 * q + H, b, 0:HALF], WG8[:, kc, H * q:H * q + H],
                                       HT[:, kc, b * HALF:(b + 1) * HALF], start=kc == 0, stop=kc == KC - 1)
            full(mm)

            def project(n):
                if n % 2 == 0:
                    pe.wait_ge(sem(f"w_in_{(n // 2) % 2}"), 16 * (n // 4 + 1))
                ring.wait_free(pe, "z", n)
                o = slot("z", n)
                w = WIN[(n // 2) % 2]
                for kc in range(KC):
                    for b in range(2):
                        mm = pe.matmul(o[:, b, 0:HALF], w[:, kc, (n % 2) * P:(n % 2 + 1) * P],
                                       HT[:, kc, b * HALF:(b + 1) * HALF], start=kc == 0, stop=kc == KC - 1)
                full(mm)

            for n in range(12):
                project(n)
            pe.wait_ge(sem("gate_rows"), 1)
            o = slot_flat("cols")
            transposes(("cols",), [(o[:, 16 * q + H * c:16 * q + H * c + H], (ar, er)[q][:, c * P:(c + 1) * P])
                                   for q in range(2) for c in range(TILES)])
            o = slot_flat("sg")
            transposes(("sg",), [(o[0:NS, 0:H], li[:, SEQ:NT]), (o[0:NS, H:2 * H], lf[:, SEQ:NT])])
            for h in range(H):
                ring.wait_free(pe, "bc", h)
                o = slot("bc", h)
                pick = const("head", H)[:, h * P:(h + 1) * P]
                pe.matmul(o[:, 0, :], pick, mr[:, 0:SEQ], start=True, stop=True)
                full(pe.matmul(o[:, 1, :], pick, wi[:, 0:SEQ], start=True, stop=True))
            ring.wait_emptied(pe, "z", 11)
            o = slot("st")
            transposes(("st",), [(o[0:NS, q, h * P:(h + 1) * P], (Zk, Zq)[q][:, h, SEQ:NT])
                                 for q in range(2) for h in range(H)])
            for c in range(TILES):
                cc = slice(c * P, (c + 1) * P)
                o = slot("kt", c)
                transposes(("kt", c), [(o[:, q, h * P:(h + 1) * P], (Zk, Zv)[q][:, h, cc])
                                       for q in range(2) for h in range(H)])
                ring.wait_free(pe, "s", c)
                o = slot("s", c)
                for h in range(H):
                    mm = pe.matmul(o[:, 0, h * P:(h + 1) * P], Zk[:, h, cc], Zq[:, h, cc], start=True, stop=True)
                full(mm)
                ring.wait_emptied(pe, "kt", c)
                ring.wait_free(pe, "kv", c)
                o = slot("kv", c)
                for h in range(H):
                    mm = pe.matmul(o[:, h // 2, (h % 2) * 129:(h % 2) * 129 + 129], KT[:, c, h], V1[:, c, h, 0:129],
                                   start=True, stop=True)
                full(mm)
            for n in range(12, 20):
                project(n)
            pe.wait_ge(sem("pool_in"), 32)
            ring.wait_free(pe, "ws")
            o = slot_flat("ws")
            for g in range(4):
                mm = pe.matmul(o[:, g * NS:(g + 1) * NS], PB[:, g * P:(g + 1) * P],
                               const("window")[0:120, g * NS:(g + 1) * NS], start=True, stop=True)
            full(mm)
            for c in range(TILES):
                ring.wait_free(pe, "num", c)
                ring.wait_emptied(pe, "s", c)
                if c:
                    ring.wait_emptied(pe, "kv", c - 1)
                o = slot("num", c)
                for h in range(H):
                    out = o[:, h // 2, (h % 2) * 129:(h % 2) * 129 + 129]
                    mm = pe.matmul(out, W[:, h, c], V1[:, c, h, 0:129], start=True, stop=c == 0)
                    if c:
                        mm = pe.matmul(out, QT[:, h, c * P:(c + 1) * P], CN[:, c - 1, h], start=False, stop=True)
                full(mm)
                ring.wait_emptied(pe, "num", c)
                o = slot("hT", c)
                transposes(("hT", c), [(o[:, 0, h * P:(h + 1) * P], HM[:, c % 2, h]) for h in range(H)])
            for g in range(4):
                pe.wait_ge(sem("pool_mixed"), g + 1)
                ring.wait_free(pe, "pw", g)
                o = slot("pw", g)
                for b in range(2):
                    mm = pe.matmul(o[:, b, 0:HALF], PW[:, g], DT[:, g, b * HALF:(b + 1) * HALF], start=True, stop=True)
                full(mm)
            pe.wait_ge(sem("w_out_in"), 16)
            for g in range(4):
                ring.wait_emptied(pe, "pw", g)
            ring.wait_emptied(pe, "hT", TILES - 1)
            for i in range(5):
                if i == TILES:
                    pe.wait_ge(sem("mix_samples"), 1)
                ring.wait_free(pe, "wo", i)
                o = slot("wo", i)
                n = ROWS[i]
                for kc in range(KC):
                    for b in range(2):
                        mm = pe.matmul(o[0:n, b, :], MIX[:, kc, i * P:i * P + n], WOUT[:, kc, b * 512:(b + 1) * 512],
                                       start=kc == 0, stop=kc == KC - 1)
                full(mm)

            def router(l):
                for i in range(5):
                    n = ROWS[i]
                    pe.wait_ge(sem(f"h_{2 * l + 1}"), i + 1)
                    if i >= 2:
                        ring.wait_emptied(pe, "lg", l, i - 2)
                    o = slot("tr", l, i)
                    transposes(("tr", l, i), [(o[:, kc // 4, (kc % 4) * P:(kc % 4) * P + n],
                                               HB[0:n, i, kc * P:(kc + 1) * P]) for kc in range(KC)])
                    ring.wait_emptied(pe, "tr", l, i)
                    ring.wait_free(pe, "lg", l, i)
                    o = slot_flat("lg", l, i)
                    for kc in range(KC):
                        mm = pe.matmul(o[0:n, 0:36], HTB[i % 2][:, kc, 0:n], WR[l][:, kc], start=kc == 0,
                                       stop=kc == KC - 1)
                    full(mm)
                pe.wait_ge(sem("chosen"), l + 1)
                ring.wait_free(pe, "pos", l)
                o = slot("pos", l)
                flat = "p t e -> p (t e)"
                pe.matmul(o[:, 0, 0:5 * E], before, OH.rearrange(flat), start=True, stop=False)
                pe.matmul(o[:, 0, 0:5 * E], ones, PRE.rearrange(flat), start=False, stop=True)
                full(pe.matmul(o[:, 1, 0:E], ones, both, start=True, stop=True))
                ring.wait_emptied(pe, "pos", l)

            def experts(l):
                def turns(r):
                    pe.wait_ge(sem(f"spots_{l}"), r + 1)
                    for q in range(10):
                        mm = pe.matmul(ps[:, 0, 0:E], OHR[:, q], oh[q // 5][:, q % 5], start=q == 0, stop=q == 9)
                    mm.then_inc(sem(f"list_done_{l}"), 1)
                    pe.wait_ge(sem(f"list_read_{l}"), r + 1)
                    pe.sem_inc(sem("round_marks"), 1)
                    with pe.Fori(0, E // 2) as k:
                        t = k + 16 * r
                        for s in range(2):
                            pe.wait_ge(sem(f"xg_in_{l}_{s}"), 16 * t + 16)
                            for b in range(4):
                                mm = pe.transpose(ps[:, s, b * P:(b + 1) * P], XG[s][:, b * P:(b + 1) * P], ident)
                            mm.then_inc(sem(f"xt_done_{l}"), 1)
                        for s in range(2):
                            pe.wait_ge(sem(f"wgu_in_{l}_{s}"), 16 * t + 16)
                            pe.wait_ge(sem(f"xt_ready_{l}"), 2 * t + s + 1)
                            for kc in range(KC):
                                for f in range(2):
                                    mm = pe.matmul(ps[CAP * f:CAP * f + CAP, 2 + s, 0:256],
                                                   XT[s][:, kc % 4, CAP * (kc // 4):CAP * (kc // 4) + CAP],
                                                   WGU[s][:, kc, 256 * f:256 * f + 256],
                                                   start=kc == 0, stop=kc == KC - 1)
                            mm.then_inc(sem(f"gu_done_{l}"), 1)
                        for s in range(2):
                            pe.wait_ge(sem(f"act_ready_{l}"), 2 * t + s + 3)
                            pe.transpose(ps[:, 4 + s, 0:P], ACTB[s], ident).then_inc(sem(f"at_done_{l}"), 1)
                        for s in range(2):
                            pe.wait_ge(sem(f"wd_in_{l}_{s}"), 16 * t + 16)
                            pe.wait_ge(sem(f"at_ready_{l}"), 2 * t + s + 1)
                            pe.wait_ge(sem(f"y_ready_{l}"), 2 * t + 2)
                            for f in range(2):
                                for b in range(2):
                                    mm = pe.matmul(ps[CAP * b:CAP * b + CAP, 6 + s, :], AT[s][:, CAP * f:CAP * f + CAP],
                                                   WD[s][:, f, 512 * b:512 * b + 512], start=f == 0, stop=f == 1)
                            mm.then_inc(sem(f"down_done_{l}"), 1)
                    pe.wait_ge(sem(f"y_ready_{l}"), E * r + E + 2)
                turns(0)
                n = pe.value_load(most[0:1, l:l + 1], min_val=0, max_val=NT)
                with pe.Fori(1, ROUNDS) as r:
                    with pe.If(n > r * CAP):
                        turns(r)

            router(0)
            experts(0)

            pe.wait_ge(sem("g_ready"), 1)
            ring.wait_free(pe, "k")
            o = slot_flat("k")
            for pb in range(8):
                for pq in range(4):
                    pr = 4 * pb + pq
                    out = o[32 * pq:32 * pq + 32, pb * P:(pb + 1) * P]
                    pe.matmul(out, BD[0][:, pr], GR[:, pr, 0:L], start=True, stop=False)
                    mm = pe.matmul(out, BD[1][:, pr], GI[:, pr, 0:L], start=False, stop=True)
            full(mm)
            pe.wait_ge(sem("v_ready"), 1)
            for q in range(8):
                o = slot_flat("mt", q)
                transposes(("mt", q), [(o[:, (2 * j + ri) * P:(2 * j + ri + 1) * P],
                                        (VR, VI)[ri][:, 4 * q + j].rearrange("p l c -> p (l c)"))
                                       for j in range(4) for ri in range(2)])
            for q in range(8):
                pe.wait_ge(sem("xr_ready"), q + 1)
                o = slot("u", q)
                transposes(("u", q), [(o[:, j // 4, (j % 4) * UC:(j % 4 + 1) * UC],
                                       XR[q % 2][:, j * P:(j + 1) * P]) for j in range(8)])
            for q in range(8):
                ring.wait_free(pe, "zs", q)
                ring.wait_emptied(pe, "mt", q)
                ring.wait_emptied(pe, "u", q)
                o = slot("zs", q)
                for j in range(4):
                    pr = 4 * q + j
                    for ri in range(2):
                        for g2 in range(2):
                            mm = pe.matmul(o[64 * g2:64 * g2 + 64, ri, j * SC:(j + 1) * SC],
                                           M[:, pr, ri, 64 * g2:64 * g2 + 64], U[:, 2 * pr + g2, 0:SC],
                                           start=True, stop=True)
                full(mm)
            pe.wait_ge(sem("taps_in"), 16 * L)
            pe.wait_ge(sem("states_in"), 1)
            for q in range(8):
                ring.wait_free(pe, "y", q)
                o = slot("y", q)
                for j in range(8):
                    g = 8 * q + j
                    pr, lo = g // 2, 64 * (g % 2)
                    out = o[0:SC, j % 2, (j // 2) * P:(j // 2 + 1) * P]
                    pe.matmul(out, U[:, g, NS:UC], TT[:, g], start=True, stop=False)
                    pe.matmul(out, HR[lo:lo + 64, pr], GR[lo:lo + 64, pr, 1:L + 1], start=False, stop=False)
                    mm = pe.matmul(out, HI[lo:lo + 64, pr], GI[lo:lo + 64, pr, 1:L + 1], start=False, stop=True)
                full(mm)
            for kc in range(KC):
                ring.wait_emptied(pe, "y", kc)
                o = slot("yT", kc)
                transposes(("yT", kc), [(o[:, l // 4, (l % 4) * SC:(l % 4 + 1) * SC],
                                         YK[0:SC, l, kc * P:(kc + 1) * P]) for l in range(L)])
            for kc in range(KC):
                ring.wait_emptied(pe, "yT", kc)
            for i in range(5):
                for ch in range(2):
                    pe.wait_ge(sem(f"w_glu_in_{ch}"), 16)
                    ring.wait_free(pe, "gl", i, ch)
                    o = slot("gl", i, ch)
                    n = ROWS[i]
                    for kc in range(KC):
                        for b in range(2):
                            mm = pe.matmul(o[0:n, b, :], YT[:, kc, i * P:i * P + n],
                                           WGL[ch][:, kc, b * 512:(b + 1) * 512], start=kc == 0, stop=kc == KC - 1)
                    full(mm)
            router(1)
            experts(1)

        def norm_squares(act, n, X_ready):
            junk = place(A + 5120, D) if n == 0 else place(A + 32768, D)
            for i in range(5):
                X_ready(i)
                ins = nc.scalar.activation(junk, X[:, i, :], ACT.Square, accum_out=ss[:, i:i + 1])
                ins.then_inc(sem("squares"), 1)
                act.wait_ge(sem("squares"), 5 * NORM[n] + i + 1)
            act.wait_ge(sem("var_ready"), NORM[n] + 1)
            nc.scalar.activation(root, var, ACT.Sqrt).then_inc(sem("root_ready"), 1)

        def norm_scale(dve, step, n, out):
            v = nc.vector
            dve.wait_ge(sem("squares"), 5 * NORM[n] + 5)
            v.tensor_scalar(var, ss, 1.0 / D, EPS, ALU.mult, ALU.add).then_inc(sem("var_ready"), 1)
            dve.wait_ge(sem("root_ready"), NORM[n] + 1)
            step(v.reciprocal(rstd, root))
            dve.wait_ge(sem("norm_in"), 16 * n + 16)
            for i in range(5):
                v.scalar_tensor_tensor(out[:, i, :], X[:, i, :], rstd[:, i:i + 1], GB, ALU.mult, ALU.mult
                                       ).then_inc(sem(f"h_{n}"), 1)
                dve.wait_ge(sem(f"h_{n}"), i + 1)

        def store_normed(act, n, src, done):
            for i in range(5):
                act.wait_ge(sem(f"h_{n}"), i + 1)
                act.dma_start(hd[i * P:i * P + ROWS[i], :], tile_rows(src, i)).then_inc(sem(done), 16)

        @block.scalar
        def _(act):
            a = nc.scalar
            chain = [0]

            def step(ins):
                chain[0] += 1
                ins.then_inc(sem("act_steps"), 1)
                act.wait_ge(sem("act_steps"), chain[0])

            for l in range(2):
                for s in range(2):
                    act.sem_inc(sem(f"y_out_{l}_{s}"), 16)

            def x_in(i):
                if i == TILES:
                    act.wait_ge(sem("x_cleared"), 1)
                act.wait_ge(sem(f"x_in_{i}"), 16)

            norm_squares(act, 0, x_in)
            for i in (1, 3):
                take(act, "ht", i)
                give(act, a.copy(HT[:, :, i * P:(i + 1) * P], slot("ht", i).rearrange("p b (k n) -> p (b k) n", n=P)),
                     "ht", i)
            act.wait_ge(sem("f_in"), 1)
            step(a.activation(er, lf, ACT.Abs))
            step(a.activation(er, er, ACT.Exp, scale=-1.0))
            a.activation(tr_, er, ACT.Ln, bias=1.0).then_inc(sem("softplus"), 1)

            def z_out(n, dst, func=ACT.Copy, scale=1.0):
                take(act, "z", n)
                give(act, a.activation(dst.rearrange("p (b n) -> p b n", b=2), slot("z", n)[:, :, 0:HALF], func,
                                       scale=scale), "z", n)

            for n in range(4):
                z_out(n, Zk[:, n], scale=KSCALE)
            act.wait_ge(sem("exps_in"), 1)
            step(a.activation(wi[:, 0:SEQ], wi[:, 0:SEQ], ACT.Exp))
            a.activation(er[:, 0:SEQ], er[:, 0:SEQ], ACT.Exp).then_inc(sem("exps_out"), 1)
            for n in range(4):
                z_out(4 + n, Zq[:, n])
            for n in range(4):
                z_out(8 + n, Zv[:, n])
            act.wait_ge(sem("sm_in"), 1)
            a.activation(SM, SM, ACT.Exp).then_inc(sem("sm_out"), 1)
            for h in range(H):
                act.wait_ge(sem("w_in_exp"), h + 1)
                for c in range(TILES):
                    ins = a.activation(W[:, h, c], W[:, h, c], ACT.Exp, bias=gcol[:, H * c + h:H * c + h + 1])
                ins.then_inc(sem("w_exp"), 1)
                act.wait_ge(sem("w_exp"), h + 1)
            for n in range(4):
                take(act, "z", 12 + n)
                src = slot("z", 12 + n)
                if n == 0:
                    act.wait_ge(sem("ue_cleared"), 1)
                step(a.copy(UE[:, n, CW:CW + HALF], src[:, 0, 0:HALF]))
                step(a.copy(UE[:, n, CW + HALF:CW + SEQ], src[:, 1, 0:SEQ - HALF]))
                give(act, a.copy(us[:, n], src[:, 1, SEQ - HALF:HALF]), "z", 12 + n)
            for n in range(4):
                z_out(16 + n, Zo[:, n], ACT.Sigmoid)
            for g in range(4):
                take(act, "pw", g)
                give(act, a.activation(MIX[:, g].rearrange("p (b n) -> p b n", b=2), slot("pw", g)[:, :, 0:HALF],
                                       ACT.Copy, scale=pscale[:, g:g + 1]), "pw", g)

            def router(l):
                n = 2 * l + 1
                act.wait_ge(sem("x_mixed"), l + 1)
                norm_squares(act, n, lambda i: act.wait_ge(sem("x_tile"), 10 * l + i + 1))
                store_normed(act, n, HB, f"h_out_{l}")
                for i in range(5):
                    take(act, "tr", l, i)
                    m = ROWS[i]
                    give(act, a.copy(HTB[i % 2][:, :, 0:m],
                                     slot("tr", l, i).rearrange("p b (k n) -> p (b k) n", n=P)[:, :, 0:m]),
                         "tr", l, i)
                act.wait_ge(sem("dg_ready"), l + 1)
                a.activation(gexp, gexp, ACT.Exp).then_inc(sem("gexp_ready"), 1)
                act.wait_ge(sem("d12_ready"), l + 1)
                a.activation(dexp, dexp, ACT.Exp).then_inc(sem("dexp_ready"), 1)

            def experts(l):
                def turns(r):
                    if not isinstance(r, int):
                        for i in range(5):
                            act.wait_ge(sem(f"yg_in_{l}_{i}"), 32 * r)
                    act.sem_inc(sem("round_marks"), 1)
                    with act.Fori(0, E // 2) as k:
                        t = k + 16 * r
                        for s in range(2):
                            act.wait_ge(sem(f"xt_done_{l}"), 2 * t + s + 3)
                            a.copy(XT[s], ps[:, s, :].rearrange("p (b n) -> p b n", b=4)
                                   ).then_inc(sem(f"xt_ready_{l}"), 1)
                        for s in range(2):
                            act.wait_ge(sem(f"gu_done_{l}"), 2 * t + s + 3)
                            act.wait_ge(sem(f"act_ready_{l}"), 2 * t + 2)
                            a.activation(SIL[s], ps[:, 2 + s, 0:P], ACT.Silu).then_inc(sem(f"silu_{l}"), 1)
                        for s in range(2):
                            act.wait_ge(sem(f"y_ready_{l}"), 2 * t + s + 3)
                            e = 2 * k + s
                            act.dma_start(yd[bass.ds(e, 1)].rearrange("e t (h c) -> h (e t) c", h=2), YE[s]
                                          ).then_inc(sem(f"y_out_{l}_{s}"), 16)
                    for s in range(2):
                        act.wait_ge(sem(f"y_out_{l}_{s}"), 256 * r + 272)
                    act.sem_inc(sem(f"y_all_out_{l}"), 1)
                turns(0)
                n = act.value_load(most[0:1, l:l + 1], min_val=0, max_val=NT)
                with act.Fori(1, ROUNDS) as r:
                    with act.If(n > r * CAP):
                        turns(r)

            router(0)
            experts(0)
            for i in range(5):
                act.wait_ge(sem("x_tile"), 5 + i + 1)
                act.dma_start(hd[i * P:i * P + ROWS[i], :], tile_rows(X, i)).then_inc(sem("x1_out"), 16)
            act.wait_ge(sem("s5_in"), 160)
            step(a.activation(sp_[0], sp_[0], ACT.Exp))
            act.sem_inc(sem("s5_dt"), 1)
            act.wait_ge(sem("s5_ath"), 1)
            step(a.activation(sp_[3], sp_[3], ACT.Exp))
            step(a.activation(sp_[5], sp_[7], ACT.Exp, scale=float(L)))
            step(a.activation(sp_[6], sp_[4], ACT.Sin, scale=0.5))
            step(a.activation(sp_[4], sp_[4], ACT.Sin))
            act.sem_inc(sem("s5_sin"), 1)
            for q in range(8):
                take(act, "mt", q)
                give(act, a.copy(M[:, 4 * q:4 * q + 4].rearrange("p a b c -> p (a b c)"), slot_flat("mt", q)), "mt", q)
            act.wait_ge(sem("xk_in"), 48)
            for l in range(L):
                step(a.activation(place(A, D, parts=UC), XK[:, l], ACT.Square, accum_out=ssk[:, l:l + 1]))
            act.sem_inc(sem("ssk_ready"), 1)
            act.wait_ge(sem("vark_ready"), 1)
            a.activation(ssk, ssk, ACT.Sqrt).then_inc(sem("rootk_ready"), 1)
            act.wait_ge(sem("rstdk_ready"), 1)
            for l in range(L):
                step(a.activation(XK[:, l], XK[:, l], ACT.Copy, scale=ssk[:, l:l + 1]))
            act.sem_inc(sem("xk_scaled"), 1)
            for q in range(1, 8, 2):
                take(act, "u", q)
                give(act, a.copy(U[:, 8 * q:8 * q + 8].rearrange("p (b j) n -> p b (j n)", b=2),
                                 slot("u", q)[:, :, 0:4 * UC]), "u", q)

            def y_out(q):
                take(act, "y", q)
                step(a.copy(*y_views(q, 0)))
                give(act, a.copy(*y_views(q, 1)), "y", q)
            for q in range(1, 8, 2):
                y_out(q)
            for kc in range(KC):
                take(act, "yT", kc)
                src = slot("yT", kc)
                if kc == 0:
                    ring.wait_full(act, "y", 7)
                step(a.activation(YT[:, kc, 0:SEQ].rearrange("p (k b l) -> p b l k", b=2, l=4),
                                  src[:, :, 0:4 * SC].rearrange("p b (l k) -> p b l k", l=4)[:, :, :, 0:NCH],
                                  ACT.Gelu_apprx_tanh))
                give(act, a.activation(YT[:, kc, SEQ:NT], src[:, 0, NCH:SC], ACT.Gelu_apprx_tanh), "yT", kc)
            for i in range(5):
                for ch in range(2):
                    take(act, "gl", i, ch)
                    q = 2 * i + ch
                    if q >= 2:
                        act.wait_ge(sem("sig_used"), q - 1)
                    a.activation(SIG[q % 2][0:ROWS[i]], slot("gl", i, ch)[0:ROWS[i], 1, :], ACT.Sigmoid
                                 ).then_inc(sem("sig_ready"), 1)
            router(1)
            experts(1)
            norm_squares(act, 4, lambda i: act.wait_ge(sem("x_tile"), 15 + i + 1))

        @block.vector
        def _(dve):
            v = nc.vector
            chain = [0]

            def step(ins):
                chain[0] += 1
                ins.then_inc(sem("dve_steps"), 1)
                dve.wait_ge(sem("dve_steps"), chain[0])

            def tt(out, a, b, op):
                step(v.tensor_tensor(out, a, b, op))

            def ts(out, a, s1, s2, op0, op1=ALU.bypass):
                step(v.tensor_scalar(out, a, s1, s2, op0, op1))

            def stt(out, a, s, b, op0, op1):
                step(v.scalar_tensor_tensor(out, a, s, b, op0, op1))

            for l in range(2):
                for name in ("act_ready", "y_ready"):
                    dve.sem_inc(sem(f"{name}_{l}"), 2)
            v.memset(X[:, TILES, :], 0.0).then_inc(sem("x_cleared"), 1)
            norm_scale(dve, step, 0, HH)
            for i in (0, 2, 4):
                take(dve, "ht", i)
                n = ROWS[i]
                give(dve, v.tensor_copy(HT[:, :, i * P:i * P + n],
                                        slot("ht", i).rearrange("p b (k n) -> p (b k) n", n=P)[:, :, 0:n]), "ht", i)
            take(dve, "gates")
            dve.wait_ge(sem("small_in"), 16 * 7)
            g = slot("gates")
            ts(li.rearrange("p (b n) -> p b n", b=2), g[0:H, :, 0:HALF], bg[:, 0:1], None, ALU.add)
            give(dve, v.tensor_copy(lf.rearrange("p (b n) -> p b n", b=2), g[32:32 + H, :, 0:HALF]), "gates")
            ts(lf, lf, bg[:, 1:2], None, ALU.add)
            dve.sem_inc(sem("f_in"), 1)
            dve.wait_ge(sem("softplus"), 1)
            stt(lf, lf, 0.0, tr_, ALU.min, ALU.subtract)
            dve.wait_ge(sem("consts"), 16)
            step(v.tensor_tensor_scan(bc_[:, 0:SEQ], const("keep", H), lf[:, 0:SEQ], 0.0, ALU.mult, ALU.add))
            tt(ar[:, 0:SEQ], li[:, 0:SEQ], bc_[:, 0:SEQ], ALU.subtract)
            step(v.memset(mrun, 0.0))
            for c in range(TILES):
                cc = slice(c * P, (c + 1) * P)
                e = (c + 1) * P - 1
                step(v.tensor_tensor_scan(mr[:, cc], ar[:, cc], ar[:, cc], mrun[:, c:c + 1], ALU.max, ALU.max))
                tt(mrun[:, c + 1:c + 2], bc_[:, e:e + 1], mr[:, e:e + 1], ALU.add)
                ts(wi[:, cc], mr[:, cc], -1.0, mrun[:, c:c + 1], ALU.mult, ALU.add)
            stt(er[:, 0:SEQ], bc_[:, 0:SEQ], -1.0, mr[:, 0:SEQ], ALU.mult, ALU.subtract)
            ts(mr[:, 0:SEQ], mr[:, 0:SEQ], -1.0, None, ALU.mult)
            dve.sem_inc(sem("exps_in"), 1)
            dve.wait_ge(sem("exps_out"), 1)
            dve.sem_inc(sem("gate_rows"), 1)
            step(v.memset(UE[:, :, 0:CW], 0.0))
            dve.sem_inc(sem("ue_cleared"), 1)
            take(dve, "cols")
            step(v.tensor_copy(gcol, slot_flat("cols")[:, 0:16]))
            give(dve, v.tensor_copy(ecol, slot_flat("cols")[:, 16:32]), "cols")
            take(dve, "sg")
            give(dve, v.tensor_copy(SG, slot_flat("sg")[0:NS, 0:8]), "sg")
            dve.wait_ge(sem("n0_in"), 16)
            tt(SM[:, 4:8], SG[:, 0:4], SG[:, 4:8], ALU.subtract)
            tt(SM[:, 8:12], SM[:, 4:8], m0s, ALU.max)
            tt(SM[:, 0:4], m0s, SM[:, 8:12], ALU.subtract)
            tt(SM[:, 4:8], SM[:, 4:8], SM[:, 8:12], ALU.subtract)
            tt(sden[:, 0:4], SM[:, 8:12], SG[:, 4:8], ALU.add)
            ts(SM[:, 8:12], sden[:, 0:4], -1.0, None, ALU.mult)
            dve.sem_inc(sem("sm_in"), 1)
            for h in range(H):
                take(dve, "bc", h)
                b = slot("bc", h)
                tt(W[:, h], b[:, 0, :].rearrange("p (c n) -> p c n", c=TILES), spread_mid(causal, TILES), ALU.add)
                dve.sem_inc(sem("w_in_exp"), 1)
                if h == 0:
                    ring.wait_emptied(dve, "z", 7)
                tt(QT[:, h], Zq[:, h, 0:SEQ], b[:, 1, :], ALU.mult)
                give(dve, v.tensor_copy(dec.rearrange("p (c h) -> p c h", h=H)[:, :, h],
                                        b[:, 1, :].rearrange("p (c n) -> p c n", c=TILES)[:, :, P - 1]), "bc", h)
            dve.sem_inc(sem("rows_dead"), 1)
            take(dve, "st")
            step(v.tensor_copy(ks, slot("st")[0:NS, 0, :].rearrange("p (h k) -> p h k", h=H)))
            dve.wait_ge(sem("w_exp"), H)
            sq = KB[0:NS, 0:H]
            give(dve, v.tensor_copy(sq, slot("st")[0:NS, 1, :].rearrange("p (h k) -> p h k", h=H)), "st")
            dve.wait_ge(sem("sm_out"), 1)
            tt(ks, ks, spread(SM[:, 4:8], P), ALU.mult)
            tt(n0s, n0s, spread(SM[:, 0:4], P), ALU.mult)
            tt(n0s, n0s, ks, ALU.add)
            ring.wait_emptied(dve, "z", 11)
            step(v.tensor_copy(vs, Zv[:, :, SEQ:NT]))
            step(v.memset(V1[:, :, :, P:P + 1], 1.0))
            for c in range(TILES):
                take(dve, "kt", c)
                kt = slot("kt", c)
                for h in range(H):
                    ts(KT[:, c, h], kt[:, 0, h * P:(h + 1) * P], W[:, h, c, P - 1:P], None, ALU.mult)
                give(dve, v.tensor_copy(V1[:, c, :, 0:P], kt[:, 1, :].rearrange("p (h k) -> p h k", h=H)), "kt", c)
                take(dve, "s", c)
                give(dve, v.tensor_tensor(W[:, :, c, :], slot("s", c)[:, 0, :].rearrange("p (h k) -> p h k", h=H),
                                          W[:, :, c, :], ALU.mult), "s", c)
                take(dve, "kv", c)
                kv = slot("kv", c)
                for h in range(H):
                    src = kv[:, h // 2, (h % 2) * 129:(h % 2) * 129 + 129]
                    if c == 0:
                        ins = v.tensor_copy(CN[:, 0, h], src)
                    else:
                        ins = v.scalar_tensor_tensor(CN[:, c, h], CN[:, c - 1, h], dec[:, H * c + h:H * c + h + 1],
                                                     src, ALU.mult, ALU.add)
                    if h < H - 1:
                        step(ins)
                give(dve, ins, "kv", c)
            dve.sem_inc(sem("cn_ready"), 1)
            prod = KB[0:NS, H:2 * H]
            tt(prod, n0s, sq, ALU.mult)
            step(v.tensor_reduce(sden[:, 4:8], prod, AX, ALU.add))
            stt(sden[:, 8:12], sden[:, 4:8], -1.0, sden[:, 4:8], ALU.mult, ALU.max)
            tt(sden[:, 8:12], sden[:, 8:12], SM[:, 8:12], ALU.max)
            step(v.reciprocal(sden[:, 4:8], sden[:, 8:12]))
            tt(qs, sq, spread(sden[:, 4:8], P), ALU.mult)
            dve.sem_inc(sem("ks_ready"), 1)
            ring.wait_emptied(dve, "z", 15)
            dve.sem_inc(sem("us_ready"), 1)
            dve.sem_inc(sem("u_in"), 1)
            take(dve, "ws")
            for g_ in range(4):
                w = 2.0 ** -(g_ + 1)
                tt(sos[:, g_], slot_flat("ws")[:, g_ * NS:(g_ + 1) * NS], us[:, g_], ALU.add)
                ins = v.scalar_tensor_tensor(DT[:, g_, SEQ:NT], sos[:, g_], w, us[:, g_], ALU.mult, ALU.subtract)
                if g_ < 3:
                    step(ins)
            give(dve, ins, "ws")
            dve.sem_inc(sem("ws_done"), 1)
            ring.wait_emptied(dve, "z", 19)
            for c in range(TILES):
                take(dve, "num", c)
                nm = slot("num", c)
                step(v.tensor_copy(den.rearrange("p (a b) -> p a b", a=2),
                                   nm[:, :, 0:258].rearrange("p a (b n) -> p a b n", b=2)[:, :, :, P]))
                stt(dab, den, -1.0, den, ALU.mult, ALU.max)
                tt(dab, dab, ecol[:, H * c:H * c + H], ALU.max)
                step(v.reciprocal(rden, dab))
                for h in range(H):
                    ins = v.tensor_scalar(HM[:, c % 2, h], nm[:, h // 2, (h % 2) * 129:(h % 2) * 129 + P],
                                          rden[:, h:h + 1], None, ALU.mult)
                    if h < H - 1:
                        step(ins)
                give(dve, ins, "num", c)
                take(dve, "hT", c)
                give(dve, v.tensor_tensor(MIX[:, H:2 * H, c * P:(c + 1) * P],
                                          slot("hT", c)[:, 0, :].rearrange("p (h n) -> p h n", h=H),
                                          Zo[:, :, c * P:(c + 1) * P], ALU.mult), "hT", c)
            dve.wait_ge(sem("kb_in"), 32)
            dve.wait_ge(sem("c0_in"), 16)
            tt(CS, CS, spread(DB, P), ALU.mult)
            kb4 = KB.rearrange("p (n h) k -> p n h k", h=H)
            tt(kb4, kb4, spread(vs.rearrange("p h n -> p n h"), P), ALU.mult)
            tt(CS, CS, KB, ALU.add)
            dve.sem_inc(sem("kb_used"), 1)
            dve.sem_inc(sem("cs_ready"), 1)
            dve.wait_ge(sem("qb_in"), 16)
            tt(KB, KB, CS, ALU.mult)
            step(v.tensor_reduce(rs, KB, AX, ALU.add))
            tt(MIX[:, H:2 * H, SEQ:NT], rs.rearrange("p (n h) -> p h n", h=H), Zo[:, :, SEQ:NT], ALU.mult)
            dve.sem_inc(sem("mix_samples"), 1)
            for i in range(5):
                take(dve, "wo", i)
                n = ROWS[i]
                give(dve, v.tensor_tensor(X[0:n, i, :], X[0:n, i, :], slot_flat("wo", i)[0:n], ALU.add), "wo", i)
                dve.sem_inc(sem("x_tile"), 1)
            dve.wait_ge(sem("stored"), 16 * 8)
            dve.sem_inc(sem("x_mixed"), 1)

            def router(l):
                step(v.memset(LG, 0.0))
                norm_scale(dve, step, 2 * l + 1, HB)
                for i in range(5):
                    take(dve, "lg", l, i)
                    n = ROWS[i]
                    give(dve, v.tensor_tensor(LG[0:n, i], slot_flat("lg", l, i)[0:n, 0:36], BR[l][0:n], ALU.add),
                         "lg", l, i)
                gl, el = LG[:, :, 0:4], LG[:, :, 4:36]

                def first_of(values, top, rev, out):
                    n = values.shape[-1]
                    step(v.tensor_reduce(top, values, AX, ALU.max))
                    tt(out, values, spread(top, n), ALU.is_equal)
                    tt(out, out, spread_mid(rev, 5), ALU.mult)
                    step(v.tensor_reduce(etop, out, AX, ALU.max))
                    tt(out, out, spread(etop, n), ALU.is_equal)

                first_of(gl, gmax, const("revg"), og)
                tt(gexp, gl, spread(gmax, 4), ALU.subtract)
                dve.sem_inc(sem("dg_ready"), 1)
                ts(gneg, og, BIG, -BIG, ALU.mult, ALU.add)
                tt(me.rearrange("p t (g k) -> p t g k", g=4), el.rearrange("p t (g k) -> p t g k", g=4),
                   spread(gneg, 8), ALU.add)
                first_of(me, m1, const("reve"), oh[0])
                stt(me, oh[0], -2 * BIG, me, ALU.mult, ALU.add)
                first_of(me, m2, const("reve"), oh[1])
                tt(dexp, m2, m1, ALU.subtract)
                dve.sem_inc(sem("d12_ready"), 1)
                for j in range(2):
                    tt(oh[j], oh[j], spread(const("valid"), E), ALU.mult)
                tt(OH, oh[0], oh[1], ALU.add)
                step(v.memset(PRE[:, 0], 0.0))
                for i in range(1, 5):
                    tt(PRE[:, i], PRE[:, i - 1], OH[:, i - 1], ALU.add)
                tt(both, PRE[:, 4], OH[:, 4], ALU.add)
                dve.sem_inc(sem("chosen"), 1)
                dve.wait_ge(sem("gexp_ready"), l + 1)
                step(v.tensor_reduce(gsum, gexp, AX, ALU.add))
                step(v.reciprocal(gw, gsum))
                dve.wait_ge(sem("dexp_ready"), l + 1)
                ts(dsum, dexp, 1.0, None, ALU.add)
                step(v.reciprocal(dsum, dsum))
                tt(pw_[0], dsum, gw, ALU.mult)
                tt(pw_[1], pw_[0], dexp, ALU.mult)
                take(dve, "pos", l)
                o = slot("pos", l)
                step(v.tensor_copy(POS, o[:, 0, 0:5 * E].rearrange("p (t e) -> p t e", t=5)))
                step(v.tensor_reduce(cntmax, o[:, 1, 0:E], AX, ALU.max))
                give(dve, v.tensor_copy(most[:, l:l + 1], cntmax), "pos", l)
                dve.sem_inc(sem("most_ready"), 1)
                for j in range(2):
                    tt(hit, oh[j], POS, ALU.mult)
                    step(v.tensor_reduce(RK[:, j], hit, AX, ALU.add))
                    tt(hit, oh[j], spread_mid(const("eio"), 5), ALU.mult)
                    step(v.tensor_reduce(EID[:, j], hit, AX, ALU.add))
                    tt(oh[j], oh[j], spread(const("tokid"), E), ALU.mult)
                ts(EID, EID, float(CAP), None, ALU.mult)
                for s in range(2):
                    step(v.memset(XG[s], 0.0))
                dve.sem_inc(sem("xg_cleared"), 1)

            def experts(l):
                def turns(r):
                    n = 19

                    def lstep(ins, k):
                        ins.then_inc(sem(f"list_steps_{l}"), 1)
                        dve.wait_ge(sem(f"list_steps_{l}"), n * r + k)

                    for q in range(10):
                        v.tensor_scalar(OHR[:, q], const("iota"), RK.rearrange("p j t -> p (j t)")[:, q:q + 1], None,
                                        ALU.is_equal).then_inc(sem(f"list_steps_{l}"), 1)
                    dve.wait_ge(sem(f"list_steps_{l}"), n * r + 10)
                    dve.sem_inc(sem(f"spots_{l}"), 1)
                    lstep(v.tensor_scalar(QR, RK, 0.0, None, ALU.is_ge), 11)
                    lstep(v.scalar_tensor_tensor(QR, RK, float(CAP), QR, ALU.is_lt, ALU.mult), 12)
                    lstep(v.tensor_scalar(QR, QR, -1e5, 1e5, ALU.mult, ALU.add), 13)
                    lstep(v.tensor_tensor(QR, QR, EID, ALU.add), 14)
                    lstep(v.tensor_tensor(idx_back[:, :], QR.rearrange("p j t -> p (j t)"),
                                          RK.rearrange("p j t -> p (j t)"), ALU.add), 15)
                    lstep(v.tensor_scalar(RK, RK, -float(CAP), None, ALU.add), 16)
                    dve.wait_ge(sem(f"list_done_{l}"), r + 1)
                    lstep(v.tensor_scalar(both, ps[:, 0, 0:E], 0.0, 4096.0, ALU.is_equal, ALU.mult), 17)
                    lstep(v.scalar_tensor_tensor(both, ps[:, 0, 0:E], 2.0, both, ALU.mult, ALU.add), 18)
                    lstep(v.tensor_scalar(idx_list[:, :], both, const("half"), None, ALU.add), 19)
                    dve.sem_inc(sem(f"list_read_{l}"), 1)
                    with dve.Fori(0, E // 2) as k:
                        t = k + 16 * r
                        for s in range(2):
                            dve.wait_ge(sem(f"silu_{l}"), 2 * t + s + 1)
                            v.tensor_tensor(ACTB[s], SIL[s], ps[:, 2 + s, P:2 * P], ALU.mult
                                            ).then_inc(sem(f"act_ready_{l}"), 1)
                        for s in range(2):
                            dve.wait_ge(sem(f"at_done_{l}"), 2 * t + s + 1)
                            v.tensor_copy(AT[s], ps[:, 4 + s, 0:P]).then_inc(sem(f"at_ready_{l}"), 1)
                        for s in range(2):
                            dve.wait_ge(sem(f"down_done_{l}"), 2 * t + s + 3)
                            dve.wait_ge(sem(f"y_out_{l}_{s}"), 16 * t + 16)
                            v.tensor_copy(YE[s], ps[:, 6 + s, :]).then_inc(sem(f"y_ready_{l}"), 1)
                    for q in range(10):
                        i, j, m = q // 2, q % 2, ROWS[q // 2]
                        dve.wait_ge(sem(f"yg_in_{l}_{i}"), 32 * r + 32)
                        v.scalar_tensor_tensor(X[0:m, i, :], YG[0:m, q], pw_[j][0:m, i:i + 1], X[0:m, i, :],
                                               ALU.mult, ALU.add).then_inc(sem(f"combined_{l}"), 1)
                        dve.wait_ge(sem(f"combined_{l}"), 10 * r + q + 1)
                    dve.sem_inc(sem("round_marks"), 1)
                turns(0)
                n = dve.value_load(most[0:1, l:l + 1], min_val=0, max_val=NT)
                with dve.Fori(1, ROUNDS) as r:
                    with dve.If(n > r * CAP):
                        turns(r)
                for i in range(5):
                    dve.sem_inc(sem("x_tile"), 1)
                dve.sem_inc(sem("x_moe"), 1)

            router(0)
            experts(0)

            ls, lr, li_, a_, th, mag8, shalf, aa = sp_[:8]
            lbr, lbi, cs, den_, qr_, qi_, t1, t2, ur, ui, nn = sp_[8:19]

            def cmul(outr, outi, ar_, ai_, br_, bi_, x1, x2, sign=1):
                tt(x1, ai_, bi_, ALU.mult)
                tt(outr, ar_, br_, ALU.mult)
                tt(outr, outr, x1, ALU.subtract if sign > 0 else ALU.add)
                tt(x2, ar_, bi_, ALU.mult)
                tt(outi, ai_, br_, ALU.mult)
                tt(outi, outi, x2, ALU.add if sign > 0 else ALU.subtract)

            dve.wait_ge(sem("s5_dt"), 1)
            tt(aa, lr, ls, ALU.mult)
            step(v.tensor_copy(a_, aa))
            tt(th, li_, ls, ALU.mult)
            magic = 1.5 * 2.0 ** 23
            ts(nn, th, 1.0 / (2 * pi), magic, ALU.mult, ALU.add)
            ts(nn, nn, -magic, None, ALU.add)
            c1 = 6.28125
            c2 = float(np.float32(round((2 * pi - c1) * 2 ** 21) / 2 ** 21))
            for c in (c1, c2, 2 * pi - c1 - c2):
                stt(th, nn, -c, th, ALU.mult, ALU.add)
            ts(th, th, 3.1415925, -3.1415925, ALU.min, ALU.max)
            dve.sem_inc(sem("s5_ath"), 1)
            dve.wait_ge(sem("s5_sin"), 1)
            tt(cs, shalf, shalf, ALU.mult)
            ts(cs, cs, -2.0, 1.0, ALU.mult, ALU.add)
            tt(lbr, a_, cs, ALU.mult)
            tt(lbi, a_, th, ALU.mult)
            tt(t1, lr, lr, ALU.mult)
            tt(t2, li_, li_, ALU.mult)
            tt(t1, t1, t2, ALU.add)
            step(v.reciprocal(den_, t1))
            ts(nn, lbr, -1.0, None, ALU.add)
            cmul(qr_, qi_, nn, lbi, lr, li_, t1, t2, sign=-1)
            tt(qr_, qr_, den_, ALU.mult)
            tt(qi_, qi_, den_, ALU.mult)
            cmul(BBR, BBI, spread(qr_, CW), spread(qi_, CW), CIN[2], CIN[3], T1, T2)
            step(v.memset(PWR[:, 0], 1.0))
            step(v.memset(PWI[:, 0], 0.0))
            for j in range(1, L + 1):
                cmul(PWR[:, j], PWI[:, j], PWR[:, j - 1], PWI[:, j - 1], lbr, lbi, t1, t2)
            for q in range(2):
                step(v.memset(BD[q], 0.0))
                for g2 in range(2):
                    step(v.tensor_copy(BD[q][64 * g2:64 * g2 + 64, :, CW * g2:CW * g2 + CW],
                                       (BBR, BBI)[q][64 * g2:64 * g2 + 64]))
            for j in range(L + 1):
                pr_, pi_ = spread(PWR[:, j], CW), spread(PWI[:, j], CW)
                cmul(GR[:, :, j], GI[:, :, j], CIN[0], CIN[1], pr_, pi_, T1, T2)
                ts(GI[:, :, j], GI[:, :, j], -1.0, None, ALU.mult)
            dve.sem_inc(sem("g_ready"), 1)
            for j in range(L):
                pr_, pi_ = spread(PWR[:, L - 1 - j], CW), spread(PWI[:, L - 1 - j], CW)
                cmul(VR[:, :, j], VI[:, :, j], BBR, BBI, pr_, pi_, T1, T2)
            dve.sem_inc(sem("v_ready"), 1)
            take(dve, "k")
            give(dve, v.tensor_copy(KS.rearrange("p a b -> p (a b)"), slot_flat("k")), "k")
            skip = T1[:, 0:KC]
            tt(skip, spread_mid(const("diag"), KC), spread(DSK, CW), ALU.mult)
            tt(KS[:, :, 0:CW], KS[:, :, 0:CW], skip, ALU.add)
            step(v.memset(KZ, 0.0))
            dve.sem_inc(sem("taps_ready"), 1)
            dve.wait_ge(sem("taps_out"), 32)
            step(v.memset(XK, 0.0))
            dve.sem_inc(sem("xk_cleared"), 1)
            step(v.tensor_copy(ur, cs))
            step(v.tensor_copy(ui, th))
            for _ in range(3):
                cmul(qr_, qi_, ur, ui, ur, ui, t1, t2)
                step(v.tensor_copy(ur, qr_))
                step(v.tensor_copy(ui, qi_))
            tt(t1, ur, ur, ALU.mult)
            tt(t2, ui, ui, ALU.mult)
            tt(t1, t1, t2, ALU.add)
            ts(t1, t1, -0.5, 1.5, ALU.mult, ALU.add)
            tt(ur, ur, t1, ALU.mult)
            tt(ui, ui, t1, ALU.mult)
            for q, (o, x, y, op) in enumerate(((SHR, H0R, H0I, ALU.subtract), (SHI, H0I, H0R, ALU.add))):
                x, y = (z.rearrange("p (r n) -> p r n", n=NS) for z in (x, y))
                tt(o, x, spread(lbr, NS), ALU.mult)
                tt(SHT, y, spread(lbi, NS), ALU.mult)
                tt(o, o, SHT, op)
            dve.wait_ge(sem("ssk_ready"), 1)
            v.tensor_scalar(ssk, ssk, 1.0 / D, EPS, ALU.mult, ALU.add).then_inc(sem("vark_ready"), 1)
            dve.wait_ge(sem("rootk_ready"), 1)
            v.reciprocal(ssk, ssk).then_inc(sem("rstdk_ready"), 1)
            dve.wait_ge(sem("xk_scaled"), 1)
            dve.wait_ge(sem("norm_in"), 48)
            ring.wait_full(dve, "mt", 7)

            def u_out(q):
                take(dve, "u", q)
                give(dve, v.tensor_copy(U[:, 8 * q:8 * q + 8].rearrange("p (b j) n -> p b (j n)", b=2),
                                        slot("u", q)[:, :, 0:4 * UC]), "u", q)
            for q in range(8):
                if q >= 2:
                    ring.wait_full(dve, "u", q - 2)
                tt(XR[q % 2].rearrange("p (g l c) -> p l g c", g=8, l=L),
                   XK[:, :, q * P:(q + 1) * P].rearrange("p l (g c) -> p l g c", c=CW),
                   spread_mid(GB[0:UC, q * P:(q + 1) * P], L).rearrange("p l (g c) -> p l g c", c=CW), ALU.mult)
                dve.sem_inc(sem("xr_ready"), 1)
                if q >= 2 and q % 2 == 0:
                    u_out(q - 2)
            u_out(6)
            ring.wait_full(dve, "u", 7)
            step(v.memset(TC[:, :, 0:1], 1.0))
            step(v.memset(TS[:, :, 0:1], 0.0))
            m = 1
            while m < NCH:
                cmul(TC[:, :, m:2 * m], TS[:, :, m:2 * m], TC[:, :, 0:m], TS[:, :, 0:m], spread(ur, m), spread(ui, m),
                     TMP[:, :, 0:m], TMP[:, :, m:2 * m])
                cmul(qr_, qi_, ur, ui, ur, ui, t1, t2)
                step(v.tensor_copy(ur, qr_))
                step(v.tensor_copy(ui, qi_))
                m *= 2
            step(v.tensor_copy(R8, spread(mag8, NCH)))
            step(v.memset(R8[:, :, 0:1], 0.0))
            for q in range(8):
                take(dve, "zs", q)
                z = slot("zs", q)[:, :, 0:4 * SC].rearrange("p r (j n) -> p r j n", j=4)
                zr, zi = z[:, 0, :, NS:SC], z[:, 1, :, NS:SC]
                rr, ri, tc, ts_, tm = (b[:, 4 * q:4 * q + 4] for b in (RR, RI, TC, TS, TMP))
                tt(rr, zr, tc, ALU.mult)
                tt(tm, zi, ts_, ALU.mult)
                tt(rr, rr, tm, ALU.add)
                tt(ri, zi, tc, ALU.mult)
                tt(tm, zr, ts_, ALU.mult)
                tt(ri, ri, tm, ALU.subtract)
                sr, si = SHR[:, 4 * q:4 * q + 4], SHI[:, 4 * q:4 * q + 4]
                tt(sr, sr, z[:, 0, :, 0:NS], ALU.add)
                give(dve, v.tensor_tensor(si, si, z[:, 1, :, 0:NS], ALU.add), "zs", q)
            for b in (RR, RI):
                f = b.rearrange("p r k -> p (r k)")
                step(v.tensor_tensor_scan(f, R8.rearrange("p r k -> p (r k)"), f, 0.0, ALU.mult, ALU.add))
            n = NCH - 1
            for o, x, y, op in ((HR, RR, RI, ALU.subtract), (HI, RI, RR, ALU.add)):
                step(v.memset(o[:, :, 0:1], 0.0))
                tt(o[:, :, 1:NCH], x[:, :, 0:n], TC[:, :, 0:n], ALU.mult)
                tt(TMP[:, :, 0:n], y[:, :, 0:n], TS[:, :, 0:n], ALU.mult)
                tt(o[:, :, 1:NCH], o[:, :, 1:NCH], TMP[:, :, 0:n], op)
            step(v.tensor_copy(HR[:, :, NCH:SC], H0R.rearrange("p (r n) -> p r n", n=NS)))
            step(v.tensor_copy(HI[:, :, NCH:SC], H0I.rearrange("p (r n) -> p r n", n=NS)))
            for q, (x, y, op) in enumerate(((RR, RI, ALU.subtract), (RI, RR, ALU.add))):
                tt(HEND[:, q], x[:, :, n], TC[:, :, n], ALU.mult)
                tt(t1, y[:, :, n], TS[:, :, n], ALU.mult)
                tt(HEND[:, q], HEND[:, q], t1, op)
            dve.sem_inc(sem("states_in"), 1)
            dve.sem_inc(sem("s5_end"), 1)
            for q in range(0, 8, 2):
                take(dve, "y", q)
                step(v.tensor_copy(*y_views(q, 0)))
                give(dve, v.tensor_copy(*y_views(q, 1)), "y", q)
            for i in range(5):
                for ch in range(2):
                    q = 2 * i + ch
                    n = ROWS[i]
                    take(dve, "gl", i, ch)
                    dve.wait_ge(sem("sig_ready"), q + 1)
                    ins = v.tensor_tensor(GT[q % 2][0:n], slot("gl", i, ch)[0:n, 0, :], SIG[q % 2][0:n], ALU.mult)
                    give(dve, ins, "gl", i, ch)
                    dve.sem_inc(sem("sig_used"), 1)
                    xs = X[0:n, i, 512 * ch:512 * ch + 512]
                    tt(xs, xs, GT[q % 2][0:n], ALU.add)
                dve.sem_inc(sem("x_tile"), 1)
            dve.wait_ge(sem("stored"), 16 * 11)
            dve.sem_inc(sem("x_mixed"), 1)
            router(1)
            experts(1)
            norm_scale(dve, step, 4, HC)

        @block.gpsimd
        def _(pool):
            g_ = nc.gpsimd
            chain = [0]

            def step(ins):
                chain[0] += 1
                ins.then_inc(sem("pool_steps"), 1)
                pool.wait_ge(sem("pool_steps"), chain[0])

            pool.wait_ge(sem("u_in"), 1)
            ring.wait_full(pool, "ws")
            ring.wait_emptied(pool, "kv", TILES - 1)
            for g in range(4):
                src = UE[:, g]
                for q in range(g + 1):
                    d = 2 ** q
                    dst = TU[q % 2]
                    step(g_.tensor_tensor(dst[:, 2 * d - 1:528], src[:, 2 * d - 1:528], src[:, d - 1:528 - d], ALU.add))
                    src = dst
                other = TU[(g + 1) % 2]
                step(g_.tensor_scalar(other[:, CW:528], src[:, CW:528], 2.0 ** -(g + 1), None, ALU.mult))
                ramp = const("ramp")[:, CW * g:CW * g + CW]
                step(g_.tensor_tensor(other[:, CW:2 * CW], src[:, CW:2 * CW], ramp, ALU.mult))
                step(g_.tensor_tensor(DT[:, g, 0:SEQ], other[:, CW:528], UE[:, g, CW:528], ALU.subtract))
                if g == 0:
                    pool.wait_ge(sem("ws_done"), 1)
                pool.sem_inc(sem("pool_mixed"), 1)

            def experts(l):
                pool.wait_ge(sem(f"h_out_{l}"), 80)
                pool.wait_ge(sem("xg_cleared"), l + 1)

                def turns(r):
                    pool.wait_ge(sem(f"list_read_{l}"), r + 1)
                    pool.sem_inc(sem("round_marks"), 1)
                    with pool.Fori(0, E // 2) as k:
                        t = k + 16 * r
                        pool.wait_ge(sem(f"xt_done_{l}"), 2 * t + 2)
                        g_.tensor_copy(idx_now[:, :], idx_list[:, bass.ds(2 * k, 2)]).then_inc(sem(f"idx_{l}"), 1)
                        pool.wait_ge(sem(f"idx_{l}"), t + 1)
                        pool.sem_inc(sem("turn_marks"), 1)
                        for s in range(2):
                            g_.indirect_dma_start(out=XG[s], out_offset=None, in_=hd_halves,
                                                  in_offset=bass.IndirectOffsetOnAxis(ap=idx_now[:, s:s + 1], axis=0),
                                                  bounds_check=2 * NT - 1, oob_is_err=False
                                                  ).then_inc(sem(f"xg_in_{l}_{s}"), 16)
                    g_.memset(YG, 0.0).then_inc(sem(f"yg_cleared_{l}"), 1)
                    pool.wait_ge(sem(f"yg_cleared_{l}"), r + 1)
                    pool.wait_ge(sem(f"y_all_out_{l}"), r + 1)
                    pool.sem_inc(sem("round_marks"), 1)
                    for q in range(10):
                        i, j, m = q // 2, q % 2, ROWS[q // 2]
                        g_.indirect_dma_start(out=YG[0:m, q], out_offset=None, in_=yd_rows,
                                              in_offset=bass.IndirectOffsetOnAxis(
                                                  ap=idx_back[0:m, 5 * j + i:5 * j + i + 1], axis=0),
                                              bounds_check=E * CAP - 1, oob_is_err=False
                                              ).then_inc(sem(f"yg_in_{l}_{i}"), 16)
                turns(0)
                n = pool.value_load(most[0:1, l:l + 1], min_val=0, max_val=NT)
                with pool.Fori(1, ROUNDS) as r:
                    with pool.If(n > r * CAP):
                        turns(r)

            experts(0)
            experts(1)


_SHAPES = dict(hd=(NT, D), yd=(E, CAP, D), sdk=(NS, 512), sdq=(NS, 512), sdd=(NS, H), kp=(D, KROW))
_OUT = dict(y=(NT, D), pool_s=(NS, 14, 512), pool_p=(P, H, 15), pool_us=(P, H, NS), n_s=(NS, 512), m_s=(NS, H),
            c_s=(P, NS * H, P), cn_p=(P, H, 129), m_p=(H, 1), s5_p=(P, 2, PAIRS), s5_sr=(P, PAIRS, NS),
            s5_si=(P, PAIRS, NS))


def kernel(**inputs):
    import concourse.bacc as bacc
    from concourse.bass_utils import run_bass_kernel_spmd

    n = {k: np.asarray(a) for k, a in inputs.items()}

    def kmajor(w):
        return w.reshape(KC, P, -1).transpose(1, 0, 2)

    def rep(a):
        return np.broadcast_to(a, (P,) + a.shape)

    def groups(a):
        a = a.reshape((PAIRS, P) + a.shape[2:])
        return a.swapaxes(0, 1)

    w = n["w_in_ab"][0]
    cols = [w[:, 1024:1536], w[:, 512:1024], w[:, 1536:2048], w[:, 0:512], w[:, 2048:2560]]
    w_in = np.stack([kmajor(c[:, 256 * b:256 * b + 256]) for c in cols for b in range(2)])
    gate, up = n["moe_w_gate"], n["moe_w_up"]
    gu = np.concatenate([gate[..., 0:P], up[..., 0:P], gate[..., P:], up[..., P:]], axis=-1)
    gu = gu.reshape(2, E, KC, P, 512).transpose(0, 1, 3, 2, 4)
    down = n["moe_w_down"].reshape(2, E, 2, P, D).transpose(0, 1, 3, 2, 4)
    glu = n["w_glu"][0]
    arrays = dict(
        const=constants(), x_prompt=n["x_prompt"][0], x_sample=n["x_sample"][:, 0],
        norms=np.stack([rep(a) for a in (n["norm_mix"][0], n["norm_ffn"][0], n["norm_mix"][1], n["norm_ffn"][1],
                                         n["norm_final"])]),
        w_gate8=kmajor(w[:, 2560:2568]), b_gates=n["b_gates"][0].reshape(2, H).T, m0=n["state_mlstm_m"][0],
        pool_scale=n["pool_scale"][0].reshape(H, P).T,
        w_router=np.stack([kmajor(np.concatenate([n["moe_w_group"][l], n["moe_w_expert"][l]], -1)) for l in range(2)]),
        b_router=np.stack([rep(np.concatenate([n["moe_b_group"][l], n["moe_b_expert"][l]])) for l in range(2)]),
        pool_w=n["pool_w"][0].transpose(1, 0, 2), pool_rows=n["state_pool"][0].reshape(120, 512),
        pool_buf=n["state_pool"][0][:, 1:], n0=n["state_mlstm_n"][0].reshape(NS, 512), w_in=w_in,
        w_out=kmajor(n["w_out_ab"][0]), c0=n["state_mlstm_c"][0].reshape(NS * H, P, P).transpose(1, 0, 2),
        w_gu=gu, w_down=down,
        s5_cb=np.stack([groups(a) for a in (n["s5_c_re"][0].swapaxes(1, 2), n["s5_c_im"][0].swapaxes(1, 2),
                                            n["s5_b_re"][0], n["s5_b_im"][0])]),
        s5_ls=groups(np.broadcast_to(n["s5_log_step"][0][:, None], (GU, 64))),
        s5_lr=groups(n["s5_lam_re"][0]), s5_li=groups(n["s5_lam_im"][0]), s5_d=n["s5_d"][0].reshape(KC, P).T,
        s5_h0r=groups(n["state_s5_re"][0].transpose(1, 2, 0)).reshape(P, -1),
        s5_h0i=groups(n["state_s5_im"][0].transpose(1, 2, 0)).reshape(P, -1),
        w_glu=np.stack([kmajor(np.concatenate([glu[:, 512 * c:512 * c + 512], glu[:, D + 512 * c:D + 512 * c + 512]], -1))
                        for c in range(2)]),
    )
    nc = bacc.Bacc("TRN2", target_bir_lowering=False, num_devices=1)
    T, feed = {}, {}
    for k, a in arrays.items():
        feed[f"in_{k}"] = a = np.ascontiguousarray(a)
        T[k] = nc.dram_tensor(f"in_{k}", a.shape, mybir.dt.from_np(a.dtype), kind="ExternalInput").ap()
    for k, s in _OUT.items():
        T[k] = nc.dram_tensor(f"out_{k}", s, F32, kind="ExternalOutput").ap()
    for k, s in _SHAPES.items():
        T[k] = nc.dram_tensor(f"scratch_{k}", s, F32, kind="Internal").ap()
    bass_hybrid_step(nc, T)
    r = run_bass_kernel_spmd(nc, [feed], core_ids=[0]).results[0]
    o = {k: np.asarray(r[f"out_{k}"]) for k in _OUT}

    def ungroup(a):
        a = a.swapaxes(0, 1)
        return a.reshape((GU, 64) + a.shape[2:])

    us = o["pool_us"].transpose(2, 1, 0).reshape(NS, 1, 512)
    cn = o["cn_p"].transpose(1, 2, 0)
    return (o["y"][None, :SEQ], o["y"][SEQ:, None],
            o["pool_p"].transpose(2, 1, 0).reshape(1, 1, 15, 512), cn[None, None, :, :P], cn[None, None, :, P],
            o["m_p"][:, 0][None, None], ungroup(o["s5_p"][:, 0])[None, None], ungroup(o["s5_p"][:, 1])[None, None],
            np.concatenate([o["pool_s"], us], axis=1)[None],
            o["c_s"].transpose(1, 0, 2).reshape(1, NS, H, P, P), o["n_s"].reshape(1, NS, H, P), o["m_s"][None],
            ungroup(o["s5_sr"]).transpose(2, 0, 1)[None], ungroup(o["s5_si"]).transpose(2, 0, 1)[None])
```

```python
from contextlib import ExitStack
from math import pi

import numpy as np

import concourse.bass as bass
from concourse import mybir

F32 = mybir.dt.float32
I32 = mybir.dt.int32
ALU = mybir.AluOpType
ACT = mybir.ActivationFunctionType
AX = mybir.AxisListType.X

P = 128
D = 1024
KC = D // P
SEQ = 512
NS = 8
NT = SEQ + NS
TILES = SEQ // P
ROWS = [P] * TILES + [NS]
HALF = NT // 2
H = 4
GU = 64
PAIRS = GU // 2
CW = 16
L = P // CW
NCH = SEQ // L
UC = NS + NCH + NS
SC = NCH + NS
E = 32
CAP = 64
ROUNDS = -(-NT // CAP)
EPS = 1e-6
BIG = 1e30
KSCALE = float(P) ** -0.5
KROW = 2 * P - CW
KZERO = KROW - P

CONST = {}
_at = 0
for _name, _n in [("ident", P), ("before", P), ("ones", P), ("causal", P), ("window", 4 * NS),
                  ("iota", P), ("eio", E), ("reve", E), ("revg", 4), ("tokid", 5), ("valid", 5),
                  ("half", 1), ("ramp", 4 * CW), ("head", 4 * P), ("keep", SEQ), ("diag", CW)]:
    CONST[_name] = (_at, _n)
    _at += _n
CONSTS = _at


def constants():
    c = np.zeros((P, CONSTS), np.float32)

    def put(name, a):
        at, n = CONST[name]
        c[:a.shape[0], at:at + n] = a.reshape(a.shape[0], n)

    p = np.arange(P)
    put("ident", np.eye(P, dtype=np.float32))
    put("before", (p[:, None] < p[None, :]).astype(np.float32))
    put("ones", np.ones((P, P), np.float32))
    put("causal", np.where(p[:, None] <= p[None, :], 0.0, -BIG).astype(np.float32))
    w = np.zeros((120, 4, NS), np.float32)
    for g in range(4):
        for n in range(NS):
            w[n * 15 + 15 - (2 ** (g + 1) - 1):n * 15 + 15, g, n] = 1.0
    put("window", w)
    put("iota", np.tile(np.arange(CAP, dtype=np.float32), (P, 2)))
    put("eio", np.tile(np.arange(E, dtype=np.float32), (P, 1)))
    put("reve", np.tile(E - np.arange(E, dtype=np.float32), (P, 1)))
    put("revg", np.tile(4 - np.arange(4, dtype=np.float32), (P, 1)))
    put("tokid", (np.arange(5)[None, :] * P + p[:, None] + 1).astype(np.float32))
    v = np.ones((P, 5), np.float32)
    v[NS:, 4] = 0
    put("valid", v)
    put("half", (p[:, None] >= CAP).astype(np.float32) - 2.0)
    t = np.arange(CW)
    put("ramp", np.tile(np.stack([1.0 / np.minimum(2 ** (g + 1), t + 1) for g in range(4)])[None],
                        (P, 1, 1)).astype(np.float32))
    h = np.zeros((4, 4, P), np.float32)
    for i in range(4):
        h[i, i] = 1.0
    put("head", h)
    k = np.ones((4, SEQ), np.float32)
    k[:, ::P] = 0
    put("keep", k)
    put("diag", (p[:, None] % CW == t[None, :]).astype(np.float32))
    return c


X_AT = 0
CONST_AT = X_AT + 5 * D
GB_AT = CONST_AT + CONSTS + CONSTS % 2
WR_AT = GB_AT + D
SMALL_AT = WR_AT + 2 * (KC * 36 + 36)
STAGE_AT = SMALL_AT + 2198
ARENA = 207 * 256


class PsumRing:

    def __init__(self, jobs, full, freed):
        self.jobs, self.full, self.freed = jobs, full, freed
        self.at = {name: n for n, (name, _) in enumerate(jobs)}
        assert len(self.at) == len(jobs)
        seen, self.count = {}, []
        for _, eng in jobs:
            seen[eng] = seen.get(eng, 0) + 1
            self.count.append(seen[eng])

    def slot(self, *name):
        return self.at[name] % 4

    def wait_free(self, pe, *name):
        n = self.at[name]
        if n >= 4:
            self.wait_emptied(pe, *self.jobs[n - 4][0])

    def wait_full(self, eng, *name):
        eng.wait_ge(self.full, self.at[name] + 1)

    def wait_emptied(self, eng, *name):
        n = self.at[name]
        eng.wait_ge(self.freed[self.jobs[n][1]], self.count[n])


def jobs_of_kernel():
    j = []
    for i in range(5):
        j.append((("ht", i), "act" if i % 2 else "dve"))
    j.append((("gates",), "dve"))
    for n in range(12):
        j.append((("z", n), "act"))
    j += [(("cols",), "dve"), (("sg",), "dve")]
    j += [(("bc", h), "dve") for h in range(H)]
    j += [(("st",), "dve")]
    for c in range(TILES):
        j += [(("kt", c), "dve"), (("s", c), "dve"), (("kv", c), "dve")]
    j += [(("z", n), "act") for n in range(12, 20)]
    j += [(("ws",), "dve")]
    for c in range(TILES):
        j += [(("num", c), "dve"), (("hT", c), "dve")]
    j += [(("pw", g), "act") for g in range(4)]
    j += [(("wo", i), "dve") for i in range(5)]

    def router(l):
        return [((k, l, i), e) for i in range(5) for k, e in (("tr", "act"), ("lg", "dve"))] + [(("pos", l), "dve")]
    j += router(0)
    j += [(("k",), "dve")]
    j += [(("u", q), "act" if q % 2 else "dve") for q in range(8)]
    j += [(("zs", q), "dve") for q in range(8)]
    j += [(("y", q), "act" if q % 2 else "dve") for q in range(8)]
    j += [(("yT", q), "act") for q in range(8)]
    j += [(("gl", ch, i), "dve") for ch in range(2) for i in range(5)]
    j += router(1)
    return j


def bass_hybrid_step(nc, T):
    ctx = ExitStack()
    with ctx:
        sems = {}

        def sem(name):
            if name not in sems:
                sems[name] = ctx.enter_context(nc.semaphore(name))
            return sems[name]

        arena = ctx.enter_context(nc.sbuf_tensor("arena", [P, ARENA], F32))
        idx_list = ctx.enter_context(nc.sbuf_tensor("idx_list", [P, E], I32))
        idx_now = ctx.enter_context(nc.sbuf_tensor("idx_now", [P, 2], I32))
        idx_back = ctx.enter_context(nc.sbuf_tensor("idx_back", [P, 10], I32))
        most = ctx.enter_context(nc.sbuf_tensor("most", [P, 2], I32))
        ps = ctx.enter_context(nc.psum_tensor("ps", [P, 8, 512], F32))

        def place(at, *shape, parts=P, base=0):
            n = int(np.prod(shape))
            assert at + n <= ARENA
            a = arena[base:base + parts, at:at + n]
            if len(shape) == 2:
                a = a.rearrange("p (a b) -> p a b", a=shape[0])
            if len(shape) == 3:
                a = a.rearrange("p (a b c) -> p a b c", a=shape[0], b=shape[1])
            if len(shape) == 4:
                a = a.rearrange("p (a b c d) -> p a b c d", a=shape[0], b=shape[1], c=shape[2])
            return a

        def const(name, parts=P):
            at, n = CONST[name]
            return arena[0:parts, CONST_AT + at:CONST_AT + at + n]

        def spread(a, n):
            a = a.unsqueeze(len(a.shape))
            return a.broadcast_to(tuple(a.shape[:-1]) + (n,))

        def spread_mid(a, n):
            a = a.unsqueeze(1)
            return a.broadcast_to((a.shape[0], n) + tuple(a.shape[2:]))

        ident, before, ones, causal = const("ident"), const("before"), const("ones"), const("causal")

        X = place(X_AT, 5, D)
        GB = place(GB_AT, D)
        WR = [place(WR_AT + l * (KC * 36 + 36), KC, 36) for l in range(2)]
        BR = [place(WR_AT + l * (KC * 36 + 36) + KC * 36, 36) for l in range(2)]

        small_at = [SMALL_AT]

        def small(*shape, parts=P):
            at = small_at[0]
            small_at[0] += int(np.prod(shape))
            assert small_at[0] <= STAGE_AT
            return place(at, *shape, parts=parts)

        ss, var, root, rstd = small(5), small(5), small(5), small(5)
        LG = small(5, 36)
        gmax, gtop, gsum, gw = small(5), small(5), small(5), small(5)
        og, gexp, gneg = small(5, 4), small(5, 4), small(5, 4)
        me, hit = small(5, E), small(5, E)
        oh = [small(5, E), small(5, E)]
        OH, PRE, POS = small(5, E), small(5, E), small(5, E)
        both = small(E)
        m1, m2, etop, dexp, dsum = small(5), small(5), small(5), small(5), small(5)
        pw_ = [small(5), small(5)]
        RK, EID, QR = small(2, 5), small(2, 5), small(2, 5)
        cntmax = small(1)
        m0s, SG, SM = small(H, parts=NS), small(8, parts=NS), small(12, parts=NS)
        gcol, dec = small(16), small(16)
        ecol = small(16)
        den, dab, rden = small(H), small(H), small(H)
        vs, us, sos = small(H, NS), small(H, NS), small(H, NS)
        rs = small(NS * H)
        bg, mrun = small(2, parts=H), small(TILES + 1, parts=H)
        pscale = small(H)
        sden = small(3 * H, parts=NS)

        A = STAGE_AT

        def slot(*name):
            s = ring.slot(*name)
            return ps[:, 2 * s:2 * s + 2, :]

        def slot_flat(*name):
            return slot(*name).rearrange("p b n -> p (b n)")

        ring = PsumRing(jobs_of_kernel(), sem("psum_full"),
                        {"dve": sem("psum_emptied_by_dve"), "act": sem("psum_emptied_by_act")})

        def take(eng, *name):
            ring.wait_full(eng, *name)

        def give(eng, ins, *name):
            who = ring.jobs[ring.at[name]][1]
            ins.then_inc(ring.freed[who], 1)
            ring.wait_emptied(eng, *name)

        HH = place(A, 5, D)
        KB = place(A, NS * H, P)
        HT = place(A + 5120, KC, NT)
        WIN = [place(A + 9280 + 2048 * b, KC, 256) for b in range(2)]
        WG8 = place(A + 40000, KC, 8)
        WOUT = place(A + 5120, KC, D)
        Zk, Zq, Zv, Zo = (place(A + 13376 + 2080 * n, H, NT) for n in range(4))
        MIX = place(A + 13376, KC, NT)
        HM = place(A + 17536, 2, H, P)
        W = place(A + 21696, H, TILES, P)
        V1 = place(A + 23744, TILES, H, 130)
        KT = place(A + 25824, TILES, H, P)
        DT = place(A + 25824, H, NT)
        UE = place(A + 27904, H, 528)
        QT = place(A + 30016, H, SEQ)
        CN = place(A + 32064, TILES, H, 129)
        KZ = place(A + 32064, KC, KZERO)
        TU = [place(A + 34128 + 528 * b, 528) for b in range(2)]
        rows = [place(A + 35184 + NT * n, NT, parts=H) for n in range(8)]
        li, lf, bc_, ar, mr, wi, er, tr_ = rows
        CS = place(A + 35184, NS * H, P)
        PW = place(A + 39344, H, P)
        PB = place(A + 34128, SEQ, parts=120)
        ks = place(A + 40500, H, P, parts=NS)
        n0s = place(A + 41012, H, P, parts=NS)
        qs = place(A + 1536, H, P, parts=NS)
        DB = place(A + 41524, NS * H)

        WGU = [place(A + 4096 * b, KC, 512) for b in range(2)]
        WD = [place(A + 8192 + 2048 * b, 2, D) for b in range(2)]
        XG = [place(A + 12288 + 512 * b, 512) for b in range(2)]
        XT = [place(A + 13312 + 512 * b, 4, P) for b in range(2)]
        SIL = [place(A + 14336 + P * b, P) for b in range(2)]
        ACTB = [place(A + 14592 + P * b, P) for b in range(2)]
        AT = [place(A + 14848 + P * b, P) for b in range(2)]
        YE = [place(A + 15104 + 512 * b, 512) for b in range(2)]
        OHR = place(A + 16128, 10, P)
        YG = place(A + 16128, 4, D)
        HB = place(A + 27648, 5, D)
        HTB = [place(A + 32768 + 1024 * b, KC, P) for b in range(2)]

        CIN = [place(A + 20224 + 512 * n, PAIRS, CW) for n in range(2)]
        VR, VI = place(A + 21248, 2, L, CW), place(A + 21504, 2, L, CW)
        S5_AT = A + 21760
        BBR, BBI = place(S5_AT, PAIRS, CW), place(S5_AT + 512, PAIRS, CW)
        sp_ = [place(S5_AT + 1024 + 32 * n, PAIRS) for n in range(20)]
        PWR, PWI = place(S5_AT + 1664, PAIRS, L + 1), place(S5_AT + 1952, PAIRS, L + 1)
        GTMP = place(S5_AT + 2240, 2, L + 1, CW)
        BACKR, BACKI = place(S5_AT + 1024 + 320, PAIRS, L), place(S5_AT + 2528, PAIRS, L)
        DSK = place(S5_AT + 2952, KC)
        BIN = [place(A + 24736 + 512 * n, PAIRS, CW) for n in range(2)]
        BTMP = [place(A + 30016 + 512 * n, PAIRS, CW) for n in range(2)]
        M = place(A + 24736, PAIRS, 2, P)
        GR, GI = place(A + 32928, PAIRS, L + 1, CW), place(A + 37536, PAIRS, L + 1, CW)

        HC = place(A + 27648, 5, D)
        H2 = place(A, 5, D)
        U = place(A, GU, UC)
        XK = place(A + 5120, L, D, parts=UC)
        HR, HI = place(A + 5120, PAIRS, SC), place(A + 7424, PAIRS, SC)
        RR, RI = place(A + 9728, PAIRS, NCH), place(A + 11776, PAIRS, NCH)
        TMQ = place(A + 13824, 4, NCH)
        BD = [place(A + 13312 + 1024 * n, PAIRS, 2 * CW) for n in range(2)]
        XR = [place(A + 13312 + 1024 * b, D, parts=UC) for b in range(2)]
        TC, TS = place(A + 15360, PAIRS, NCH), place(A + 17408, PAIRS, NCH)
        R8 = TMP = place(A + 19456, PAIRS, NCH)
        KS = place(S5_AT, KC, P)
        H0R, H0I = place(S5_AT + 1664, PAIRS * NS), place(S5_AT + 1920, PAIRS * NS)
        SHR, SHI, SHT = (place(S5_AT + 2176 + 256 * n, PAIRS, NS) for n in range(3))
        SKIP = place(A + 21504, KC, CW)
        HEND = place(A + 21632, 2, PAIRS)
        YK = place(A + 9728, L, D)
        TT = place(A + 24736, GU, P)
        YT = place(A, KC, NT)
        WGL = [place(A + 24736 + 8192 * ch, KC, D) for ch in range(2)]
        SIG = [place(A + 5120 + 512 * b, 512) for b in range(2)]
        GT = [place(A + 6144 + 512 * b, 512) for b in range(2)]

        def y_views(q, b):
            return (YK[0:SC, :, q * P:(q + 1) * P].rearrange("p l (j b c) -> p b j l c", b=2, c=CW)[:, b],
                    slot("y", q)[0:SC, b, :].rearrange("p (j l c) -> p j l c", j=4, l=L))

        hd, yd, kp = T["hd"], T["yd"], T["kp"]
        sdk, sdq, sdd = T["sdk"], T["sdq"], T["sdd"]
        hd_halves = hd.rearrange("t (h c) -> (t h) c", h=2)
        yd_rows = yd.rearrange("j t c -> (j t) c")

        block = ctx.enter_context(nc.Block())

        def tile_rows(a, i):
            return a[0:ROWS[i], i, :]

        @block.sync
        def _(sp):
            def load(dst, src, name):
                sp.dma_start(dst, src).then_inc(sem(name), 16)

            load(place(CONST_AT, CONSTS), T["const"], "consts")
            for i in range(TILES):
                load(X[:, i, :], T["x_prompt"][i * P:(i + 1) * P, :], f"x_in_{i}")
            sp.wait_ge(sem("x_cleared"), 1)
            load(X[0:NS, TILES, :], T["x_sample"], f"x_in_{TILES}")
            load(GB, T["norms"][0], "norm_in")
            load(WG8, T["w_gate8"], "w_gates_in")
            load(bg, T["b_gates"], "small_in")
            load(m0s, T["m0"], "small_in")
            load(pscale, T["pool_scale"], "small_in")
            for l in range(2):
                load(WR[l], T["w_router"][l], "small_in")
                load(BR[l], T["b_router"][l], "small_in")
            load(PW, T["pool_w"], "pool_in")
            load(PB, T["pool_rows"], "pool_in")
            load(n0s, T["n0"], "n0_in")
            kv = kp.rearrange("(b p) n -> p b n", p=P)
            sp.wait_ge(sem("kz_cleared"), 1)
            sp.dma_start(kv[:, :, 0:KZERO], KZ).then_inc(sem("kz_out"), 16)
            for n in range(10):
                if n >= 2:
                    ring.wait_full(sp, "z", 2 * (n - 2) + 1)
                load(WIN[n % 2], T["w_in"][n], f"w_in_{n % 2}")
            sp.wait_ge(sem("h_0"), 5)
            load(GB, T["norms"][1], "norm_in")
            sp.dma_start(T["pool_s"], T["pool_buf"]).then_inc(sem("stored"), 16)
            sp.wait_ge(sem("rows_dead"), 1)
            load(CS, T["c0"], "c0_in")
            ring.wait_full(sp, "z", 19)
            load(WOUT, T["w_out"], "w_out_in")
            sp.wait_ge(sem("ks_ready"), 1)
            sp.dma_start(sdk, ks.rearrange("p h k -> p (h k)")).then_inc(sem("sd_out"), 16)
            sp.dma_start(sdd, SM[:, 0:H]).then_inc(sem("sd_out"), 16)
            sp.dma_start(sdq, qs.rearrange("p h k -> p (h k)")).then_inc(sem("sd_out"), 16)
            sp.dma_start(T["n_s"], n0s.rearrange("p h k -> p (h k)")).then_inc(sem("stored"), 16)
            sp.dma_start(T["m_s"], sden[:, 0:H]).then_inc(sem("stored"), 16)
            sp.wait_ge(sem("sd_out"), 48)
            load(KB, sdk.rearrange("n (h k) -> (n h) k", h=H).partition_broadcast(P), "kb_in")
            load(DB, sdd.rearrange("n h -> (n h)").partition_broadcast(P), "kb_in")
            ring.wait_full(sp, "num", TILES - 1)
            for n in range(2):
                load(BIN[n], T["s5_cb"][2 + n], "s5_in")
            load(sp_[0], T["s5_ls"], "s5_in")
            load(sp_[1], T["s5_lr"], "s5_in")
            load(sp_[2], T["s5_li"], "s5_in")
            load(DSK, T["s5_d"], "s5_in")
            sp.wait_ge(sem("kb_used"), 1)
            load(KB, sdq.rearrange("n (h k) -> (n h) k", h=H).partition_broadcast(P), "qb_in")
            sp.wait_ge(sem("cs_ready"), 1)
            sp.dma_start(T["c_s"], CS).then_inc(sem("stored"), 16)
            sp.wait_ge(sem("us_ready"), 1)
            sp.dma_start(T["pool_p"], UE[:, :, 528 - 15:528]).then_inc(sem("stored"), 16)
            sp.dma_start(T["pool_us"], us).then_inc(sem("stored"), 16)
            sp.wait_ge(sem("cn_ready"), 1)
            sp.dma_start(T["cn_p"], CN[:, TILES - 1]).then_inc(sem("stored"), 16)
            sp.dma_start(T["m_p"], mrun[:, TILES:TILES + 1]).then_inc(sem("stored"), 16)

            def experts(l):
                def turns(r):
                    with sp.Fori(0, E // 2) as k:
                        t = k + 16 * r
                        for s in range(2):
                            sp.wait_ge(sem(f"gu_done_{l}"), 2 * t + 2)
                            e = 2 * k + s
                            sp.dma_start(WGU[s], T["w_gu"][l][bass.ds(e, 1)].rearrange("e p k n -> p (e k) n")
                                         ).then_inc(sem(f"wgu_in_{l}_{s}"), 16)
                        for s in range(2):
                            sp.wait_ge(sem(f"down_done_{l}"), 2 * t + 2)
                            e = 2 * k + s
                            sp.dma_start(WD[s], T["w_down"][l][bass.ds(e, 1)].rearrange("e p k n -> p (e k) n")
                                         ).then_inc(sem(f"wd_in_{l}_{s}"), 16)
                turns(0)
                sp.wait_ge(sem(f"h_{2 * l + 1}"), 5)
                load(GB, T["norms"][2 * l + 2], "norm_in")
                sp.wait_ge(sem("most_ready"), l + 1)
                n = sp.value_load(most[0:1, l:l + 1], min_val=0, max_val=NT)
                with sp.Fori(1, ROUNDS) as r:
                    with sp.If(n > r * CAP):
                        turns(r)

            sp.wait_ge(sem("x_mixed"), 1)
            for n in range(2):
                load(CIN[n], T["s5_cb"][n], "s5_in")
            experts(0)
            sp.wait_ge(sem("x_moe"), 1)
            load(H0R, T["s5_h0r"], "s5_in")
            load(H0I, T["s5_h0i"], "s5_in")
            sp.wait_ge(sem("xk_cleared"), 2)
            for i in range(5):
                sp.wait_ge(sem("h_2"), i + 1)
                if i < TILES:
                    n = NS + i * P // L
                    load(XK[n:n + P // L], H2[:, i, :], "xk_in")
            load(XK[0:NS, L - 1, :], H2[0:NS, TILES], "xk_in")
            load(XK[NS + NCH:UC, 0, :], H2[0:NS, TILES], "xk_in")
            load(GB, T["norms"][3], "norm_in")
            sp.wait_ge(sem("taps_ready"), 1)
            sp.dma_start(kv[:, :, KZERO:KROW], KS).then_inc(sem("taps_out"), 16)
            sp.wait_ge(sem("taps_out"), 16)
            sp.wait_ge(sem("kz_out"), 16)
            ring.wait_full(sp, "zs", 7)
            kg = kp.rearrange("(g c) n -> c g n", c=CW)
            for s in range(L):
                load(TT[CW * s:CW * s + CW], kg[:, :, KZERO - CW * s:KZERO - CW * s + P], "taps_in")
            sp.wait_ge(sem("s5_end"), 1)
            sp.dma_start(T["s5_p"], HEND).then_inc(sem("stored"), 16)
            sp.dma_start(T["s5_sr"], SHR).then_inc(sem("stored"), 16)
            sp.dma_start(T["s5_si"], SHI).then_inc(sem("stored"), 16)
            ring.wait_full(sp, "y", 3)
            load(WGL[0][:, 0:4], T["w_glu"][0][:, 0:4], "w_glu_in_0")
            ring.wait_full(sp, "y", 7)
            load(WGL[0][:, 4:8], T["w_glu"][0][:, 4:8], "w_glu_in_1")
            load(WGL[1], T["w_glu"][1], "w_glu_in_2")
            sp.wait_ge(sem("x_mixed"), 2)
            experts(1)
            for i in range(5):
                sp.wait_ge(sem("h_4"), i + 1)
                sp.dma_start(T["y"][i * P:i * P + ROWS[i], :], tile_rows(HC, i)).then_inc(sem("stored"), 16)
            sp.wait_ge(sem("stored"), 16 * (1 + 2 + 1 + 2 + 2 + 3 + 5))

        @block.tensor
        def _(pe):
            def full(mm):
                mm.then_inc(ring.full, 1)

            def transposes(name, pieces):
                ring.wait_free(pe, *name)
                for out, in_ in pieces:
                    k = in_.shape[0]
                    mm = pe.transpose(out, in_, ident[0:k, 0:k])
                full(mm)

            pe.sem_inc(sem("m_turned"), 1)
            for l in range(2):
                for name in ("gu_done", "down_done", "xt_done"):
                    pe.sem_inc(sem(f"{name}_{l}"), 2)
            pe.wait_ge(sem("consts"), 16)
            for i in range(5):
                n = ROWS[i]
                pe.wait_ge(sem("h_0"), i + 1)
                o = slot("ht", i)
                transposes(("ht", i), [(o[:, kc // 4, (kc % 4) * P:(kc % 4) * P + n], HH[0:n, i, kc * P:(kc + 1) * P])
                                       for kc in range(KC)])
            pe.wait_ge(sem("w_gates_in"), 16)
            for i in range(5):
                ring.wait_emptied(pe, "ht", i)
            ring.wait_free(pe, "gates")
            o = slot("gates")
            for b in range(2):
                for kc in range(KC):
                    for q in range(2):
                        mm = pe.matmul(o[32 * q:32 * q + H, b, 0:HALF], WG8[:, kc, H * q:H * q + H],
                                       HT[:, kc, b * HALF:(b + 1) * HALF], start=kc == 0, stop=kc == KC - 1)
            full(mm)

            def project(n):
                if n % 2 == 0:
                    pe.wait_ge(sem(f"w_in_{(n // 2) % 2}"), 16 * (n // 4 + 1))
                ring.wait_free(pe, "z", n)
                o = slot("z", n)
                w = WIN[(n // 2) % 2]
                for kc in range(KC):
                    for b in range(2):
                        mm = pe.matmul(o[:, b, 0:HALF], w[:, kc, (n % 2) * P:(n % 2 + 1) * P],
                                       HT[:, kc, b * HALF:(b + 1) * HALF], start=kc == 0, stop=kc == KC - 1)
                full(mm)

            for n in range(12):
                project(n)
            pe.wait_ge(sem("gate_rows"), 1)
            o = slot_flat("cols")
            transposes(("cols",), [(o[:, 16 * q + H * c:16 * q + H * c + H], (ar, er)[q][:, c * P:(c + 1) * P])
                                   for q in range(2) for c in range(TILES)])
            o = slot_flat("sg")
            transposes(("sg",), [(o[0:NS, 0:H], li[:, SEQ:NT]), (o[0:NS, H:2 * H], lf[:, SEQ:NT])])
            for h in range(H):
                ring.wait_free(pe, "bc", h)
                o = slot("bc", h)
                pick = const("head", H)[:, h * P:(h + 1) * P]
                pe.matmul(o[:, 0, :], pick, mr[:, 0:SEQ], start=True, stop=True)
                full(pe.matmul(o[:, 1, :], pick, wi[:, 0:SEQ], start=True, stop=True))
            ring.wait_emptied(pe, "z", 11)
            o = slot("st")
            transposes(("st",), [(o[0:NS, q, h * P:(h + 1) * P], (Zk, Zq)[q][:, h, SEQ:NT])
                                 for q in range(2) for h in range(H)])
            for c in range(TILES):
                cc = slice(c * P, (c + 1) * P)
                o = slot("kt", c)
                transposes(("kt", c), [(o[:, q, h * P:(h + 1) * P], (Zk, Zv)[q][:, h, cc])
                                       for q in range(2) for h in range(H)])
                ring.wait_free(pe, "s", c)
                o = slot("s", c)
                for h in range(H):
                    mm = pe.matmul(o[:, 0, h * P:(h + 1) * P], Zk[:, h, cc], Zq[:, h, cc], start=True, stop=True)
                full(mm)
                ring.wait_emptied(pe, "kt", c)
                ring.wait_free(pe, "kv", c)
                o = slot("kv", c)
                for h in range(H):
                    mm = pe.matmul(o[:, h // 2, (h % 2) * 129:(h % 2) * 129 + 129], KT[:, c, h], V1[:, c, h, 0:129],
                                   start=True, stop=True)
                full(mm)
            for n in range(12, 20):
                project(n)
            pe.wait_ge(sem("pool_in"), 32)
            ring.wait_free(pe, "ws")
            o = slot_flat("ws")
            for g in range(4):
                mm = pe.matmul(o[:, g * NS:(g + 1) * NS], PB[:, g * P:(g + 1) * P],
                               const("window")[0:120, g * NS:(g + 1) * NS], start=True, stop=True)
            full(mm)
            for c in range(TILES):
                ring.wait_free(pe, "num", c)
                ring.wait_emptied(pe, "s", c)
                if c:
                    ring.wait_emptied(pe, "kv", c - 1)
                o = slot("num", c)
                for h in range(H):
                    out = o[:, h // 2, (h % 2) * 129:(h % 2) * 129 + 129]
                    mm = pe.matmul(out, W[:, h, c], V1[:, c, h, 0:129], start=True, stop=c == 0)
                    if c:
                        mm = pe.matmul(out, QT[:, h, c * P:(c + 1) * P], CN[:, c - 1, h], start=False, stop=True)
                full(mm)
                ring.wait_emptied(pe, "num", c)
                o = slot("hT", c)
                transposes(("hT", c), [(o[:, 0, h * P:(h + 1) * P], HM[:, c % 2, h]) for h in range(H)])
            for g in range(4):
                pe.wait_ge(sem("pool_mixed"), g + 1)
                ring.wait_free(pe, "pw", g)
                o = slot("pw", g)
                for b in range(2):
                    mm = pe.matmul(o[:, b, 0:HALF], PW[:, g], DT[:, g, b * HALF:(b + 1) * HALF], start=True, stop=True)
                full(mm)
            pe.wait_ge(sem("w_out_in"), 16)
            for g in range(4):
                ring.wait_emptied(pe, "pw", g)
            ring.wait_emptied(pe, "hT", TILES - 1)
            for i in range(5):
                if i == TILES:
                    pe.wait_ge(sem("mix_samples"), 1)
                ring.wait_free(pe, "wo", i)
                o = slot("wo", i)
                n = ROWS[i]
                for kc in range(KC):
                    for b in range(2):
                        mm = pe.matmul(o[0:n, b, :], MIX[:, kc, i * P:i * P + n], WOUT[:, kc, b * 512:(b + 1) * 512],
                                       start=kc == 0, stop=kc == KC - 1)
                full(mm)

            def router(l):
                for i in range(5):
                    n = ROWS[i]
                    pe.wait_ge(sem(f"h_{2 * l + 1}"), i + 1)
                    if i >= 2:
                        ring.wait_emptied(pe, "lg", l, i - 2)
                    o = slot("tr", l, i)
                    transposes(("tr", l, i), [(o[:, kc // 4, (kc % 4) * P:(kc % 4) * P + n],
                                               HB[0:n, i, kc * P:(kc + 1) * P]) for kc in range(KC)])
                    ring.wait_emptied(pe, "tr", l, i)
                    ring.wait_free(pe, "lg", l, i)
                    o = slot_flat("lg", l, i)
                    for kc in range(KC):
                        mm = pe.matmul(o[0:n, 0:36], HTB[i % 2][:, kc, 0:n], WR[l][:, kc], start=kc == 0,
                                       stop=kc == KC - 1)
                    full(mm)
                pe.wait_ge(sem("chosen"), l + 1)
                ring.wait_free(pe, "pos", l)
                o = slot("pos", l)
                flat = "p t e -> p (t e)"
                pe.matmul(o[:, 0, 0:5 * E], before, OH.rearrange(flat), start=True, stop=False)
                pe.matmul(o[:, 0, 0:5 * E], ones, PRE.rearrange(flat), start=False, stop=True)
                full(pe.matmul(o[:, 1, 0:E], ones, both, start=True, stop=True))
                ring.wait_emptied(pe, "pos", l)

            def experts(l):
                def turns(r):
                    pe.wait_ge(sem(f"spots_{l}"), r + 1)
                    for q in range(10):
                        mm = pe.matmul(ps[:, 0, 0:E], OHR[:, q], oh[q // 5][:, q % 5], start=q == 0, stop=q == 9)
                    mm.then_inc(sem(f"list_done_{l}"), 1)
                    pe.wait_ge(sem(f"list_read_{l}"), r + 1)
                    pe.sem_inc(sem("round_marks"), 1)
                    with pe.Fori(0, E // 2) as k:
                        t = k + 16 * r
                        for s in range(2):
                            pe.wait_ge(sem(f"xg_in_{l}_{s}"), 16 * t + 16)
                            for b in range(4):
                                mm = pe.transpose(ps[:, s, b * P:(b + 1) * P], XG[s][:, b * P:(b + 1) * P], ident)
                            mm.then_inc(sem(f"xt_done_{l}"), 1)
                        for s in range(2):
                            pe.wait_ge(sem(f"wgu_in_{l}_{s}"), 16 * t + 16)
                            pe.wait_ge(sem(f"xt_ready_{l}"), 2 * t + s + 1)
                            for kc in range(KC):
                                for f in range(2):
                                    mm = pe.matmul(ps[CAP * f:CAP * f + CAP, 2 + s, 0:256],
                                                   XT[s][:, kc % 4, CAP * (kc // 4):CAP * (kc // 4) + CAP],
                                                   WGU[s][:, kc, 256 * f:256 * f + 256],
                                                   start=kc == 0, stop=kc == KC - 1)
                            mm.then_inc(sem(f"gu_done_{l}"), 1)
                        for s in range(2):
                            pe.wait_ge(sem(f"act_ready_{l}"), 2 * t + s + 3)
                            pe.transpose(ps[:, 4 + s, 0:P], ACTB[s], ident).then_inc(sem(f"at_done_{l}"), 1)
                        for s in range(2):
                            pe.wait_ge(sem(f"wd_in_{l}_{s}"), 16 * t + 16)
                            pe.wait_ge(sem(f"at_ready_{l}"), 2 * t + s + 1)
                            pe.wait_ge(sem(f"y_ready_{l}"), 2 * t + 2)
                            for f in range(2):
                                for b in range(2):
                                    mm = pe.matmul(ps[CAP * b:CAP * b + CAP, 6 + s, :], AT[s][:, CAP * f:CAP * f + CAP],
                                                   WD[s][:, f, 512 * b:512 * b + 512], start=f == 0, stop=f == 1)
                            mm.then_inc(sem(f"down_done_{l}"), 1)
                        if l == 0:
                            pe.wait_ge(sem("v_ready"), t + 1)
                            pe.wait_ge(sem("m_copied"), t + 1)
                            for j in range(2):
                                for ri in range(2):
                                    mm = pe.transpose(ps[:, 4 + j, P * (1 + ri):P * (2 + ri)],
                                                      (VR, VI)[ri][:, j].rearrange("p l c -> p (l c)"), ident)
                            mm.then_inc(sem("m_turned"), 1)
                    if l == 0:
                        pe.wait_ge(sem("m_copied"), 16 * r + 17)
                    pe.wait_ge(sem(f"y_ready_{l}"), E * r + E + 2)
                turns(0)
                n = pe.value_load(most[0:1, l:l + 1], min_val=0, max_val=NT)
                with pe.Fori(1, ROUNDS) as r:
                    with pe.If(n > r * CAP):
                        turns(r)

            router(0)
            experts(0)

            pe.wait_ge(sem("bd_ready"), 1)
            ring.wait_free(pe, "k")
            o = slot_flat("k")
            for pb in range(8):
                for pq in range(4):
                    pr = 4 * pb + pq
                    out = o[32 * pq:32 * pq + 32, pb * P:(pb + 1) * P]
                    pe.matmul(out, BD[0][:, pr], GR[:, pr, 0:L], start=True, stop=False)
                    mm = pe.matmul(out, BD[1][:, pr], GI[:, pr, 0:L], start=False, stop=True)
            full(mm)
            for q in range(8):
                pe.wait_ge(sem(f"xr_ready_{q % 2}"), q // 2 + 1)
                o = slot("u", q)
                transposes(("u", q), [(o[:, j // 4, (j % 4) * UC:(j % 4 + 1) * UC],
                                       XR[q % 2][:, j * P:(j + 1) * P]) for j in range(8)])
            for q in range(8):
                ring.wait_free(pe, "zs", q)
                ring.wait_emptied(pe, "u", q)
                o = slot("zs", q)
                for j in range(4):
                    pr = 4 * q + j
                    for ri in range(2):
                        for g2 in range(2):
                            mm = pe.matmul(o[64 * g2:64 * g2 + 64, ri, j * SC:(j + 1) * SC],
                                           M[:, pr, ri, 64 * g2:64 * g2 + 64], U[:, 2 * pr + g2, 0:SC],
                                           start=True, stop=True)
                full(mm)
            pe.wait_ge(sem("taps_in"), 16 * L)
            pe.wait_ge(sem("states_in"), 1)
            for q in range(8):
                ring.wait_free(pe, "y", q)
                o = slot("y", q)
                for j in range(8):
                    g = 8 * q + j
                    pr, lo = g // 2, 64 * (g % 2)
                    out = o[0:SC, j % 2, (j // 2) * P:(j // 2 + 1) * P]
                    pe.matmul(out, U[:, g, NS:UC], TT[:, g], start=True, stop=False)
                    pe.matmul(out, HR[lo:lo + 64, pr], GR[lo:lo + 64, pr, 1:L + 1], start=False, stop=False)
                    mm = pe.matmul(out, HI[lo:lo + 64, pr], GI[lo:lo + 64, pr, 1:L + 1], start=False, stop=True)
                full(mm)
            for kc in range(KC):
                ring.wait_emptied(pe, "y", kc)
                o = slot("yT", kc)
                transposes(("yT", kc), [(o[:, l // 4, (l % 4) * SC:(l % 4 + 1) * SC],
                                         YK[0:SC, l, kc * P:(kc + 1) * P]) for l in range(L)])
            for kc in range(KC):
                ring.wait_emptied(pe, "yT", kc)
            for ch in range(2):
                for i in range(5):
                    ring.wait_free(pe, "gl", ch, i)
                    o = slot("gl", ch, i)
                    n = ROWS[i]
                    for kc in range(KC):
                        if i == 0 and kc % 4 == 0:
                            pe.wait_ge(sem(f"w_glu_in_{2 if ch else kc // 4}"), 16)
                        for b in range(2):
                            mm = pe.matmul(o[0:n, b, :], YT[:, kc, i * P:i * P + n],
                                           WGL[ch][:, kc, b * 512:(b + 1) * 512], start=kc == 0, stop=kc == KC - 1)
                    full(mm)
            router(1)
            experts(1)

        def norm_squares(act, n, X_ready):
            junk = place(A + {0: 5120, 1: 31040, 3: 31040}.get(n, 0), D)
            for i in range(5):
                X_ready(i)
                ins = nc.scalar.activation(junk, X[:, i, :], ACT.Square, accum_out=ss[:, i:i + 1])
                ins.then_inc(sem("squares"), 1)
                act.wait_ge(sem("squares"), 5 * n + i + 1)
            act.wait_ge(sem("var_ready"), n + 1)
            nc.scalar.activation(root, var, ACT.Sqrt).then_inc(sem("root_ready"), 1)

        def norm_scale(dve, step, n, out):
            v = nc.vector
            dve.wait_ge(sem("squares"), 5 * n + 5)
            v.tensor_scalar(var, ss, 1.0 / D, EPS, ALU.mult, ALU.add).then_inc(sem("var_ready"), 1)
            dve.wait_ge(sem("root_ready"), n + 1)
            step(v.reciprocal(rstd, root))
            dve.wait_ge(sem("norm_in"), 16 * n + 16)
            for i in range(5):
                v.scalar_tensor_tensor(out[:, i, :], X[:, i, :], rstd[:, i:i + 1], GB, ALU.mult, ALU.mult
                                       ).then_inc(sem(f"h_{n}"), 1)
                dve.wait_ge(sem(f"h_{n}"), i + 1)

        def recut(eng, step, copy, odd):
            def u_out(q):
                take(eng, "u", q)
                give(eng, copy(U[:, 8 * q:8 * q + 8].rearrange("p (b j) n -> p b (j n)", b=2),
                               slot("u", q)[:, :, 0:4 * UC]), "u", q)
            for q in range(odd, 8, 2):
                if q >= 2:
                    ring.wait_full(eng, "u", q - 2)
                copy(XR[odd].rearrange("p (g l c) -> p l g c", g=8, l=L),
                     XK[:, :, q * P:(q + 1) * P].rearrange("p l (g c) -> p l g c", c=CW)
                     ).then_inc(sem(f"xr_ready_{odd}"), 1)
                if q >= 2:
                    u_out(q - 2)
            u_out(6 + odd)

        def cmul(tt, outr, outi, ar_, ai_, br_, bi_, x1, x2, sign=1):
            tt(x1, ai_, bi_, ALU.mult)
            tt(outr, ar_, br_, ALU.mult)
            tt(outr, outr, x1, ALU.subtract if sign > 0 else ALU.add)
            tt(x2, ar_, bi_, ALU.mult)
            tt(outi, ai_, br_, ALU.mult)
            tt(outi, outi, x2, ALU.add if sign > 0 else ALU.subtract)

        ls, lr, li_, a_, th, mag8, shalf, cs, lbr, lbi = sp_[:10]
        aa, den_, qr_, qi_, t1, t2, ur, ui, nn = sp_[10:19]

        def store_normed(act, n, src, done):
            for i in range(5):
                act.wait_ge(sem(f"h_{n}"), i + 1)
                act.dma_start(hd[i * P:i * P + ROWS[i], :], tile_rows(src, i)).then_inc(sem(done), 16)

        @block.scalar
        def _(act):
            a = nc.scalar
            chain = [0]

            def step(ins):
                chain[0] += 1
                ins.then_inc(sem("act_steps"), 1)
                act.wait_ge(sem("act_steps"), chain[0])

            act.sem_inc(sem("m_copied"), 1)
            for l in range(2):
                for s in range(2):
                    act.sem_inc(sem(f"y_out_{l}_{s}"), 16)

            def x_in(i):
                if i == TILES:
                    act.wait_ge(sem("x_cleared"), 1)
                act.wait_ge(sem(f"x_in_{i}"), 16)

            norm_squares(act, 0, x_in)
            for i in (1, 3):
                take(act, "ht", i)
                give(act, a.copy(HT[:, :, i * P:(i + 1) * P], slot("ht", i).rearrange("p b (k n) -> p (b k) n", n=P)),
                     "ht", i)
            act.wait_ge(sem("f_in"), 1)
            step(a.activation(er, lf, ACT.Abs))
            step(a.activation(er, er, ACT.Exp, scale=-1.0))
            a.activation(tr_, er, ACT.Ln, bias=1.0).then_inc(sem("softplus"), 1)

            def z_out(n, dst, func=ACT.Copy, scale=1.0):
                take(act, "z", n)
                give(act, a.activation(dst.rearrange("p (b n) -> p b n", b=2), slot("z", n)[:, :, 0:HALF], func,
                                       scale=scale), "z", n)

            for n in range(4):
                z_out(n, Zk[:, n], scale=KSCALE)
            act.wait_ge(sem("exps_in"), 1)
            step(a.activation(wi[:, 0:SEQ], wi[:, 0:SEQ], ACT.Exp))
            a.activation(er[:, 0:SEQ], er[:, 0:SEQ], ACT.Exp).then_inc(sem("exps_out"), 1)
            for n in range(4):
                z_out(4 + n, Zq[:, n])
            for n in range(4):
                z_out(8 + n, Zv[:, n])
            act.wait_ge(sem("sm_in"), 1)
            a.activation(SM, SM, ACT.Exp).then_inc(sem("sm_out"), 1)
            for h in range(H):
                act.wait_ge(sem("w_in_exp"), h + 1)
                for c in range(TILES):
                    ins = a.activation(W[:, h, c], W[:, h, c], ACT.Exp, bias=gcol[:, H * c + h:H * c + h + 1])
                ins.then_inc(sem("w_exp"), 1)
                act.wait_ge(sem("w_exp"), h + 1)
            for n in range(4):
                take(act, "z", 12 + n)
                src = slot("z", 12 + n)
                if n == 0:
                    act.wait_ge(sem("ue_cleared"), 1)
                step(a.copy(UE[:, n, CW:CW + HALF], src[:, 0, 0:HALF]))
                step(a.copy(UE[:, n, CW + HALF:CW + SEQ], src[:, 1, 0:SEQ - HALF]))
                give(act, a.copy(us[:, n], src[:, 1, SEQ - HALF:HALF]), "z", 12 + n)
            for n in range(4):
                z_out(16 + n, Zo[:, n], ACT.Sigmoid)
            for g in range(4):
                take(act, "pw", g)
                give(act, a.activation(MIX[:, g].rearrange("p (b n) -> p b n", b=2), slot("pw", g)[:, :, 0:HALF],
                                       ACT.Copy, scale=pscale[:, g:g + 1]), "pw", g)
            act.wait_ge(sem("s5_in"), 96)
            step(a.activation(sp_[0], sp_[0], ACT.Exp))
            act.sem_inc(sem("s5_dt"), 1)
            act.wait_ge(sem("s5_ath"), 1)
            step(a.activation(sp_[5], sp_[3], ACT.Exp, scale=float(L)))
            step(a.activation(sp_[3], sp_[3], ACT.Exp))
            step(a.activation(sp_[6], sp_[4], ACT.Sin, scale=0.5))
            step(a.activation(sp_[4], sp_[4], ACT.Sin))
            act.sem_inc(sem("s5_sin"), 1)
            act.wait_ge(sem("mix_samples"), 1)

            def router(l):
                n = 2 * l + 1
                norm_squares(act, n, lambda i: act.wait_ge(sem("x_tile"), 10 * l + i + 1))
                store_normed(act, n, HB, f"h_out_{l}")
                for i in range(5):
                    take(act, "tr", l, i)
                    m = ROWS[i]
                    give(act, a.copy(HTB[i % 2][:, :, 0:m],
                                     slot("tr", l, i).rearrange("p b (k n) -> p (b k) n", n=P)[:, :, 0:m]),
                         "tr", l, i)
                act.wait_ge(sem("dg_ready"), l + 1)
                a.activation(gexp, gexp, ACT.Exp).then_inc(sem("gexp_ready"), 1)
                act.wait_ge(sem("d12_ready"), l + 1)
                a.activation(dexp, dexp, ACT.Exp).then_inc(sem("dexp_ready"), 1)

            def experts(l):
                def turns(r):
                    if not isinstance(r, int):
                        for i in range(5):
                            act.wait_ge(sem(f"yg_in_{l}_{i}"), 32 * r)
                    act.sem_inc(sem("round_marks"), 1)
                    with act.Fori(0, E // 2) as k:
                        t = k + 16 * r
                        for s in range(2):
                            act.wait_ge(sem(f"xt_done_{l}"), 2 * t + s + 3)
                            a.copy(XT[s], ps[:, s, :].rearrange("p (b n) -> p b n", b=4)
                                   ).then_inc(sem(f"xt_ready_{l}"), 1)
                        for s in range(2):
                            act.wait_ge(sem(f"gu_done_{l}"), 2 * t + s + 3)
                            act.wait_ge(sem(f"act_ready_{l}"), 2 * t + 2)
                            a.activation(SIL[s], ps[:, 2 + s, 0:P], ACT.Silu).then_inc(sem(f"silu_{l}"), 1)
                        for s in range(2):
                            act.wait_ge(sem(f"y_ready_{l}"), 2 * t + s + 3)
                            e = 2 * k + s
                            act.dma_start(yd[bass.ds(e, 1)].rearrange("e t (h c) -> h (e t) c", h=2), YE[s]
                                          ).then_inc(sem(f"y_out_{l}_{s}"), 16)
                        if l == 0:
                            act.wait_ge(sem("m_turned"), t + 2)
                            a.copy(M[:, bass.ds(2 * k, 2)].rearrange("p j r n -> p j (r n)"), ps[:, 4:6, P:3 * P]
                                   ).then_inc(sem("m_copied"), 1)
                    for s in range(2):
                        act.wait_ge(sem(f"y_out_{l}_{s}"), 256 * r + 272)
                    act.sem_inc(sem(f"y_all_out_{l}"), 1)
                turns(0)
                n = act.value_load(most[0:1, l:l + 1], min_val=0, max_val=NT)
                with act.Fori(1, ROUNDS) as r:
                    with act.If(n > r * CAP):
                        turns(r)

            router(0)
            experts(0)
            norm_squares(act, 2, lambda i: act.wait_ge(sem("x_tile"), 5 + i + 1))
            act.wait_ge(sem("xk_in"), 96)
            ring.wait_full(act, "k")
            recut(act, step, a.copy, 1)
            def y_out(q):
                take(act, "y", q)
                step(a.copy(*y_views(q, 0)))
                give(act, a.copy(*y_views(q, 1)), "y", q)
            for q in range(1, 8, 2):
                y_out(q)
            for kc in range(KC):
                take(act, "yT", kc)
                src = slot("yT", kc)
                if kc == 0:
                    ring.wait_full(act, "y", 7)
                step(a.activation(YT[:, kc, 0:SEQ].rearrange("p (k b l) -> p b l k", b=2, l=4),
                                  src[:, :, 0:4 * SC].rearrange("p b (l k) -> p b l k", l=4)[:, :, :, 0:NCH],
                                  ACT.Gelu_apprx_tanh))
                give(act, a.activation(YT[:, kc, SEQ:NT], src[:, 0, NCH:SC], ACT.Gelu_apprx_tanh), "yT", kc)
            for ch in range(2):
                for i in range(5):
                    take(act, "gl", ch, i)
                    q = 5 * ch + i
                    if q >= 2:
                        act.wait_ge(sem("sig_used"), q - 1)
                    a.activation(SIG[q % 2][0:ROWS[i]], slot("gl", ch, i)[0:ROWS[i], 1, :], ACT.Sigmoid
                                 ).then_inc(sem("sig_ready"), 1)
            router(1)
            experts(1)
            norm_squares(act, 4, lambda i: act.wait_ge(sem("x_tile"), 15 + i + 1))

        @block.vector
        def _(dve):
            v = nc.vector
            chain = [0]

            def step(ins):
                chain[0] += 1
                ins.then_inc(sem("dve_steps"), 1)
                dve.wait_ge(sem("dve_steps"), chain[0])

            def tt(out, a, b, op):
                step(v.tensor_tensor(out, a, b, op))

            def ts(out, a, s1, s2, op0, op1=ALU.bypass):
                step(v.tensor_scalar(out, a, s1, s2, op0, op1))

            def stt(out, a, s, b, op0, op1):
                step(v.scalar_tensor_tensor(out, a, s, b, op0, op1))

            for l in range(2):
                for name in ("act_ready", "y_ready"):
                    dve.sem_inc(sem(f"{name}_{l}"), 2)
            v.memset(X[:, TILES, :], 0.0).then_inc(sem("x_cleared"), 1)
            norm_scale(dve, step, 0, HH)
            for i in (0, 2, 4):
                take(dve, "ht", i)
                n = ROWS[i]
                give(dve, v.tensor_copy(HT[:, :, i * P:i * P + n],
                                        slot("ht", i).rearrange("p b (k n) -> p (b k) n", n=P)[:, :, 0:n]), "ht", i)
            take(dve, "gates")
            dve.wait_ge(sem("small_in"), 16 * 7)
            g = slot("gates")
            ts(li.rearrange("p (b n) -> p b n", b=2), g[0:H, :, 0:HALF], bg[:, 0:1], None, ALU.add)
            give(dve, v.tensor_copy(lf.rearrange("p (b n) -> p b n", b=2), g[32:32 + H, :, 0:HALF]), "gates")
            ts(lf, lf, bg[:, 1:2], None, ALU.add)
            dve.sem_inc(sem("f_in"), 1)
            dve.wait_ge(sem("softplus"), 1)
            stt(lf, lf, 0.0, tr_, ALU.min, ALU.subtract)
            dve.wait_ge(sem("consts"), 16)
            step(v.tensor_tensor_scan(bc_[:, 0:SEQ], const("keep", H), lf[:, 0:SEQ], 0.0, ALU.mult, ALU.add))
            tt(ar[:, 0:SEQ], li[:, 0:SEQ], bc_[:, 0:SEQ], ALU.subtract)
            step(v.memset(mrun, 0.0))
            for c in range(TILES):
                cc = slice(c * P, (c + 1) * P)
                e = (c + 1) * P - 1
                step(v.tensor_tensor_scan(mr[:, cc], ar[:, cc], ar[:, cc], mrun[:, c:c + 1], ALU.max, ALU.max))
                tt(mrun[:, c + 1:c + 2], bc_[:, e:e + 1], mr[:, e:e + 1], ALU.add)
                ts(wi[:, cc], mr[:, cc], -1.0, mrun[:, c:c + 1], ALU.mult, ALU.add)
            stt(er[:, 0:SEQ], bc_[:, 0:SEQ], -1.0, mr[:, 0:SEQ], ALU.mult, ALU.subtract)
            ts(mr[:, 0:SEQ], mr[:, 0:SEQ], -1.0, None, ALU.mult)
            dve.sem_inc(sem("exps_in"), 1)
            dve.wait_ge(sem("exps_out"), 1)
            dve.sem_inc(sem("gate_rows"), 1)
            step(v.memset(UE[:, :, 0:CW], 0.0))
            dve.sem_inc(sem("ue_cleared"), 1)
            take(dve, "cols")
            step(v.tensor_copy(gcol, slot_flat("cols")[:, 0:16]))
            give(dve, v.tensor_copy(ecol, slot_flat("cols")[:, 16:32]), "cols")
            take(dve, "sg")
            give(dve, v.tensor_copy(SG, slot_flat("sg")[0:NS, 0:8]), "sg")
            dve.wait_ge(sem("n0_in"), 16)
            tt(SM[:, 4:8], SG[:, 0:4], SG[:, 4:8], ALU.subtract)
            tt(SM[:, 8:12], SM[:, 4:8], m0s, ALU.max)
            tt(SM[:, 0:4], m0s, SM[:, 8:12], ALU.subtract)
            tt(SM[:, 4:8], SM[:, 4:8], SM[:, 8:12], ALU.subtract)
            tt(sden[:, 0:4], SM[:, 8:12], SG[:, 4:8], ALU.add)
            ts(SM[:, 8:12], sden[:, 0:4], -1.0, None, ALU.mult)
            dve.sem_inc(sem("sm_in"), 1)
            for h in range(H):
                take(dve, "bc", h)
                b = slot("bc", h)
                tt(W[:, h], b[:, 0, :].rearrange("p (c n) -> p c n", c=TILES), spread_mid(causal, TILES), ALU.add)
                dve.sem_inc(sem("w_in_exp"), 1)
                if h == 0:
                    ring.wait_emptied(dve, "z", 7)
                tt(QT[:, h], Zq[:, h, 0:SEQ], b[:, 1, :], ALU.mult)
                give(dve, v.tensor_copy(dec.rearrange("p (c h) -> p c h", h=H)[:, :, h],
                                        b[:, 1, :].rearrange("p (c n) -> p c n", c=TILES)[:, :, P - 1]), "bc", h)
            dve.sem_inc(sem("rows_dead"), 1)
            take(dve, "st")
            step(v.tensor_copy(ks, slot("st")[0:NS, 0, :].rearrange("p (h k) -> p h k", h=H)))
            dve.wait_ge(sem("w_exp"), H)
            sq = KB[0:NS, 0:H]
            give(dve, v.tensor_copy(sq, slot("st")[0:NS, 1, :].rearrange("p (h k) -> p h k", h=H)), "st")
            dve.wait_ge(sem("sm_out"), 1)
            tt(ks, ks, spread(SM[:, 4:8], P), ALU.mult)
            tt(n0s, n0s, spread(SM[:, 0:4], P), ALU.mult)
            tt(n0s, n0s, ks, ALU.add)
            ring.wait_emptied(dve, "z", 11)
            step(v.tensor_copy(vs, Zv[:, :, SEQ:NT]))
            step(v.memset(V1[:, :, :, P:P + 1], 1.0))
            for c in range(TILES):
                take(dve, "kt", c)
                kt = slot("kt", c)
                for h in range(H):
                    ts(KT[:, c, h], kt[:, 0, h * P:(h + 1) * P], W[:, h, c, P - 1:P], None, ALU.mult)
                give(dve, v.tensor_copy(V1[:, c, :, 0:P], kt[:, 1, :].rearrange("p (h k) -> p h k", h=H)), "kt", c)
                take(dve, "s", c)
                give(dve, v.tensor_tensor(W[:, :, c, :], slot("s", c)[:, 0, :].rearrange("p (h k) -> p h k", h=H),
                                          W[:, :, c, :], ALU.mult), "s", c)
                take(dve, "kv", c)
                kv = slot("kv", c)
                for h in range(H):
                    src = kv[:, h // 2, (h % 2) * 129:(h % 2) * 129 + 129]
                    if c == 0:
                        if h == 0:
                            dve.wait_ge(sem("kz_out"), 16)
                        ins = v.tensor_copy(CN[:, 0, h], src)
                    else:
                        ins = v.scalar_tensor_tensor(CN[:, c, h], CN[:, c - 1, h], dec[:, H * c + h:H * c + h + 1],
                                                     src, ALU.mult, ALU.add)
                    if h < H - 1:
                        step(ins)
                give(dve, ins, "kv", c)
            dve.sem_inc(sem("cn_ready"), 1)
            prod = KB[0:NS, H:2 * H]
            tt(prod, n0s, sq, ALU.mult)
            step(v.tensor_reduce(sden[:, 4:8], prod, AX, ALU.add))
            stt(sden[:, 8:12], sden[:, 4:8], -1.0, sden[:, 4:8], ALU.mult, ALU.max)
            tt(sden[:, 8:12], sden[:, 8:12], SM[:, 8:12], ALU.max)
            step(v.reciprocal(sden[:, 4:8], sden[:, 8:12]))
            tt(qs, sq, spread(sden[:, 4:8], P), ALU.mult)
            dve.sem_inc(sem("ks_ready"), 1)
            ring.wait_emptied(dve, "z", 15)
            dve.sem_inc(sem("us_ready"), 1)
            dve.sem_inc(sem("u_in"), 1)
            take(dve, "ws")
            for g_ in range(4):
                w = 2.0 ** -(g_ + 1)
                tt(sos[:, g_], slot_flat("ws")[:, g_ * NS:(g_ + 1) * NS], us[:, g_], ALU.add)
                ins = v.scalar_tensor_tensor(DT[:, g_, SEQ:NT], sos[:, g_], w, us[:, g_], ALU.mult, ALU.subtract)
                if g_ < 3:
                    step(ins)
            give(dve, ins, "ws")
            dve.sem_inc(sem("ws_done"), 1)
            ring.wait_emptied(dve, "z", 19)
            for c in range(TILES):
                take(dve, "num", c)
                nm = slot("num", c)
                step(v.tensor_copy(den.rearrange("p (a b) -> p a b", a=2),
                                   nm[:, :, 0:258].rearrange("p a (b n) -> p a b n", b=2)[:, :, :, P]))
                stt(dab, den, -1.0, den, ALU.mult, ALU.max)
                tt(dab, dab, ecol[:, H * c:H * c + H], ALU.max)
                step(v.reciprocal(rden, dab))
                for h in range(H):
                    ins = v.tensor_scalar(HM[:, c % 2, h], nm[:, h // 2, (h % 2) * 129:(h % 2) * 129 + P],
                                          rden[:, h:h + 1], None, ALU.mult)
                    if h < H - 1:
                        step(ins)
                give(dve, ins, "num", c)
                take(dve, "hT", c)
                give(dve, v.tensor_tensor(MIX[:, H:2 * H, c * P:(c + 1) * P],
                                          slot("hT", c)[:, 0, :].rearrange("p (h n) -> p h n", h=H),
                                          Zo[:, :, c * P:(c + 1) * P], ALU.mult), "hT", c)
            dve.wait_ge(sem("s5_in"), 96)
            lr2, li2 = GTMP[:, 0, 0:2].rearrange("p l c -> p (l c)"), GTMP[:, 0, 2:4].rearrange("p l c -> p (l c)")
            tt(lr2, lr, lr, ALU.mult)
            tt(li2, li_, li_, ALU.mult)
            tt(lr2, lr2, li2, ALU.add)
            step(v.reciprocal(den_, lr2))
            dve.sem_inc(sem("s5_den"), 1)
            dve.wait_ge(sem("kb_in"), 32)
            dve.wait_ge(sem("c0_in"), 16)
            tt(CS, CS, spread(DB, P), ALU.mult)
            kb4 = KB.rearrange("p (n h) k -> p n h k", h=H)
            tt(kb4, kb4, spread(vs.rearrange("p h n -> p n h"), P), ALU.mult)
            tt(CS, CS, KB, ALU.add)
            dve.sem_inc(sem("kb_used"), 1)
            dve.sem_inc(sem("cs_ready"), 1)
            dve.wait_ge(sem("qb_in"), 16)
            tt(KB, KB, CS, ALU.mult)
            step(v.tensor_reduce(rs, KB, AX, ALU.add))
            tt(MIX[:, H:2 * H, SEQ:NT], rs.rearrange("p (n h) -> p h n", h=H), Zo[:, :, SEQ:NT], ALU.mult)
            dve.sem_inc(sem("mix_samples"), 1)
            for i in range(5):
                take(dve, "wo", i)
                n = ROWS[i]
                give(dve, v.tensor_tensor(X[0:n, i, :], X[0:n, i, :], slot_flat("wo", i)[0:n], ALU.add), "wo", i)
                dve.sem_inc(sem("x_tile"), 1)
            dve.wait_ge(sem("stored"), 16 * 8)
            dve.wait_ge(sem("s5_ready"), 1)
            dve.sem_inc(sem("x_mixed"), 1)

            def router(l):
                step(v.memset(LG, 0.0))
                norm_scale(dve, step, 2 * l + 1, HB)
                for i in range(5):
                    take(dve, "lg", l, i)
                    n = ROWS[i]
                    give(dve, v.tensor_tensor(LG[0:n, i], slot_flat("lg", l, i)[0:n, 0:36], BR[l][0:n], ALU.add),
                         "lg", l, i)
                gl, el = LG[:, :, 0:4], LG[:, :, 4:36]

                def first_of(values, top, rev, out):
                    n = values.shape[-1]
                    step(v.tensor_reduce(top, values, AX, ALU.max))
                    tt(out, values, spread(top, n), ALU.is_equal)
                    tt(out, out, spread_mid(rev, 5), ALU.mult)
                    step(v.tensor_reduce(etop, out, AX, ALU.max))
                    tt(out, out, spread(etop, n), ALU.is_equal)

                first_of(gl, gmax, const("revg"), og)
                tt(gexp, gl, spread(gmax, 4), ALU.subtract)
                dve.sem_inc(sem("dg_ready"), 1)
                ts(gneg, og, BIG, -BIG, ALU.mult, ALU.add)
                tt(me.rearrange("p t (g k) -> p t g k", g=4), el.rearrange("p t (g k) -> p t g k", g=4),
                   spread(gneg, 8), ALU.add)
                first_of(me, m1, const("reve"), oh[0])
                stt(me, oh[0], -2 * BIG, me, ALU.mult, ALU.add)
                first_of(me, m2, const("reve"), oh[1])
                tt(dexp, m2, m1, ALU.subtract)
                dve.sem_inc(sem("d12_ready"), 1)
                for j in range(2):
                    tt(oh[j], oh[j], spread(const("valid"), E), ALU.mult)
                tt(OH, oh[0], oh[1], ALU.add)
                step(v.memset(PRE[:, 0], 0.0))
                for i in range(1, 5):
                    tt(PRE[:, i], PRE[:, i - 1], OH[:, i - 1], ALU.add)
                tt(both, PRE[:, 4], OH[:, 4], ALU.add)
                dve.sem_inc(sem("chosen"), 1)
                dve.wait_ge(sem("gexp_ready"), l + 1)
                step(v.tensor_reduce(gsum, gexp, AX, ALU.add))
                step(v.reciprocal(gw, gsum))
                dve.wait_ge(sem("dexp_ready"), l + 1)
                ts(dsum, dexp, 1.0, None, ALU.add)
                step(v.reciprocal(dsum, dsum))
                tt(pw_[0], dsum, gw, ALU.mult)
                tt(pw_[1], pw_[0], dexp, ALU.mult)
                take(dve, "pos", l)
                o = slot("pos", l)
                step(v.tensor_copy(POS, o[:, 0, 0:5 * E].rearrange("p (t e) -> p t e", t=5)))
                step(v.tensor_reduce(cntmax, o[:, 1, 0:E], AX, ALU.max))
                give(dve, v.tensor_copy(most[:, l:l + 1], cntmax), "pos", l)
                dve.sem_inc(sem("most_ready"), 1)
                for j in range(2):
                    tt(hit, oh[j], POS, ALU.mult)
                    step(v.tensor_reduce(RK[:, j], hit, AX, ALU.add))
                    tt(hit, oh[j], spread_mid(const("eio"), 5), ALU.mult)
                    step(v.tensor_reduce(EID[:, j], hit, AX, ALU.add))
                    tt(oh[j], oh[j], spread(const("tokid"), E), ALU.mult)
                ts(EID, EID, float(CAP), None, ALU.mult)
                for s in range(2):
                    step(v.memset(XG[s], 0.0))
                dve.sem_inc(sem("xg_cleared"), 1)

            def experts(l):
                def turns(r):
                    n = 19

                    def lstep(ins, k):
                        ins.then_inc(sem(f"list_steps_{l}"), 1)
                        dve.wait_ge(sem(f"list_steps_{l}"), n * r + k)

                    for q in range(10):
                        v.tensor_scalar(OHR[:, q], const("iota"), RK.rearrange("p j t -> p (j t)")[:, q:q + 1], None,
                                        ALU.is_equal).then_inc(sem(f"list_steps_{l}"), 1)
                    dve.wait_ge(sem(f"list_steps_{l}"), n * r + 10)
                    dve.sem_inc(sem(f"spots_{l}"), 1)
                    lstep(v.tensor_scalar(QR, RK, 0.0, None, ALU.is_ge), 11)
                    lstep(v.scalar_tensor_tensor(QR, RK, float(CAP), QR, ALU.is_lt, ALU.mult), 12)
                    lstep(v.tensor_scalar(QR, QR, -1e5, 1e5, ALU.mult, ALU.add), 13)
                    lstep(v.tensor_tensor(QR, QR, EID, ALU.add), 14)
                    lstep(v.tensor_tensor(idx_back[:, :], QR.rearrange("p j t -> p (j t)"),
                                          RK.rearrange("p j t -> p (j t)"), ALU.add), 15)
                    lstep(v.tensor_scalar(RK, RK, -float(CAP), None, ALU.add), 16)
                    dve.wait_ge(sem(f"list_done_{l}"), r + 1)
                    lstep(v.tensor_scalar(both, ps[:, 0, 0:E], 0.0, 4096.0, ALU.is_equal, ALU.mult), 17)
                    lstep(v.scalar_tensor_tensor(both, ps[:, 0, 0:E], 2.0, both, ALU.mult, ALU.add), 18)
                    lstep(v.tensor_scalar(idx_list[:, :], both, const("half"), None, ALU.add), 19)
                    dve.sem_inc(sem(f"list_read_{l}"), 1)
                    with dve.Fori(0, E // 2) as k:
                        t = k + 16 * r
                        for s in range(2):
                            dve.wait_ge(sem(f"silu_{l}"), 2 * t + s + 1)
                            v.tensor_tensor(ACTB[s], SIL[s], ps[:, 2 + s, P:2 * P], ALU.mult
                                            ).then_inc(sem(f"act_ready_{l}"), 1)
                        for s in range(2):
                            dve.wait_ge(sem(f"at_done_{l}"), 2 * t + s + 1)
                            v.tensor_copy(AT[s], ps[:, 4 + s, 0:P]).then_inc(sem(f"at_ready_{l}"), 1)
                        for s in range(2):
                            dve.wait_ge(sem(f"down_done_{l}"), 2 * t + s + 3)
                            dve.wait_ge(sem(f"y_out_{l}_{s}"), 16 * t + 16)
                            v.tensor_copy(YE[s], ps[:, 6 + s, :]).then_inc(sem(f"y_ready_{l}"), 1)
                    for q in range(10):
                        i, j, m = q // 2, q % 2, ROWS[q // 2]
                        dve.wait_ge(sem(f"yg_in_{l}_{i}"), 32 * r + 32)
                        v.scalar_tensor_tensor(X[0:m, i, :], YG[0:m, 2 * (i % 2) + j], pw_[j][0:m, i:i + 1], X[0:m, i, :],
                                               ALU.mult, ALU.add).then_inc(sem(f"combined_{l}"), 1)
                        dve.wait_ge(sem(f"combined_{l}"), 10 * r + q + 1)
                    dve.sem_inc(sem("round_marks"), 1)
                turns(0)
                n = dve.value_load(most[0:1, l:l + 1], min_val=0, max_val=NT)
                with dve.Fori(1, ROUNDS) as r:
                    with dve.If(n > r * CAP):
                        turns(r)
                for i in range(5):
                    dve.sem_inc(sem("x_tile"), 1)
                dve.sem_inc(sem("x_moe"), 1)

            router(0)
            experts(0)

            step(v.memset(XK[:, 0:L // 2], 0.0))
            dve.sem_inc(sem("xk_cleared"), 1)
            norm_scale(dve, step, 2, H2)
            take(dve, "k")
            give(dve, v.tensor_copy(KS.rearrange("p a b -> p (a b)"), slot_flat("k")), "k")
            tt(SKIP, spread_mid(const("diag"), KC), spread(DSK, CW), ALU.mult)
            tt(KS[:, :, 0:CW], KS[:, :, 0:CW], SKIP, ALU.add)
            dve.sem_inc(sem("taps_ready"), 1)
            dve.wait_ge(sem("xk_in"), 96)
            recut(dve, step, v.tensor_copy, 0)
            ring.wait_full(dve, "u", 7)
            dve.wait_ge(sem("phases_ready"), 1)
            for q in range(8):
                take(dve, "zs", q)
                z = slot("zs", q)[:, :, 0:4 * SC].rearrange("p r (j n) -> p r j n", j=4)
                zr, zi = z[:, 0, :, NS:SC], z[:, 1, :, NS:SC]
                rr, ri, tc, ts_ = (b[:, 4 * q:4 * q + 4] for b in (RR, RI, TC, TS))
                tm = TMQ
                tt(rr, zr, tc, ALU.mult)
                tt(tm, zi, ts_, ALU.mult)
                tt(rr, rr, tm, ALU.add)
                tt(ri, zi, tc, ALU.mult)
                tt(tm, zr, ts_, ALU.mult)
                tt(ri, ri, tm, ALU.subtract)
                sr, si = SHR[:, 4 * q:4 * q + 4], SHI[:, 4 * q:4 * q + 4]
                tt(sr, sr, z[:, 0, :, 0:NS], ALU.add)
                give(dve, v.tensor_tensor(si, si, z[:, 1, :, 0:NS], ALU.add), "zs", q)
            for b in (RR, RI):
                f = b.rearrange("p r k -> p (r k)")
                step(v.tensor_tensor_scan(f, R8.rearrange("p r k -> p (r k)"), f, 0.0, ALU.mult, ALU.add))
            n = NCH - 1
            for o, x, y, op in ((HR, RR, RI, ALU.subtract), (HI, RI, RR, ALU.add)):
                step(v.memset(o[:, :, 0:1], 0.0))
                tt(o[:, :, 1:NCH], x[:, :, 0:n], TC[:, :, 0:n], ALU.mult)
                tt(TMP[:, :, 0:n], y[:, :, 0:n], TS[:, :, 0:n], ALU.mult)
                tt(o[:, :, 1:NCH], o[:, :, 1:NCH], TMP[:, :, 0:n], op)
            step(v.tensor_copy(HR[:, :, NCH:SC], H0R.rearrange("p (r n) -> p r n", n=NS)))
            step(v.tensor_copy(HI[:, :, NCH:SC], H0I.rearrange("p (r n) -> p r n", n=NS)))
            for q, (x, y, op) in enumerate(((RR, RI, ALU.subtract), (RI, RR, ALU.add))):
                last = TMQ[:, 0, 0:PAIRS]
                tt(HEND[:, q], x[:, :, n], TC[:, :, n], ALU.mult)
                tt(last, y[:, :, n], TS[:, :, n], ALU.mult)
                tt(HEND[:, q], HEND[:, q], last, op)
            dve.sem_inc(sem("states_in"), 1)
            dve.sem_inc(sem("s5_end"), 1)
            for q in range(0, 8, 2):
                take(dve, "y", q)
                step(v.tensor_copy(*y_views(q, 0)))
                give(dve, v.tensor_copy(*y_views(q, 1)), "y", q)
            for ch in range(2):
                for i in range(5):
                    q = 5 * ch + i
                    n = ROWS[i]
                    take(dve, "gl", ch, i)
                    dve.wait_ge(sem("sig_ready"), q + 1)
                    ins = v.tensor_tensor(GT[q % 2][0:n], slot("gl", ch, i)[0:n, 0, :], SIG[q % 2][0:n], ALU.mult)
                    give(dve, ins, "gl", ch, i)
                    dve.sem_inc(sem("sig_used"), 1)
                    xs = X[0:n, i, 512 * ch:512 * ch + 512]
                    tt(xs, xs, GT[q % 2][0:n], ALU.add)
                    if ch:
                        dve.sem_inc(sem("x_tile"), 1)
            dve.wait_ge(sem("stored"), 16 * 11)
            dve.sem_inc(sem("x_mixed"), 1)
            router(1)
            experts(1)
            norm_scale(dve, step, 4, HC)

        @block.gpsimd
        def _(pool):
            g_ = nc.gpsimd
            chain = [0]

            def step(ins):
                chain[0] += 1
                ins.then_inc(sem("pool_steps"), 1)
                pool.wait_ge(sem("pool_steps"), chain[0])

            step(g_.memset(KZ, 0.0))
            pool.sem_inc(sem("kz_cleared"), 1)
            pool.wait_ge(sem("u_in"), 1)
            ring.wait_full(pool, "ws")
            ring.wait_emptied(pool, "kv", TILES - 1)
            for g in range(4):
                src = UE[:, g]
                for q in range(g + 1):
                    d = 2 ** q
                    dst = TU[q % 2]
                    step(g_.tensor_tensor(dst[:, 2 * d - 1:528], src[:, 2 * d - 1:528], src[:, d - 1:528 - d], ALU.add))
                    src = dst
                other = TU[(g + 1) % 2]
                step(g_.tensor_scalar(other[:, CW:528], src[:, CW:528], 2.0 ** -(g + 1), None, ALU.mult))
                ramp = const("ramp")[:, CW * g:CW * g + CW]
                step(g_.tensor_tensor(other[:, CW:2 * CW], src[:, CW:2 * CW], ramp, ALU.mult))
                step(g_.tensor_tensor(DT[:, g, 0:SEQ], other[:, CW:528], UE[:, g, CW:528], ALU.subtract))
                if g == 0:
                    pool.wait_ge(sem("ws_done"), 1)
                pool.sem_inc(sem("pool_mixed"), 1)

            def tt(out, a, b, op):
                step(g_.tensor_tensor(out, a, b, op))

            def ts(out, a, s1, s2, op0, op1=ALU.bypass):
                step(g_.tensor_scalar(out, a, s1, s2, op0, op1))

            pool.wait_ge(sem("s5_dt"), 1)
            tt(a_, lr, ls, ALU.mult)
            tt(th, li_, ls, ALU.mult)
            magic = 1.5 * 2.0 ** 23
            ts(nn, th, 1.0 / (2 * pi), magic, ALU.mult, ALU.add)
            ts(nn, nn, -magic, None, ALU.add)
            c1 = 6.28125
            c2 = float(np.float32(round((2 * pi - c1) * 2 ** 21) / 2 ** 21))
            for c in (c1, c2, 2 * pi - c1 - c2):
                ts(t1, nn, -c, None, ALU.mult)
                tt(th, th, t1, ALU.add)
            ts(th, th, 3.1415925, -3.1415925, ALU.min, ALU.max)
            pool.sem_inc(sem("s5_ath"), 1)
            pool.wait_ge(sem("s5_sin"), 1)
            tt(cs, shalf, shalf, ALU.mult)
            ts(cs, cs, -2.0, 1.0, ALU.mult, ALU.add)
            tt(lbr, a_, cs, ALU.mult)
            tt(lbi, a_, th, ALU.mult)
            ts(nn, lbr, -1.0, None, ALU.add)
            cmul(tt, qr_, qi_, nn, lbi, lr, li_, t1, t2, sign=-1)
            pool.wait_ge(sem("s5_den"), 1)
            tt(qr_, qr_, den_, ALU.mult)
            tt(qi_, qi_, den_, ALU.mult)
            cmul(tt, BBR, BBI, spread(qr_, CW), spread(qi_, CW), BIN[0], BIN[1], BTMP[0], BTMP[1])
            step(g_.tensor_copy(ur, cs))
            step(g_.tensor_copy(ui, th))
            for _ in range(3):
                cmul(tt, qr_, qi_, ur, ui, ur, ui, t1, t2)
                step(g_.tensor_copy(ur, qr_))
                step(g_.tensor_copy(ui, qi_))
            tt(t1, ur, ur, ALU.mult)
            tt(t2, ui, ui, ALU.mult)
            tt(t1, t1, t2, ALU.add)
            ts(t1, t1, -0.5, 1.5, ALU.mult, ALU.add)
            tt(cs, ur, t1, ALU.mult)
            tt(th, ui, t1, ALU.mult)
            step(g_.memset(PWR[:, :, 0], 1.0))
            step(g_.memset(PWI[:, :, 0], 0.0))
            for j in range(1, L + 1):
                cmul(tt, PWR[:, :, j], PWI[:, :, j], PWR[:, :, j - 1], PWI[:, :, j - 1], lbr, lbi, ls, lr)
            for j in range(L):
                step(g_.tensor_copy(BACKR[:, :, j], PWR[:, :, L - 1 - j]))
                step(g_.tensor_copy(BACKI[:, :, j], PWI[:, :, L - 1 - j]))
            pool.sem_inc(sem("s5_ready"), 1)

            def experts(l):
                pool.wait_ge(sem(f"h_out_{l}"), 80)
                pool.wait_ge(sem("xg_cleared"), l + 1)
                if l == 0:
                    pool.wait_ge(sem("s5_in"), 128)
                    step(g_.tensor_scalar(CIN[1], CIN[1], -1.0, None, ALU.mult))

                def matrices(k, t):
                    done = [0]

                    def mul_add(out, a, b, c, d, op, tmp):
                        for o, x, y, f in ((out, a, b, ALU.mult), (tmp, c, d, ALU.mult), (out, out, tmp, op)):
                            done[0] += 1
                            g_.tensor_tensor(o, x, y, f).then_inc(sem("matrix_steps"), 1)
                            pool.wait_ge(sem("matrix_steps"), 12 * t + done[0])
                            pool.sem_inc(sem("turn_marks"), 1)

                    two = bass.ds(2 * k, 2)

                    def by_step(a, n):
                        return a[:, two].unsqueeze(2).broadcast_to((P, 2, n, CW))

                    pr_, pi_ = spread(PWR[:, two], CW), spread(PWI[:, two], CW)
                    cr_, nci = by_step(CIN[0], L + 1), by_step(CIN[1], L + 1)
                    mul_add(GR[:, two], pr_, cr_, pi_, nci, ALU.add, GTMP)
                    mul_add(GI[:, two], pr_, nci, pi_, cr_, ALU.subtract, GTMP)
                    pr_, pi_ = spread(BACKR[:, two], CW), spread(BACKI[:, two], CW)
                    br_, bi_ = by_step(BBR, L), by_step(BBI, L)
                    pool.wait_ge(sem("m_turned"), t + 1)
                    pool.sem_inc(sem("turn_marks"), 1)
                    mul_add(VR, pr_, br_, pi_, bi_, ALU.subtract, GTMP[:, :, 0:L])
                    mul_add(VI, pr_, bi_, pi_, br_, ALU.add, GTMP[:, :, 0:L])
                    pool.sem_inc(sem("v_ready"), 1)

                def turns(r):
                    pool.wait_ge(sem(f"list_read_{l}"), r + 1)
                    pool.sem_inc(sem("round_marks"), 1)
                    with pool.Fori(0, E // 2) as k:
                        t = k + 16 * r
                        pool.wait_ge(sem(f"xt_done_{l}"), 2 * t + 2)
                        g_.tensor_copy(idx_now[:, :], idx_list[:, bass.ds(2 * k, 2)]).then_inc(sem(f"idx_{l}"), 1)
                        pool.wait_ge(sem(f"idx_{l}"), t + 1)
                        pool.sem_inc(sem("turn_marks"), 1)
                        for s in range(2):
                            g_.indirect_dma_start(out=XG[s], out_offset=None, in_=hd_halves,
                                                  in_offset=bass.IndirectOffsetOnAxis(ap=idx_now[:, s:s + 1], axis=0),
                                                  bounds_check=2 * NT - 1, oob_is_err=False
                                                  ).then_inc(sem(f"xg_in_{l}_{s}"), 16)
                        if l == 0:
                            matrices(k, t)
                    if l == 0:
                        pool.wait_ge(sem("m_turned"), 16 * r + 17)
                    pool.sem_inc(sem("turn_marks"), 1)
                    for i in range(5):
                        m, at = ROWS[i], 2 * (i % 2)
                        if i >= 2:
                            pool.wait_ge(sem(f"combined_{l}"), 10 * r + 2 * i - 2)
                            pool.sem_inc(sem("turn_marks"), 1)
                        g_.memset(YG[:, at:at + 2], 0.0).then_inc(sem(f"yg_cleared_{l}"), 1)
                        pool.wait_ge(sem(f"yg_cleared_{l}"), 5 * r + i + 1)
                        if i == 0:
                            pool.wait_ge(sem(f"y_all_out_{l}"), r + 1)
                        pool.sem_inc(sem("round_marks"), 1)
                        for j in range(2):
                            g_.indirect_dma_start(out=YG[0:m, at + j], out_offset=None, in_=yd_rows,
                                                  in_offset=bass.IndirectOffsetOnAxis(
                                                      ap=idx_back[0:m, 5 * j + i:5 * j + i + 1], axis=0),
                                                  bounds_check=E * CAP - 1, oob_is_err=False
                                                  ).then_inc(sem(f"yg_in_{l}_{i}"), 16)
                turns(0)
                n = pool.value_load(most[0:1, l:l + 1], min_val=0, max_val=NT)
                with pool.Fori(1, ROUNDS) as r:
                    with pool.If(n > r * CAP):
                        turns(r)

            experts(0)
            pool.wait_ge(sem("x_moe"), 1)
            step(g_.memset(XK[:, L // 2:L], 0.0))
            pool.sem_inc(sem("xk_cleared"), 1)
            for q in range(2):
                step(g_.memset(BD[q], 0.0))
                for g2 in range(2):
                    step(g_.tensor_copy(BD[q][64 * g2:64 * g2 + 64, :, CW * g2:CW * g2 + CW],
                                        (BBR, BBI)[q][64 * g2:64 * g2 + 64]))
            pool.sem_inc(sem("bd_ready"), 1)
            pr_, pi_, x1, x2 = sp_[0], sp_[1], sp_[2], sp_[3]
            step(g_.memset(TC[:, :, 0:1], 1.0))
            step(g_.memset(TS[:, :, 0:1], 0.0))
            m = 1
            while m < NCH:
                cmul(tt, TC[:, :, m:2 * m], TS[:, :, m:2 * m], TC[:, :, 0:m], TS[:, :, 0:m], spread(cs, m),
                     spread(th, m), TMP[:, :, 0:m], TMP[:, :, m:2 * m])
                cmul(tt, pr_, pi_, cs, th, cs, th, x1, x2)
                step(g_.tensor_copy(cs, pr_))
                step(g_.tensor_copy(th, pi_))
                m *= 2
            step(g_.tensor_copy(R8, spread(mag8, NCH)))
            step(g_.memset(R8[:, :, 0:1], 0.0))
            pool.wait_ge(sem("s5_in"), 160)
            for o, x, y, op in ((SHR, H0R, H0I, ALU.subtract), (SHI, H0I, H0R, ALU.add)):
                x, y = (z.rearrange("p (r n) -> p r n", n=NS) for z in (x, y))
                tt(o, x, spread(lbr, NS), ALU.mult)
                tt(SHT, y, spread(lbi, NS), ALU.mult)
                tt(o, o, SHT, op)
            pool.sem_inc(sem("phases_ready"), 1)
            experts(1)


_SHAPES = dict(hd=(NT, D), yd=(E, CAP, D), sdk=(NS, 512), sdq=(NS, 512), sdd=(NS, H), kp=(D, KROW))
_OUT = dict(y=(NT, D), pool_s=(NS, 14, 512), pool_p=(P, H, 15), pool_us=(P, H, NS), n_s=(NS, 512), m_s=(NS, H),
            c_s=(P, NS * H, P), cn_p=(P, H, 129), m_p=(H, 1), s5_p=(P, 2, PAIRS), s5_sr=(P, PAIRS, NS),
            s5_si=(P, PAIRS, NS))


def kernel(**inputs):
    import concourse.bacc as bacc
    from concourse.bass_utils import run_bass_kernel_spmd

    n = {k: np.asarray(a) for k, a in inputs.items()}

    def kmajor(w):
        return w.reshape(KC, P, -1).transpose(1, 0, 2)

    def rep(a):
        return np.broadcast_to(a, (P,) + a.shape)

    def groups(a):
        a = a.reshape((PAIRS, P) + a.shape[2:])
        return a.swapaxes(0, 1)

    w = n["w_in_ab"][0]
    cols = [w[:, 1024:1536], w[:, 512:1024], w[:, 1536:2048], w[:, 0:512], w[:, 2048:2560]]
    w_in = np.stack([kmajor(c[:, 256 * b:256 * b + 256]) for c in cols for b in range(2)])
    gate, up = n["moe_w_gate"], n["moe_w_up"]
    gu = np.concatenate([gate[..., 0:P], up[..., 0:P], gate[..., P:], up[..., P:]], axis=-1)
    gu = gu.reshape(2, E, KC, P, 512).transpose(0, 1, 3, 2, 4)
    down = n["moe_w_down"].reshape(2, E, 2, P, D).transpose(0, 1, 3, 2, 4)
    glu = n["w_glu"][0]
    arrays = dict(
        const=constants(), x_prompt=n["x_prompt"][0], x_sample=n["x_sample"][:, 0],
        norms=np.stack([rep(a) for a in (n["norm_mix"][0], n["norm_ffn"][0], n["norm_mix"][1], n["norm_ffn"][1],
                                         n["norm_final"])]),
        w_gate8=kmajor(w[:, 2560:2568]), b_gates=n["b_gates"][0].reshape(2, H).T, m0=n["state_mlstm_m"][0],
        pool_scale=n["pool_scale"][0].reshape(H, P).T,
        w_router=np.stack([kmajor(np.concatenate([n["moe_w_group"][l], n["moe_w_expert"][l]], -1)) for l in range(2)]),
        b_router=np.stack([rep(np.concatenate([n["moe_b_group"][l], n["moe_b_expert"][l]])) for l in range(2)]),
        pool_w=n["pool_w"][0].transpose(1, 0, 2), pool_rows=n["state_pool"][0].reshape(120, 512),
        pool_buf=n["state_pool"][0][:, 1:], n0=n["state_mlstm_n"][0].reshape(NS, 512), w_in=w_in,
        w_out=kmajor(n["w_out_ab"][0]), c0=n["state_mlstm_c"][0].reshape(NS * H, P, P).transpose(1, 0, 2),
        w_gu=gu, w_down=down,
        s5_cb=np.stack([groups(a) for a in (n["s5_c_re"][0].swapaxes(1, 2), n["s5_c_im"][0].swapaxes(1, 2),
                                            n["s5_b_re"][0], n["s5_b_im"][0])]),
        s5_ls=groups(np.broadcast_to(n["s5_log_step"][0][:, None], (GU, 64))),
        s5_lr=groups(n["s5_lam_re"][0]), s5_li=groups(n["s5_lam_im"][0]), s5_d=n["s5_d"][0].reshape(KC, P).T,
        s5_h0r=groups(n["state_s5_re"][0].transpose(1, 2, 0)).reshape(P, -1),
        s5_h0i=groups(n["state_s5_im"][0].transpose(1, 2, 0)).reshape(P, -1),
        w_glu=np.stack([kmajor(np.concatenate([glu[:, 512 * c:512 * c + 512], glu[:, D + 512 * c:D + 512 * c + 512]], -1))
                        for c in range(2)]),
    )
    nc = bacc.Bacc("TRN2", target_bir_lowering=False, num_devices=1)
    T, feed = {}, {}
    for k, a in arrays.items():
        feed[f"in_{k}"] = a = np.ascontiguousarray(a)
        T[k] = nc.dram_tensor(f"in_{k}", a.shape, mybir.dt.from_np(a.dtype), kind="ExternalInput").ap()
    for k, s in _OUT.items():
        T[k] = nc.dram_tensor(f"out_{k}", s, F32, kind="ExternalOutput").ap()
    for k, s in _SHAPES.items():
        T[k] = nc.dram_tensor(f"scratch_{k}", s, F32, kind="Internal").ap()
    bass_hybrid_step(nc, T)
    r = run_bass_kernel_spmd(nc, [feed], core_ids=[0]).results[0]
    o = {k: np.asarray(r[f"out_{k}"]) for k in _OUT}

    def ungroup(a):
        a = a.swapaxes(0, 1)
        return a.reshape((GU, 64) + a.shape[2:])

    us = o["pool_us"].transpose(2, 1, 0).reshape(NS, 1, 512)
    cn = o["cn_p"].transpose(1, 2, 0)
    return (o["y"][None, :SEQ], o["y"][SEQ:, None],
            o["pool_p"].transpose(2, 1, 0).reshape(1, 1, 15, 512), cn[None, None, :, :P], cn[None, None, :, P],
            o["m_p"][:, 0][None, None], ungroup(o["s5_p"][:, 0])[None, None], ungroup(o["s5_p"][:, 1])[None, None],
            np.concatenate([o["pool_s"], us], axis=1)[None],
            o["c_s"].transpose(1, 0, 2).reshape(1, NS, H, P, P), o["n_s"].reshape(1, NS, H, P), o["m_s"][None],
            ungroup(o["s5_sr"]).transpose(2, 0, 1)[None], ungroup(o["s5_si"]).transpose(2, 0, 1)[None])
```

```python
from contextlib import ExitStack
from math import pi

import numpy as np

import concourse.bass as bass
from concourse import mybir

F32 = mybir.dt.float32
I32 = mybir.dt.int32
ALU = mybir.AluOpType
ACT = mybir.ActivationFunctionType
AX = mybir.AxisListType.X

P = 128
D = 1024
KC = D // P
SEQ = 512
NS = 8
NT = SEQ + NS
TILES = SEQ // P
ROWS = [P] * TILES + [NS]
HALF = NT // 2
H = 4
GU = 64
PAIRS = GU // 2
CW = 16
L = P // CW
NCH = SEQ // L
UC = NS + NCH + NS
SC = NCH + NS
E = 32
CAP = 64
ROUNDS = -(-NT // CAP)
EPS = 1e-6
BIG = 1e30
KSCALE = float(P) ** -0.5
KROW = 2 * P - CW
KZERO = KROW - P

CONST = {}
_at = 0
for _name, _n in [("ident", P), ("before", P), ("ones", P), ("causal", P), ("window", 4 * NS),
                  ("iota", P), ("eio", E), ("reve", E), ("revg", 4), ("tokid", 5), ("valid", 5),
                  ("half", 1), ("ramp", 4 * CW), ("head", 4 * P), ("keep", SEQ), ("diag", CW)]:
    CONST[_name] = (_at, _n)
    _at += _n
CONSTS = _at


def constants():
    c = np.zeros((P, CONSTS), np.float32)

    def put(name, a):
        at, n = CONST[name]
        c[:a.shape[0], at:at + n] = a.reshape(a.shape[0], n)

    p = np.arange(P)
    put("ident", np.eye(P, dtype=np.float32))
    put("before", (p[:, None] < p[None, :]).astype(np.float32))
    put("ones", np.ones((P, P), np.float32))
    put("causal", np.where(p[:, None] <= p[None, :], 0.0, -BIG).astype(np.float32))
    w = np.zeros((120, 4, NS), np.float32)
    for g in range(4):
        for n in range(NS):
            w[n * 15 + 15 - (2 ** (g + 1) - 1):n * 15 + 15, g, n] = 1.0
    put("window", w)
    put("iota", np.tile(np.arange(CAP, dtype=np.float32), (P, 2)))
    put("eio", np.tile(np.arange(E, dtype=np.float32), (P, 1)))
    put("reve", np.tile(E - np.arange(E, dtype=np.float32), (P, 1)))
    put("revg", np.tile(4 - np.arange(4, dtype=np.float32), (P, 1)))
    put("tokid", (np.arange(5)[None, :] * P + p[:, None] + 1).astype(np.float32))
    v = np.ones((P, 5), np.float32)
    v[NS:, 4] = 0
    put("valid", v)
    put("half", (p[:, None] >= CAP).astype(np.float32) - 2.0)
    t = np.arange(CW)
    put("ramp", np.tile(np.stack([1.0 / np.minimum(2 ** (g + 1), t + 1) for g in range(4)])[None],
                        (P, 1, 1)).astype(np.float32))
    h = np.zeros((4, 4, P), np.float32)
    for i in range(4):
        h[i, i] = 1.0
    put("head", h)
    k = np.ones((4, SEQ), np.float32)
    k[:, ::P] = 0
    put("keep", k)
    put("diag", (p[:, None] % CW == t[None, :]).astype(np.float32))
    return c


X_AT = 0
CONST_AT = X_AT + 5 * D
GB_AT = CONST_AT + CONSTS + CONSTS % 2
WR_AT = GB_AT + D
SMALL_AT = WR_AT + 2 * (KC * 36 + 36)
STAGE_AT = SMALL_AT + 2182
ARENA = 207 * 256


class PsumRing:

    def __init__(self, jobs, full, freed):
        self.jobs, self.full, self.freed = jobs, full, freed
        self.at = {name: n for n, (name, _) in enumerate(jobs)}
        assert len(self.at) == len(jobs)
        seen, self.count = {}, []
        for _, eng in jobs:
            seen[eng] = seen.get(eng, 0) + 1
            self.count.append(seen[eng])

    def slot(self, *name):
        return self.at[name] % 4

    def wait_free(self, pe, *name):
        n = self.at[name]
        if n >= 4:
            self.wait_emptied(pe, *self.jobs[n - 4][0])

    def wait_full(self, eng, *name):
        eng.wait_ge(self.full, self.at[name] + 1)

    def wait_emptied(self, eng, *name):
        n = self.at[name]
        eng.wait_ge(self.freed[self.jobs[n][1]], self.count[n])


def in_order_of_router(main, transpose, logits):
    for i in range(5):
        main(i)
        if i >= 1:
            transpose(i - 1)
        if i >= 2:
            logits(i - 2)
    transpose(4)
    logits(3)
    logits(4)


def jobs_of_kernel():
    j = []
    for i in range(5):
        j.append((("ht", i), "act" if i % 2 else "dve"))
    j.append((("gates",), "dve"))
    j += [(("z", n), "act") for n in range(4)] + [(("ws",), "dve")]
    j += [(("z", n), "act") for n in range(4, 16)]
    j += [(("cols",), "dve"), (("sg",), "dve")]
    j += [(("bc", h), "dve") for h in range(H)]
    j += [(("st",), "dve")]
    for c in range(TILES):
        j += [(("kt", c), "dve"), (("s", c), "dve")]
        if c < 2:
            j += [(("z", 16 + c), "act")]
        j += [(("kv", c), "dve")]
    j += [(("num", 0), "dve"), (("z", 18), "act"), (("num", 1), "dve"), (("z", 19), "act"), (("num", 2), "dve")]
    j += [(("pw", g), "act") for g in range(4)]
    j += [(("num", 3), "dve")]
    j += [(("hT", c), "dve") for c in range(TILES)]

    def routed(l, main):
        in_order_of_router(lambda i: j.append((main(i), "dve")), lambda i: j.append((("tr", l, i), "act")),
                           lambda i: j.append((("lg", l, i), "dve")))
        j.append((("pos", l), "dve"))
    routed(0, lambda i: ("wo", i))
    j += [(("k",), "dve")]
    j += [(("u", q), "act" if q % 2 else "dve") for q in range(8)]
    j += [(("zs", q), "dve") for q in range(8)]
    j += [(("y", q), "act" if q % 2 else "dve") for q in range(8)]
    j += [(("yT", q), "act") for q in range(8)]
    j += [(("gl", 0, i), "dve") for i in range(5)]
    routed(1, lambda i: ("gl", 1, i))
    return j


def bass_hybrid_step(nc, T):
    ctx = ExitStack()
    with ctx:
        sems = {}

        def sem(name):
            if name not in sems:
                sems[name] = ctx.enter_context(nc.semaphore(name))
            return sems[name]

        arena = ctx.enter_context(nc.sbuf_tensor("arena", [P, ARENA], F32))
        idx_list = ctx.enter_context(nc.sbuf_tensor("idx_list", [P, E], I32))
        idx_now = ctx.enter_context(nc.sbuf_tensor("idx_now", [P, 2], I32))
        idx_back = ctx.enter_context(nc.sbuf_tensor("idx_back", [P, 10], I32))
        most = ctx.enter_context(nc.sbuf_tensor("most", [P, 2], I32))
        ps = ctx.enter_context(nc.psum_tensor("ps", [P, 8, 512], F32))

        def place(at, *shape, parts=P, base=0):
            n = int(np.prod(shape))
            assert at + n <= ARENA
            a = arena[base:base + parts, at:at + n]
            if len(shape) == 2:
                a = a.rearrange("p (a b) -> p a b", a=shape[0])
            if len(shape) == 3:
                a = a.rearrange("p (a b c) -> p a b c", a=shape[0], b=shape[1])
            if len(shape) == 4:
                a = a.rearrange("p (a b c d) -> p a b c d", a=shape[0], b=shape[1], c=shape[2])
            return a

        def const(name, parts=P):
            at, n = CONST[name]
            return arena[0:parts, CONST_AT + at:CONST_AT + at + n]

        def spread(a, n):
            a = a.unsqueeze(len(a.shape))
            return a.broadcast_to(tuple(a.shape[:-1]) + (n,))

        def spread_mid(a, n):
            a = a.unsqueeze(1)
            return a.broadcast_to((a.shape[0], n) + tuple(a.shape[2:]))

        ident, before, ones, causal = const("ident"), const("before"), const("ones"), const("causal")

        X = place(X_AT, 5, D)
        GB = place(GB_AT, D)
        WR = [place(WR_AT + l * (KC * 36 + 36), KC, 36) for l in range(2)]
        BR = [place(WR_AT + l * (KC * 36 + 36) + KC * 36, 36) for l in range(2)]

        small_at = [SMALL_AT]

        def small(*shape, parts=P):
            at = small_at[0]
            small_at[0] += int(np.prod(shape))
            assert small_at[0] <= STAGE_AT
            return place(at, *shape, parts=parts)

        ss, var, root, rstd = small(5), small(5), small(5), small(5)
        LG = small(5, 36)
        gmax, gtop, gsum, gw = small(5), small(5), small(5), small(5)
        og, gexp, gneg = small(5, 4), small(5, 4), small(5, 4)
        scratch_at = small_at[0]
        me, hit = small(5, E), small(5, E)
        oh = [small(5, E), small(5, E)]
        OH, PRE, POS = small(5, E), small(5, E), small(5, E)
        both = small(E)
        m1, m2, etop, dexp, dsum = small(5), small(5), small(5), small(5), small(5)
        pw_ = [small(5), small(5)]
        RK, EID, QR = small(2, 5), small(2, 5), small(2, 5)
        cntmax = small(1)
        m0s, SG, SM = small(H, parts=NS), small(8, parts=NS), small(12, parts=NS)
        gcol, dec = small(16), small(16)
        ecol = small(16)
        den, dab, rden = small(H), small(H), small(H)
        vs, us, sos = small(H, NS), small(H, NS), small(H, NS)
        rs = small(NS * H)
        bg, mrun = small(2, parts=H), small(TILES + 1, parts=H)
        pscale = small(H)
        GK = small(2, KC)
        sden = small(3 * H, parts=NS)

        A = STAGE_AT

        def slot(*name):
            s = ring.slot(*name)
            return ps[:, 2 * s:2 * s + 2, :]

        def slot_flat(*name):
            return slot(*name).rearrange("p b n -> p (b n)")

        ring = PsumRing(jobs_of_kernel(), sem("psum_full"),
                        {"dve": sem("psum_emptied_by_dve"), "act": sem("psum_emptied_by_act")})

        def take(eng, *name):
            ring.wait_full(eng, *name)

        def give(eng, ins, *name):
            who = ring.jobs[ring.at[name]][1]
            ins.then_inc(ring.freed[who], 1)
            ring.wait_emptied(eng, *name)

        HH = place(A, 5, D)
        KB = place(A, NS * H, P)
        HT = place(A + 5120, KC, NT)
        WIN = [place(A + 9280 + 2048 * b, KC, 256) for b in range(2)]
        WG8 = place(A + 40000, KC, 8)
        WOUT = place(A + 5120, KC, D)
        Zk, Zq, Zv, Zo = (place(A + 13376 + 2080 * n, H, NT) for n in range(4))
        MIX = place(A + 13376, KC, NT)
        HM = place(A + 17536, TILES, H, P)
        W = place(A + 21696, H, TILES, P)
        V1 = place(A + 23744, TILES, H, 130)
        KT = place(A + 25824, TILES, H, P)
        DT = place(A + 2560, H, NT)
        UE = place(A + 27904, H, 528)
        QT = place(A + 30016, H, SEQ)
        CN = place(A + 32064, TILES, H, 129)
        KZ = place(A + 32064, KC, KZERO)
        TU = [place(A + 34128 + 528 * b, 528) for b in range(2)]
        rows = [place(A + 35184 + NT * n, NT, parts=H) for n in range(8)]
        li, lf, bc_, ar, mr, wi, er, tr_ = rows
        CS = place(A + 35184, NS * H, P)
        PW = place(A + 39344, H, P)
        PB = place(A + 34128, SEQ, parts=120)
        ks = place(A + 40500, H, P, parts=NS)
        n0s = place(A + 41012, H, P, parts=NS)
        qs = place(A + 1536, H, P, parts=NS)
        DB = place(A + 41524, NS * H)

        WGU = [place(A + 4096 * b, KC, 512) for b in range(2)]
        WD = [place(A + 8192 + 2048 * b, 2, D) for b in range(2)]
        XG = [place(A + 12288 + 512 * b, 512) for b in range(2)]
        XT = [place(A + 13312 + 512 * b, 4, P) for b in range(2)]
        SIL = [place(A + 14336 + P * b, P) for b in range(2)]
        ACTB = [place(A + 14592 + P * b, P) for b in range(2)]
        AT = [place(A + 14848 + P * b, P) for b in range(2)]
        YE = [place(A + 15104 + 512 * b, 512) for b in range(2)]
        OHR = place(A + 16128, 10, P)
        YG = [place(A + 16128, 4, D),
              place(A + 17408, 10, D)]
        HB = place(A + 27872, 5, D)
        HTB = [[place(at + 1024 * b, KC, P) for b in range(2)] for at in (A + 25824, A + 17408)]

        CIN = [place(A + 20224 + 512 * n, PAIRS, CW) for n in range(2)]
        VR, VI = place(A + 21248, 2, L, CW), place(A + 21504, 2, L, CW)
        S5_AT = A + 21760
        BBR, BBI = place(S5_AT, PAIRS, CW), place(S5_AT + 512, PAIRS, CW)
        sp_ = [place(S5_AT + 1024 + 32 * n, PAIRS) for n in range(20)]
        PWR, PWI = place(S5_AT + 1664, PAIRS, L + 1), place(S5_AT + 1952, PAIRS, L + 1)
        GTMP = place(S5_AT + 2240, 2, L + 1, CW)
        UNIT = [(sp_[7], sp_[4])] + [(place(at, PAIRS), place(at2, PAIRS)) for at, at2 in (
            (S5_AT + 1024, S5_AT + 1056), (S5_AT + 1088, S5_AT + 1120), (S5_AT + 1216, S5_AT + 2784),
            (S5_AT + 2816, S5_AT + 2848), (S5_AT + 2880, S5_AT + 2912))]
        BACKR, BACKI = place(S5_AT + 1024 + 320, PAIRS, L), place(S5_AT + 2528, PAIRS, L)
        DSK = place(S5_AT + 2952, KC)
        BIN = [place(A + 24736 + 512 * n, PAIRS, CW) for n in range(2)]
        BTMP = [place(A + 30016 + 512 * n, PAIRS, CW) for n in range(2)]
        M = place(A + 24736, PAIRS, 2, P)
        GR, GI = place(A + 32928, PAIRS, L + 1, CW), place(A + 37536, PAIRS, L + 1, CW)

        HC = place(A + 27648, 5, D)
        H2 = place(A, 5, D)
        U = place(A, GU, UC)
        XK = place(A + 5120, L, D, parts=UC)
        HR, HI = place(A + 5120, PAIRS, SC), place(A + 7424, PAIRS, SC)
        RR, RI = place(A + 9728, PAIRS, NCH), place(A + 11776, PAIRS, NCH)
        TMQ = place(A + 13824, 4, NCH)
        BD = [place(A + 13312 + 1024 * n, PAIRS, 2 * CW) for n in range(2)]
        XR = [place(A + 13312 + 1024 * b, D, parts=UC) for b in range(2)]
        TC, TS = place(A + 15360, PAIRS, NCH), place(A + 17408, PAIRS, NCH)
        R8 = TMP = place(A + 19456, PAIRS, NCH)
        KS = place(S5_AT, KC, P)
        H0R, H0I = place(S5_AT + 1664, PAIRS * NS), place(S5_AT + 1920, PAIRS * NS)
        SHR, SHI = (place(S5_AT + 2176 + 256 * n, PAIRS, NS) for n in range(2))
        SHT = place(scratch_at, PAIRS, NS)
        SKIP = place(A + 21504, KC, CW)
        HEND = place(A + 21632, 2, PAIRS)
        YK = place(A + 9728, L, D)
        TT = place(A + 24736, GU, P)
        YT = place(A, KC, NT)
        WGL = [place(A + 24736 + 8192 * ch, KC, D) for ch in range(2)]
        SIG = [place(A + 5120 + 512 * b, 512) for b in range(2)]
        GT = [place(A + 6144 + 512 * b, 512) for b in range(2)]
        SUM = place(A + 7168, 2, 512, parts=NS)

        def y_views(q, b):
            return (YK[0:SC, :, q * P:(q + 1) * P].rearrange("p l (j b c) -> p b j l c", b=2, c=CW)[:, b],
                    slot("y", q)[0:SC, b, :].rearrange("p (j l c) -> p j l c", j=4, l=L))

        hd, yd, kp = T["hd"], T["yd"], T["kp"]
        sdk, sdq, sdd = T["sdk"], T["sdq"], T["sdd"]
        hd_halves = hd.rearrange("t (h c) -> (t h) c", h=2)
        yd_rows = yd.rearrange("j t c -> (j t) c")

        block = ctx.enter_context(nc.Block())

        def tile_rows(a, i):
            return a[0:ROWS[i], i, :]

        @block.sync
        def _(sp):
            def load(dst, src, name):
                sp.dma_start(dst, src).then_inc(sem(name), 16)

            load(place(CONST_AT, CONSTS), T["const"], "consts")
            for i in range(TILES):
                load(X[:, i, :], T["x_prompt"][i * P:(i + 1) * P, :], f"x_in_{i}")
            sp.wait_ge(sem("x_cleared"), 1)
            load(X[0:NS, TILES, :], T["x_sample"], f"x_in_{TILES}")
            load(GB, T["norms"][0], "norm_in")
            load(WG8, T["w_gate8"], "w_gates_in")
            load(bg, T["b_gates"], "small_in")
            load(m0s, T["m0"], "small_in")
            load(pscale, T["pool_scale"], "small_in")
            load(GK, T["norm_ffn"], "small_in")
            for l in range(2):
                load(WR[l], T["w_router"][l], "small_in")
                load(BR[l], T["b_router"][l], "small_in")
            load(PW, T["pool_w"], "pool_in")
            load(PB, T["pool_rows"], "pool_in")
            load(n0s, T["n0"], "n0_in")
            kv = kp.rearrange("(b p) n -> p b n", p=P)
            sp.wait_ge(sem("kz_cleared"), 1)
            sp.dma_start(kv[:, :, 0:KZERO], KZ).then_inc(sem("kz_out"), 16)
            for n in range(10):
                if n >= 2:
                    ring.wait_full(sp, "z", 2 * (n - 2) + 1)
                load(WIN[n % 2], T["w_in"][n], f"w_in_{n % 2}")
            sp.wait_ge(sem("h_0"), 5)
            load(GB, T["norms"][1], "norm_in")
            sp.dma_start(T["pool_s"], T["pool_buf"]).then_inc(sem("stored"), 16)
            sp.wait_ge(sem("rows_dead"), 1)
            load(CS, T["c0"], "c0_in")
            ring.wait_emptied(sp, "z", 3)
            sp.dma_start(T["pool_p"], UE[:, :, 528 - 15:528]).then_inc(sem("stored"), 16)
            sp.dma_start(T["pool_us"], us).then_inc(sem("stored"), 16)
            sp.wait_ge(sem("ks_ready"), 1)
            sp.dma_start(sdk, ks.rearrange("p h k -> p (h k)")).then_inc(sem("sd_out"), 16)
            sp.dma_start(sdd, SM[:, 0:H]).then_inc(sem("sd_out"), 16)
            sp.dma_start(sdq, qs.rearrange("p h k -> p (h k)")).then_inc(sem("sd_out"), 16)
            sp.dma_start(T["n_s"], n0s.rearrange("p h k -> p (h k)")).then_inc(sem("stored"), 16)
            sp.dma_start(T["m_s"], sden[:, 0:H]).then_inc(sem("stored"), 16)
            ring.wait_full(sp, "z", 19)
            load(WOUT, T["w_out"], "w_out_in")
            sp.wait_ge(sem("sd_out"), 48)
            ring.wait_full(sp, "pw", 3)
            load(KB, sdk.rearrange("n (h k) -> (n h) k", h=H).partition_broadcast(P), "kb_in")
            load(DB, sdd.rearrange("n h -> (n h)").partition_broadcast(P), "kb_in")
            ring.wait_full(sp, "num", TILES - 1)
            for n in range(2):
                load(BIN[n], T["s5_cb"][2 + n], "s5_in")
            load(sp_[0], T["s5_ls"], "s5_in")
            load(sp_[1], T["s5_lr"], "s5_in")
            load(sp_[2], T["s5_li"], "s5_in")
            load(DSK, T["s5_d"], "s5_in")
            sp.wait_ge(sem("kb_used"), 1)
            load(KB, sdq.rearrange("n (h k) -> (n h) k", h=H).partition_broadcast(P), "kb_in")
            sp.wait_ge(sem("kb_used"), 1)
            sp.dma_start(T["c_s"], CS).then_inc(sem("stored"), 16)
            sp.wait_ge(sem("cn_ready"), 1)
            sp.dma_start(T["cn_p"], CN[:, TILES - 1]).then_inc(sem("stored"), 16)
            sp.dma_start(T["m_p"], mrun[:, TILES:TILES + 1]).then_inc(sem("stored"), 16)

            def experts(l):
                def turns(r):
                    with sp.Fori(0, E // 2) as k:
                        t = k + 16 * r
                        for s in range(2):
                            sp.wait_ge(sem(f"gu_done_{l}"), 2 * t + s + 1)
                            e = 2 * k + s
                            sp.dma_start(WGU[s], T["w_gu"][l][bass.ds(e, 1)].rearrange("e p k n -> p (e k) n")
                                         ).then_inc(sem(f"wgu_in_{l}_{s}"), 16)
                        for s in range(2):
                            sp.wait_ge(sem(f"down_done_{l}"), 2 * t + s + 1)
                            e = 2 * k + s
                            sp.dma_start(WD[s], T["w_down"][l][bass.ds(e, 1)].rearrange("e p k n -> p (e k) n")
                                         ).then_inc(sem(f"wd_in_{l}_{s}"), 16)
                turns(0)
                sp.wait_ge(sem(f"h_{2 * l + 1}"), 5)
                load(GB, T["norms"][2 * l + 2], "norm_in")
                sp.wait_ge(sem("most_ready"), l + 1)
                n = sp.value_load(most[0:1, l:l + 1], min_val=0, max_val=NT)
                with sp.If(n > CAP):
                    with sp.Fori(1, ROUNDS) as r:
                        with sp.If(n > r * CAP):
                            turns(r)

            sp.wait_ge(sem("x_mixed"), 1)
            for n in range(2):
                load(CIN[n], T["s5_cb"][n], "s5_in")
            experts(0)
            sp.wait_ge(sem("x_moe"), 1)
            load(H0R, T["s5_h0r"], "s5_in")
            load(H0I, T["s5_h0i"], "s5_in")
            sp.wait_ge(sem("xk_cleared"), 2)
            for i in range(5):
                sp.wait_ge(sem("h_2"), i + 1)
                if i < TILES:
                    n = NS + i * P // L
                    load(XK[n:n + P // L], H2[:, i, :], "xk_in")
            load(XK[0:NS, L - 1, :], H2[0:NS, TILES], "xk_in")
            load(XK[NS + NCH:UC, 0, :], H2[0:NS, TILES], "xk_in")
            load(GB, T["norms"][3], "norm_in")
            sp.wait_ge(sem("taps_ready"), 1)
            sp.dma_start(kv[:, :, KZERO:KROW], KS).then_inc(sem("taps_out"), 16)
            sp.wait_ge(sem("taps_out"), 16)
            sp.wait_ge(sem("kz_out"), 16)
            ring.wait_full(sp, "zs", 7)
            kg = kp.rearrange("(g c) n -> c g n", c=CW)
            for s in range(L):
                load(TT[CW * s:CW * s + CW], kg[:, :, KZERO - CW * s:KZERO - CW * s + P], "taps_in")
            sp.wait_ge(sem("states_in"), 3)
            sp.dma_start(T["s5_p"], HEND).then_inc(sem("stored"), 16)
            sp.dma_start(T["s5_sr"], SHR).then_inc(sem("stored"), 16)
            sp.dma_start(T["s5_si"], SHI).then_inc(sem("stored"), 16)
            ring.wait_full(sp, "y", 3)
            load(WGL[0][:, 0:4], T["w_glu"][0][:, 0:4], "w_glu_in_0")
            ring.wait_full(sp, "y", 7)
            load(WGL[0][:, 4:8], T["w_glu"][0][:, 4:8], "w_glu_in_1")
            load(WGL[1], T["w_glu"][1], "w_glu_in_2")
            sp.wait_ge(sem("x_mixed"), 2)
            experts(1)
            for i in range(5):
                sp.wait_ge(sem("h_4"), i + 1)
                sp.dma_start(T["y"][i * P:i * P + ROWS[i], :], tile_rows(HC, i)).then_inc(sem("stored"), 16)
            sp.wait_ge(sem("stored"), 16 * (1 + 2 + 1 + 2 + 2 + 3 + 5))

        @block.tensor
        def _(pe):
            def full(mm):
                mm.then_inc(ring.full, 1)

            def transposes(name, pieces):
                ring.wait_free(pe, *name)
                for out, in_ in pieces:
                    k = in_.shape[0]
                    mm = pe.transpose(out, in_, ident[0:k, 0:k])
                full(mm)

            pe.sem_inc(sem("m_turned"), 1)
            for l in range(2):
                for name in ("gu_done", "down_done", "xt_done"):
                    pe.sem_inc(sem(f"{name}_{l}"), 2)
            pe.wait_ge(sem("consts"), 16)
            for i in range(5):
                n = ROWS[i]
                pe.wait_ge(sem("h_0"), i + 1)
                o = slot("ht", i)
                transposes(("ht", i), [(o[:, kc // 4, (kc % 4) * P:(kc % 4) * P + n], HH[0:n, i, kc * P:(kc + 1) * P])
                                       for kc in range(KC)])
            pe.wait_ge(sem("w_gates_in"), 16)
            for i in range(5):
                ring.wait_emptied(pe, "ht", i)
            ring.wait_free(pe, "gates")
            o = slot("gates")
            for b in range(2):
                for kc in range(KC):
                    for q in range(2):
                        mm = pe.matmul(o[32 * q:32 * q + H, b, 0:HALF], WG8[:, kc, H * q:H * q + H],
                                       HT[:, kc, b * HALF:(b + 1) * HALF], start=kc == 0, stop=kc == KC - 1)
            full(mm)

            def project(n):
                if n % 2 == 0:
                    pe.wait_ge(sem(f"w_in_{(n // 2) % 2}"), 16 * (n // 4 + 1))
                ring.wait_free(pe, "z", n)
                o = slot("z", n)
                w = WIN[(n // 2) % 2]
                for kc in range(KC):
                    for b in range(2):
                        mm = pe.matmul(o[:, b, 0:HALF], w[:, kc, (n % 2) * P:(n % 2 + 1) * P],
                                       HT[:, kc, b * HALF:(b + 1) * HALF], start=kc == 0, stop=kc == KC - 1)
                full(mm)

            for n in range(4):
                project(n)
            pe.wait_ge(sem("pool_in"), 32)
            ring.wait_free(pe, "ws")
            o = slot_flat("ws")
            for g in range(4):
                mm = pe.matmul(o[:, g * NS:(g + 1) * NS], PB[:, g * P:(g + 1) * P],
                               const("window")[0:120, g * NS:(g + 1) * NS], start=True, stop=True)
            full(mm)
            for n in range(4, 16):
                project(n)
            pe.wait_ge(sem("gate_rows"), 1)
            ring.wait_free(pe, "cols")
            o = slot_flat("cols")
            transposes(("cols",), [(o[:, 16 * q + H * c:16 * q + H * c + H], (ar, er)[q][:, c * P:(c + 1) * P])
                                   for q in range(2) for c in range(TILES)])
            o = slot_flat("sg")
            transposes(("sg",), [(o[0:NS, 0:H], li[:, SEQ:NT]), (o[0:NS, H:2 * H], lf[:, SEQ:NT])])
            for h in range(H):
                ring.wait_free(pe, "bc", h)
                o = slot("bc", h)
                pick = const("head", H)[:, h * P:(h + 1) * P]
                pe.matmul(o[:, 0, :], pick, mr[:, 0:SEQ], start=True, stop=True)
                full(pe.matmul(o[:, 1, :], pick, wi[:, 0:SEQ], start=True, stop=True))
            ring.wait_emptied(pe, "z", 15)
            o = slot("st")
            transposes(("st",), [(o[0:NS, q, h * P:(h + 1) * P], (Zk, Zq)[q][:, h, SEQ:NT])
                                 for q in range(2) for h in range(H)])
            for c in range(TILES):
                cc = slice(c * P, (c + 1) * P)
                o = slot("kt", c)
                transposes(("kt", c), [(o[:, q, h * P:(h + 1) * P], (Zk, Zv)[q][:, h, cc])
                                       for q in range(2) for h in range(H)])
                ring.wait_free(pe, "s", c)
                o = slot("s", c)
                for h in range(H):
                    mm = pe.matmul(o[:, 0, h * P:(h + 1) * P], Zk[:, h, cc], Zq[:, h, cc], start=True, stop=True)
                full(mm)
                if c < 2:
                    project(16 + c)
                ring.wait_emptied(pe, "kt", c)
                ring.wait_free(pe, "kv", c)
                o = slot("kv", c)
                for h in range(H):
                    mm = pe.matmul(o[:, h // 2, (h % 2) * 129:(h % 2) * 129 + 129], KT[:, c, h], V1[:, c, h, 0:129],
                                   start=True, stop=True)
                full(mm)

            def numerator(c):
                ring.wait_free(pe, "num", c)
                ring.wait_emptied(pe, "s", c)
                if c:
                    ring.wait_emptied(pe, "kv", c - 1)
                o = slot("num", c)
                for h in range(H):
                    out = o[:, h // 2, (h % 2) * 129:(h % 2) * 129 + 129]
                    mm = pe.matmul(out, W[:, h, c], V1[:, c, h, 0:129], start=True, stop=c == 0)
                    if c:
                        mm = pe.matmul(out, QT[:, h, c * P:(c + 1) * P], CN[:, c - 1, h], start=False, stop=True)
                full(mm)
            numerator(0)
            project(18)
            numerator(1)
            project(19)
            numerator(2)
            for g in range(4):
                pe.wait_ge(sem("pool_mixed"), g + 1)
                ring.wait_free(pe, "pw", g)
                o = slot("pw", g)
                for b in range(2):
                    mm = pe.matmul(o[:, b, 0:HALF], PW[:, g], DT[:, g, b * HALF:(b + 1) * HALF], start=True, stop=True)
                full(mm)
            numerator(3)
            for c in range(TILES):
                ring.wait_emptied(pe, "num", c)
                ring.wait_free(pe, "hT", c)
                o = slot("hT", c)
                transposes(("hT", c), [(o[:, 0, h * P:(h + 1) * P], HM[:, c, h]) for h in range(H)])
            pe.wait_ge(sem("w_out_in"), 16)
            for g in range(4):
                ring.wait_emptied(pe, "pw", g)
            ring.wait_emptied(pe, "hT", TILES - 1)
            def sample_product(o, x, w):
                for k0 in range(0, KC, 4):
                    for b in range(2):
                        for q in range(4):
                            kc = k0 + q
                            mm = pe.matmul(o[32 * q:32 * q + NS, b, :], x[:, kc, SEQ:NT],
                                           w[:, kc, b * 512:(b + 1) * 512], start=k0 == 0, stop=k0 == KC - 4)
                return mm

            def w_out(i):
                if i == TILES:
                    pe.wait_ge(sem("mix_samples"), 1)
                ring.wait_free(pe, "wo", i)
                o = slot("wo", i)
                n = ROWS[i]
                if i == TILES:
                    full(sample_product(o, MIX, WOUT))
                    return
                for kc in range(KC):
                    for b in range(2):
                        mm = pe.matmul(o[0:n, b, :], MIX[:, kc, i * P:i * P + n], WOUT[:, kc, b * 512:(b + 1) * 512],
                                       start=kc == 0, stop=kc == KC - 1)
                full(mm)

            def router(l, main):
                def transpose(i):
                    n = ROWS[i]
                    pe.wait_ge(sem("x_tile"), 10 * l + i + 1)
                    o = slot("tr", l, i)
                    transposes(("tr", l, i), [(o[:, kc // 4, (kc % 4) * P:(kc % 4) * P + n],
                                               X[0:n, i, kc * P:(kc + 1) * P]) for kc in range(KC)])

                def logits(i):
                    n = ROWS[i]
                    ring.wait_emptied(pe, "tr", l, i)
                    ring.wait_free(pe, "lg", l, i)
                    o = slot_flat("lg", l, i)
                    for kc in range(KC):
                        mm = pe.matmul(o[0:n, 0:36], HTB[l][i % 2][:, kc, 0:n], WR[l][:, kc], start=kc == 0,
                                       stop=kc == KC - 1)
                    full(mm)
                in_order_of_router(main, transpose, logits)
                pe.wait_ge(sem("chosen"), l + 1)
                ring.wait_free(pe, "pos", l)
                o = slot("pos", l)
                flat = "p t e -> p (t e)"
                pe.matmul(o[:, 0, 0:5 * E], before, OH.rearrange(flat), start=True, stop=False)
                pe.matmul(o[:, 0, 0:5 * E], ones, PRE.rearrange(flat), start=False, stop=True)
                full(pe.matmul(o[:, 1, 0:E], ones, both, start=True, stop=True))
                ring.wait_emptied(pe, "pos", l)

            def experts(l):
                def turns(r):
                    pe.wait_ge(sem(f"spots_{l}"), r + 1)
                    for q in range(10):
                        mm = pe.matmul(ps[:, 0, 0:E], OHR[:, q], oh[q // 5][:, q % 5], start=q == 0, stop=q == 9)
                    mm.then_inc(sem(f"list_done_{l}"), 1)
                    pe.wait_ge(sem(f"list_read_{l}"), r + 1)
                    pe.sem_inc(sem("round_marks"), 1)
                    with pe.Fori(0, E // 2) as k:
                        t = k + 16 * r
                        for s in range(2):
                            pe.wait_ge(sem(f"xg_in_{l}_{s}"), 16 * t + 16)
                            for b in range(4):
                                mm = pe.transpose(ps[:, s, b * P:(b + 1) * P], XG[s][:, b * P:(b + 1) * P], ident)
                            mm.then_inc(sem(f"xt_done_{l}"), 1)
                        for s in range(2):
                            pe.wait_ge(sem(f"wgu_in_{l}_{s}"), 16 * t + 16)
                            pe.wait_ge(sem(f"xt_ready_{l}"), 2 * t + s + 1)
                            for kc in range(KC):
                                for f in range(2):
                                    mm = pe.matmul(ps[CAP * f:CAP * f + CAP, 2 + s, 0:256],
                                                   XT[s][:, kc % 4, CAP * (kc // 4):CAP * (kc // 4) + CAP],
                                                   WGU[s][:, kc, 256 * f:256 * f + 256],
                                                   start=kc == 0, stop=kc == KC - 1)
                            mm.then_inc(sem(f"gu_done_{l}"), 1)
                        for s in range(2):
                            pe.wait_ge(sem(f"act_ready_{l}"), 2 * t + s + 3)
                            pe.transpose(ps[:, 4 + s, 0:P], ACTB[s], ident).then_inc(sem(f"at_done_{l}"), 1)
                        for s in range(2):
                            pe.wait_ge(sem(f"wd_in_{l}_{s}"), 16 * t + 16)
                            pe.wait_ge(sem(f"at_ready_{l}"), 2 * t + s + 1)
                            pe.wait_ge(sem(f"y_ready_{l}"), 2 * t + 2)
                            for f in range(2):
                                for b in range(2):
                                    mm = pe.matmul(ps[CAP * b:CAP * b + CAP, 6 + s, :], AT[s][:, CAP * f:CAP * f + CAP],
                                                   WD[s][:, f, 512 * b:512 * b + 512], start=f == 0, stop=f == 1)
                            mm.then_inc(sem(f"down_done_{l}"), 1)
                        if l == 0:
                            pe.wait_ge(sem("v_ready"), t + 1)
                            pe.wait_ge(sem("m_copied"), t + 1)
                            for j in range(2):
                                for ri in range(2):
                                    mm = pe.transpose(ps[:, 4 + j, P * (1 + ri):P * (2 + ri)],
                                                      (VR, VI)[ri][:, j].rearrange("p l c -> p (l c)"), ident)
                            mm.then_inc(sem("m_turned"), 1)
                    if l == 0:
                        pe.wait_ge(sem("m_copied"), 16 * r + 17)
                    pe.wait_ge(sem(f"y_ready_{l}"), E * r + E + 2)
                turns(0)
                n = pe.value_load(most[0:1, l:l + 1], min_val=0, max_val=NT)
                with pe.If(n > CAP):
                    with pe.Fori(1, ROUNDS) as r:
                        with pe.If(n > r * CAP):
                            turns(r)

            router(0, w_out)
            experts(0)

            pe.wait_ge(sem("bd_ready"), 2)
            ring.wait_free(pe, "k")
            o = slot_flat("k")
            for pb in range(8):
                for pq in range(4):
                    pr = 4 * pb + pq
                    out = o[32 * pq:32 * pq + 32, pb * P:(pb + 1) * P]
                    pe.matmul(out, BD[0][:, pr], GR[:, pr, 0:L], start=True, stop=False)
                    mm = pe.matmul(out, BD[1][:, pr], GI[:, pr, 0:L], start=False, stop=True)
            full(mm)
            for q in range(8):
                pe.wait_ge(sem(f"xr_ready_{q % 2}"), q // 2 + 1)
                o = slot("u", q)
                transposes(("u", q), [(o[:, j // 4, (j % 4) * UC:(j % 4 + 1) * UC],
                                       XR[q % 2][:, j * P:(j + 1) * P]) for j in range(8)])
            for q in range(8):
                ring.wait_free(pe, "zs", q)
                ring.wait_emptied(pe, "u", q)
                o = slot("zs", q)
                for j in range(4):
                    pr = 4 * q + j
                    for ri in range(2):
                        for g2 in range(2):
                            mm = pe.matmul(o[64 * g2:64 * g2 + 64, ri, j * SC:(j + 1) * SC],
                                           M[:, pr, ri, 64 * g2:64 * g2 + 64], U[:, 2 * pr + g2, 0:SC],
                                           start=True, stop=True)
                full(mm)
            pe.wait_ge(sem("taps_in"), 16 * L)
            pe.wait_ge(sem("states_in"), 1)
            for q in range(8):
                ring.wait_free(pe, "y", q)
                o = slot("y", q)
                if q == 4:
                    pe.wait_ge(sem("states_in"), 2)
                for j in range(4):
                    pr = 4 * q + j
                    outs = [o[0:SC, b, j * P:(j + 1) * P] for b in range(2)]
                    for b in range(2):
                        pe.matmul(outs[b], U[:, 2 * pr + b, NS:UC], TT[:, 2 * pr + b], start=True, stop=False)
                    for h_, g_ in ((HR, GR), (HI, GI)):
                        for b in range(2):
                            half = slice(64 * b, 64 * b + 64)
                            mm = pe.matmul(outs[b], h_[half, pr], g_[half, pr, 1:L + 1], start=False, stop=h_ is HI)
                full(mm)
            for kc in range(KC):
                ring.wait_emptied(pe, "y", kc)
                o = slot("yT", kc)
                transposes(("yT", kc), [(o[:, l // 4, (l % 4) * SC:(l % 4 + 1) * SC],
                                         YK[0:SC, l, kc * P:(kc + 1) * P]) for l in range(L)])
            for kc in range(KC):
                ring.wait_emptied(pe, "yT", kc)
            def glu(ch, i):
                ring.wait_free(pe, "gl", ch, i)
                o = slot("gl", ch, i)
                n = ROWS[i]
                if i == TILES:
                    full(sample_product(o, YT, WGL[ch]))
                    return
                for kc in range(KC):
                    if i == 0 and kc % 4 == 0:
                        pe.wait_ge(sem(f"w_glu_in_{2 if ch else kc // 4}"), 16)
                    for b in range(2):
                        mm = pe.matmul(o[0:n, b, :], YT[:, kc, i * P:i * P + n],
                                       WGL[ch][:, kc, b * 512:(b + 1) * 512], start=kc == 0, stop=kc == KC - 1)
                full(mm)
            for i in range(5):
                glu(0, i)
            router(1, lambda i: glu(1, i))
            experts(1)

        def norm_squares(act, n, X_ready):
            junk = place(A + (0 if n else 5120), D)
            for i in range(5):
                X_ready(i)
                tile_squares(act, n, i, junk)
            norm_root(act, n)

        def tile_squares(act, n, i, junk):
            nc.scalar.activation(junk, X[:, i, :], ACT.Square, accum_out=ss[:, i:i + 1]).then_inc(sem("squares"), 1)
            act.wait_ge(sem("squares"), 5 * n + i + 1)

        def norm_root(act, n):
            act.wait_ge(sem("var_ready"), n + 1)
            nc.scalar.activation(root, var, ACT.Sqrt).then_inc(sem("root_ready"), 1)

        def norm_recip(dve, step, n):
            v = nc.vector
            dve.wait_ge(sem("squares"), 5 * n + 5)
            v.tensor_scalar(var, ss, 1.0 / D, EPS, ALU.mult, ALU.add).then_inc(sem("var_ready"), 1)
            dve.wait_ge(sem("root_ready"), n + 1)
            step(v.reciprocal(rstd, root))

        def norm_scale(dve, step, n, out):
            v = nc.vector
            norm_recip(dve, step, n)
            dve.wait_ge(sem("norm_in"), 16 * n + 16)
            for i in range(5):
                v.scalar_tensor_tensor(out[:, i, :], X[:, i, :], rstd[:, i:i + 1], GB, ALU.mult, ALU.mult
                                       ).then_inc(sem(f"h_{n}"), 1)
                dve.wait_ge(sem(f"h_{n}"), i + 1)

        def recut(eng, step, copy, odd):
            def u_out(q):
                take(eng, "u", q)
                give(eng, copy(U[:, 8 * q:8 * q + 8].rearrange("p (b j) n -> p b (j n)", b=2),
                               slot("u", q)[:, :, 0:4 * UC]), "u", q)
            for q in range(odd, 8, 2):
                if q >= 2:
                    ring.wait_full(eng, "u", q - 2)
                copy(XR[odd].rearrange("p (g l c) -> p l g c", g=8, l=L),
                     XK[:, :, q * P:(q + 1) * P].rearrange("p l (g c) -> p l g c", c=CW)
                     ).then_inc(sem(f"xr_ready_{odd}"), 1)
                if q >= 2:
                    u_out(q - 2)
            u_out(6 + odd)

        def cmul(tt, outr, outi, ar_, ai_, br_, bi_, x1, x2, sign=1):
            tt(x1, ai_, bi_, ALU.mult)
            tt(outr, ar_, br_, ALU.mult)
            tt(outr, outr, x1, ALU.subtract if sign > 0 else ALU.add)
            tt(x2, ar_, bi_, ALU.mult)
            tt(outi, ai_, br_, ALU.mult)
            tt(outi, outi, x2, ALU.add if sign > 0 else ALU.subtract)

        ls, lr, li_, a_, th, mag8, shalf, cs, lbr, lbi = sp_[:10]
        aa, den_, qr_, qi_, t1, t2, ur, ui, nn = sp_[10:19]

        def make_bd(eng, step, on, q):
            step(on.memset(BD[q], 0.0))
            for g2 in range(2):
                step(on.tensor_copy(BD[q][64 * g2:64 * g2 + 64, :, CW * g2:CW * g2 + CW],
                                    (BBR, BBI)[q][64 * g2:64 * g2 + 64]))
            eng.sem_inc(sem("bd_ready"), 1)

        def phases(tt, m):
            ur_, ui_ = UNIT[m.bit_length() - 1]
            cmul(tt, TC[:, :, m:2 * m], TS[:, :, m:2 * m], TC[:, :, 0:m], TS[:, :, 0:m], spread(ur_, m),
                 spread(ui_, m), TMP[:, :, 0:m], TMP[:, :, m:2 * m])

        def store_normed(act, n, src, done):
            for i in range(5):
                act.wait_ge(sem(f"h_{n}"), i + 1)
                act.dma_start(hd[i * P:i * P + ROWS[i], :], tile_rows(src, i)).then_inc(sem(done), 16)

        @block.scalar
        def _(act):
            a = nc.scalar
            chain = [0]

            def step(ins):
                chain[0] += 1
                ins.then_inc(sem("act_steps"), 1)
                act.wait_ge(sem("act_steps"), chain[0])

            act.sem_inc(sem("m_copied"), 1)
            for l in range(2):
                for s in range(2):
                    act.sem_inc(sem(f"y_out_{l}_{s}"), 16)

            def x_in(i):
                if i == TILES:
                    act.wait_ge(sem("x_cleared"), 1)
                act.wait_ge(sem(f"x_in_{i}"), 16)

            norm_squares(act, 0, x_in)
            for i in (1, 3):
                take(act, "ht", i)
                give(act, a.copy(HT[:, :, i * P:(i + 1) * P], slot("ht", i).rearrange("p b (k n) -> p (b k) n", n=P)),
                     "ht", i)
            act.wait_ge(sem("f_in"), 1)
            step(a.activation(er, lf, ACT.Abs))
            step(a.activation(er, er, ACT.Exp, scale=-1.0))
            a.activation(tr_, er, ACT.Ln, bias=1.0).then_inc(sem("softplus"), 1)

            def z_out(n, dst, func=ACT.Copy, scale=1.0):
                take(act, "z", n)
                give(act, a.activation(dst.rearrange("p (b n) -> p b n", b=2), slot("z", n)[:, :, 0:HALF], func,
                                       scale=scale), "z", n)

            for n in range(4):
                take(act, "z", n)
                src = slot("z", n)
                if n == 0:
                    act.wait_ge(sem("ue_cleared"), 1)
                step(a.copy(UE[:, n, CW:CW + HALF], src[:, 0, 0:HALF]))
                step(a.copy(UE[:, n, CW + HALF:CW + SEQ], src[:, 1, 0:SEQ - HALF]))
                give(act, a.copy(us[:, n], src[:, 1, SEQ - HALF:HALF]), "z", n)
            for n in range(4):
                z_out(4 + n, Zk[:, n], scale=KSCALE)
            act.wait_ge(sem("exps_in"), 1)
            step(a.activation(wi[:, 0:SEQ], wi[:, 0:SEQ], ACT.Exp))
            a.activation(er[:, 0:SEQ], er[:, 0:SEQ], ACT.Exp).then_inc(sem("exps_out"), 1)
            for n in range(4):
                z_out(8 + n, Zq[:, n])
            for n in range(4):
                z_out(12 + n, Zv[:, n])
            act.wait_ge(sem("sm_in"), 1)
            a.activation(SM, SM, ACT.Exp).then_inc(sem("sm_out"), 1)
            for h in range(H):
                act.wait_ge(sem("w_in_exp"), h + 1)
                for c in range(TILES):
                    ins = a.activation(W[:, h, c], W[:, h, c], ACT.Exp, bias=gcol[:, H * c + h:H * c + h + 1])
                ins.then_inc(sem("w_exp"), 1)
                act.wait_ge(sem("w_exp"), h + 1)
            for n in range(4):
                z_out(16 + n, Zo[:, n], ACT.Sigmoid)
            for g in range(4):
                take(act, "pw", g)
                give(act, a.activation(MIX[:, g].rearrange("p (b n) -> p b n", b=2), slot("pw", g)[:, :, 0:HALF],
                                       ACT.Copy, scale=pscale[:, g:g + 1]), "pw", g)
            act.wait_ge(sem("s5_in"), 96)
            step(a.activation(sp_[0], sp_[0], ACT.Exp))
            act.sem_inc(sem("s5_dt"), 1)
            act.wait_ge(sem("s5_ath"), 1)
            step(a.activation(sp_[5], sp_[3], ACT.Exp, scale=float(L)))
            step(a.activation(sp_[3], sp_[3], ACT.Exp))
            step(a.activation(sp_[6], sp_[4], ACT.Sin, scale=0.5))
            step(a.activation(sp_[4], sp_[4], ACT.Sin))
            act.sem_inc(sem("s5_sin"), 1)

            def router(l, before):
                n = 2 * l + 1
                for i in range(5):
                    before(i)
                    act.wait_ge(sem("x_tile"), 10 * l + i + 1)
                    tile_squares(act, n, i, place(A + 31040, D))
                    take(act, "tr", l, i)
                    m = ROWS[i]
                    give(act, a.copy(HTB[l][i % 2][:, :, 0:m],
                                     slot("tr", l, i).rearrange("p b (k n) -> p (b k) n", n=P)[:, :, 0:m]),
                         "tr", l, i)
                norm_root(act, n)
                act.wait_ge(sem("x_mixed"), l + 1)
                act.wait_ge(sem("rstd_ready"), l + 1)
                for i in range(5):
                    a.activation(HB[:, i], X[:, i], ACT.Copy, scale=rstd[:, i:i + 1]).then_inc(sem("h_scaled"), 1)
                act.wait_ge(sem("dg_ready"), l + 1)
                a.activation(gexp, gexp, ACT.Exp).then_inc(sem("gexp_ready"), 1)
                act.wait_ge(sem("d12_ready"), l + 1)
                a.activation(dexp, dexp, ACT.Exp).then_inc(sem("dexp_ready"), 1)
                store_normed(act, n, HB, f"h_out_{l}")

            def experts(l):
                def turns(r):
                    if not isinstance(r, int):
                        for i in range(5):
                            act.wait_ge(sem(f"yg_in_{l}_{i}"), 32 * r)
                    act.sem_inc(sem("round_marks"), 1)
                    with act.Fori(0, E // 2) as k:
                        t = k + 16 * r
                        for s in range(2):
                            act.wait_ge(sem(f"xt_done_{l}"), 2 * t + s + 3)
                            a.copy(XT[s], ps[:, s, :].rearrange("p (b n) -> p b n", b=4)
                                   ).then_inc(sem(f"xt_ready_{l}"), 1)
                        for s in range(2):
                            act.wait_ge(sem(f"gu_done_{l}"), 2 * t + s + 3)
                            act.wait_ge(sem(f"act_ready_{l}"), 2 * t + 2)
                            a.activation(SIL[s], ps[:, 2 + s, 0:P], ACT.Silu).then_inc(sem(f"silu_{l}"), 1)
                        for s in range(2):
                            act.wait_ge(sem(f"y_ready_{l}"), 2 * t + s + 3)
                            e = 2 * k + s
                            act.dma_start(yd[bass.ds(e, 1)].rearrange("e t (h c) -> h (e t) c", h=2), YE[s]
                                          ).then_inc(sem(f"y_out_{l}_{s}"), 16)
                        if l == 0:
                            act.wait_ge(sem("m_turned"), t + 2)
                            a.copy(M[:, bass.ds(2 * k, 2)].rearrange("p j r n -> p j (r n)"), ps[:, 4:6, P:3 * P]
                                   ).then_inc(sem("m_copied"), 1)
                    for s in range(2):
                        act.wait_ge(sem(f"y_out_{l}_{s}"), 256 * r + 272)
                    act.sem_inc(sem(f"y_all_out_{l}"), 1)
                turns(0)
                n = act.value_load(most[0:1, l:l + 1], min_val=0, max_val=NT)
                with act.If(n > CAP):
                    with act.Fori(1, ROUNDS) as r:
                        with act.If(n > r * CAP):
                            turns(r)

            router(0, lambda i: None)
            experts(0)
            norm_squares(act, 2, lambda i: act.wait_ge(sem("x_tile"), 5 + i + 1))
            act.wait_ge(sem("xk_in"), 96)
            ring.wait_full(act, "k")
            recut(act, step, a.copy, 1)
            act.wait_ge(sem("states_in"), 3)

            def y_out(q):
                take(act, "y", q)
                step(a.copy(*y_views(q, 0)))
                give(act, a.copy(*y_views(q, 1)), "y", q)
            for q in range(1, 8, 2):
                y_out(q)
            for kc in range(KC):
                take(act, "yT", kc)
                src = slot("yT", kc)
                if kc == 0:
                    ring.wait_full(act, "y", 7)
                step(a.activation(YT[:, kc, 0:SEQ].rearrange("p (k b l) -> p b l k", b=2, l=4),
                                  src[:, :, 0:4 * SC].rearrange("p b (l k) -> p b l k", l=4)[:, :, :, 0:NCH],
                                  ACT.Gelu_apprx_tanh))
                give(act, a.activation(YT[:, kc, SEQ:NT], src[:, 0, NCH:SC], ACT.Gelu_apprx_tanh), "yT", kc)
            def gate(ch, i):
                take(act, "gl", ch, i)
                q = 5 * ch + i
                if q >= 2:
                    act.wait_ge(sem("sig_used"), q - 1)
                if i == TILES:
                    act.wait_ge(sem("summed"), ch + 1)
                a.activation(SIG[q % 2][0:ROWS[i]], SUM[:, 1] if i == TILES else slot("gl", ch, i)[:, 1, :], ACT.Sigmoid
                             ).then_inc(sem("sig_ready"), 1)
            for i in range(5):
                gate(0, i)
            gate(1, 0)
            router(1, lambda i: gate(1, i + 1) if i < 4 else None)
            experts(1)
            norm_squares(act, 4, lambda i: act.wait_ge(sem("x_tile"), 15 + i + 1))

        @block.vector
        def _(dve):
            v = nc.vector
            chain = [0]

            def step(ins):
                chain[0] += 1
                ins.then_inc(sem("dve_steps"), 1)
                dve.wait_ge(sem("dve_steps"), chain[0])

            def tt(out, a, b, op):
                step(v.tensor_tensor(out, a, b, op))

            def ts(out, a, s1, s2, op0, op1=ALU.bypass):
                step(v.tensor_scalar(out, a, s1, s2, op0, op1))

            def stt(out, a, s, b, op0, op1):
                step(v.scalar_tensor_tensor(out, a, s, b, op0, op1))

            for l in range(2):
                for name in ("act_ready", "y_ready"):
                    dve.sem_inc(sem(f"{name}_{l}"), 2)
            v.memset(X[:, TILES, :], 0.0).then_inc(sem("x_cleared"), 1)
            norm_scale(dve, step, 0, HH)
            for i in (0, 2, 4):
                take(dve, "ht", i)
                n = ROWS[i]
                give(dve, v.tensor_copy(HT[:, :, i * P:i * P + n],
                                        slot("ht", i).rearrange("p b (k n) -> p (b k) n", n=P)[:, :, 0:n]), "ht", i)
            step(v.memset(UE[:, :, 0:CW], 0.0))
            dve.sem_inc(sem("ue_cleared"), 1)
            take(dve, "gates")
            dve.wait_ge(sem("small_in"), 16 * 8)
            for l in range(2):
                tt(WR[l], WR[l], spread(GK[:, l], 36), ALU.mult)
            g = slot("gates")
            ts(li.rearrange("p (b n) -> p b n", b=2), g[0:H, :, 0:HALF], bg[:, 0:1], None, ALU.add)
            give(dve, v.tensor_copy(lf.rearrange("p (b n) -> p b n", b=2), g[32:32 + H, :, 0:HALF]), "gates")
            ts(lf, lf, bg[:, 1:2], None, ALU.add)
            dve.sem_inc(sem("f_in"), 1)
            dve.wait_ge(sem("softplus"), 1)
            stt(lf, lf, 0.0, tr_, ALU.min, ALU.subtract)
            dve.wait_ge(sem("consts"), 16)
            step(v.tensor_tensor_scan(bc_[:, 0:SEQ], const("keep", H), lf[:, 0:SEQ], 0.0, ALU.mult, ALU.add))
            tt(ar[:, 0:SEQ], li[:, 0:SEQ], bc_[:, 0:SEQ], ALU.subtract)
            step(v.memset(mrun, 0.0))
            for c in range(TILES):
                cc = slice(c * P, (c + 1) * P)
                e = (c + 1) * P - 1
                step(v.tensor_tensor_scan(mr[:, cc], ar[:, cc], ar[:, cc], mrun[:, c:c + 1], ALU.max, ALU.max))
                tt(mrun[:, c + 1:c + 2], bc_[:, e:e + 1], mr[:, e:e + 1], ALU.add)
                ts(wi[:, cc], mr[:, cc], -1.0, mrun[:, c:c + 1], ALU.mult, ALU.add)
            stt(er[:, 0:SEQ], bc_[:, 0:SEQ], -1.0, mr[:, 0:SEQ], ALU.mult, ALU.subtract)
            ts(mr[:, 0:SEQ], mr[:, 0:SEQ], -1.0, None, ALU.mult)
            dve.sem_inc(sem("exps_in"), 1)
            ring.wait_emptied(dve, "z", 3)
            take(dve, "ws")
            for g_ in range(4):
                w = 2.0 ** -(g_ + 1)
                tt(sos[:, g_], slot_flat("ws")[:, g_ * NS:(g_ + 1) * NS], us[:, g_], ALU.add)
                ins = v.scalar_tensor_tensor(DT[:, g_, SEQ:NT], sos[:, g_], w, us[:, g_], ALU.mult, ALU.subtract)
                if g_ < 3:
                    step(ins)
            give(dve, ins, "ws")
            dve.sem_inc(sem("ws_done"), 1)
            dve.wait_ge(sem("exps_out"), 1)
            dve.sem_inc(sem("gate_rows"), 1)
            take(dve, "cols")
            step(v.tensor_copy(gcol, slot_flat("cols")[:, 0:16]))
            give(dve, v.tensor_copy(ecol, slot_flat("cols")[:, 16:32]), "cols")
            take(dve, "sg")
            give(dve, v.tensor_copy(SG, slot_flat("sg")[0:NS, 0:8]), "sg")
            dve.wait_ge(sem("n0_in"), 16)
            tt(SM[:, 4:8], SG[:, 0:4], SG[:, 4:8], ALU.subtract)
            tt(SM[:, 8:12], SM[:, 4:8], m0s, ALU.max)
            tt(SM[:, 0:4], m0s, SM[:, 8:12], ALU.subtract)
            tt(SM[:, 4:8], SM[:, 4:8], SM[:, 8:12], ALU.subtract)
            tt(sden[:, 0:4], SM[:, 8:12], SG[:, 4:8], ALU.add)
            ts(SM[:, 8:12], sden[:, 0:4], -1.0, None, ALU.mult)
            dve.sem_inc(sem("sm_in"), 1)
            for h in range(H):
                take(dve, "bc", h)
                b = slot("bc", h)
                tt(W[:, h], b[:, 0, :].rearrange("p (c n) -> p c n", c=TILES), spread_mid(causal, TILES), ALU.add)
                dve.sem_inc(sem("w_in_exp"), 1)
                if h == 0:
                    ring.wait_emptied(dve, "z", 11)
                tt(QT[:, h], Zq[:, h, 0:SEQ], b[:, 1, :], ALU.mult)
                give(dve, v.tensor_copy(dec.rearrange("p (c h) -> p c h", h=H)[:, :, h],
                                        b[:, 1, :].rearrange("p (c n) -> p c n", c=TILES)[:, :, P - 1]), "bc", h)
            dve.sem_inc(sem("rows_dead"), 1)
            take(dve, "st")
            step(v.tensor_copy(ks, slot("st")[0:NS, 0, :].rearrange("p (h k) -> p h k", h=H)))
            dve.wait_ge(sem("w_exp"), H)
            sq = KB[0:NS, 0:H]
            give(dve, v.tensor_copy(sq, slot("st")[0:NS, 1, :].rearrange("p (h k) -> p h k", h=H)), "st")
            dve.wait_ge(sem("sm_out"), 1)
            tt(ks, ks, spread(SM[:, 4:8], P), ALU.mult)
            tt(n0s, n0s, spread(SM[:, 0:4], P), ALU.mult)
            tt(n0s, n0s, ks, ALU.add)
            ring.wait_emptied(dve, "z", 15)
            step(v.tensor_copy(vs, Zv[:, :, SEQ:NT]))
            step(v.memset(V1[:, :, :, P:P + 1], 1.0))
            for c in range(TILES):
                take(dve, "kt", c)
                kt = slot("kt", c)
                for h in range(H):
                    ts(KT[:, c, h], kt[:, 0, h * P:(h + 1) * P], W[:, h, c, P - 1:P], None, ALU.mult)
                give(dve, v.tensor_copy(V1[:, c, :, 0:P], kt[:, 1, :].rearrange("p (h k) -> p h k", h=H)), "kt", c)
                take(dve, "s", c)
                give(dve, v.tensor_tensor(W[:, :, c, :], slot("s", c)[:, 0, :].rearrange("p (h k) -> p h k", h=H),
                                          W[:, :, c, :], ALU.mult), "s", c)
                take(dve, "kv", c)
                kv = slot("kv", c)
                for h in range(H):
                    src = kv[:, h // 2, (h % 2) * 129:(h % 2) * 129 + 129]
                    if c == 0:
                        if h == 0:
                            dve.wait_ge(sem("kz_out"), 16)
                        ins = v.tensor_copy(CN[:, 0, h], src)
                    else:
                        ins = v.scalar_tensor_tensor(CN[:, c, h], CN[:, c - 1, h], dec[:, H * c + h:H * c + h + 1],
                                                     src, ALU.mult, ALU.add)
                    if h < H - 1:
                        step(ins)
                give(dve, ins, "kv", c)
            dve.sem_inc(sem("cn_ready"), 1)
            prod = KB[0:NS, H:2 * H]
            tt(prod, n0s, sq, ALU.mult)
            step(v.tensor_reduce(sden[:, 4:8], prod, AX, ALU.add))
            stt(sden[:, 8:12], sden[:, 4:8], -1.0, sden[:, 4:8], ALU.mult, ALU.max)
            tt(sden[:, 8:12], sden[:, 8:12], SM[:, 8:12], ALU.max)
            step(v.reciprocal(sden[:, 4:8], sden[:, 8:12]))
            tt(qs, sq, spread(sden[:, 4:8], P), ALU.mult)
            dve.sem_inc(sem("ks_ready"), 1)
            for c in range(TILES):
                take(dve, "num", c)
                nm = slot("num", c)
                step(v.tensor_copy(den.rearrange("p (a b) -> p a b", a=2),
                                   nm[:, :, 0:258].rearrange("p a (b n) -> p a b n", b=2)[:, :, :, P]))
                stt(dab, den, -1.0, den, ALU.mult, ALU.max)
                tt(dab, dab, ecol[:, H * c:H * c + H], ALU.max)
                step(v.reciprocal(rden, dab))
                for h in range(H):
                    ins = v.tensor_scalar(HM[:, c, h], nm[:, h // 2, (h % 2) * 129:(h % 2) * 129 + P],
                                          rden[:, h:h + 1], None, ALU.mult)
                    if h < H - 1:
                        step(ins)
                give(dve, ins, "num", c)
            ring.wait_emptied(dve, "z", 19)
            for c in range(TILES):
                take(dve, "hT", c)
                give(dve, v.tensor_tensor(MIX[:, H:2 * H, c * P:(c + 1) * P],
                                          slot("hT", c)[:, 0, :].rearrange("p (h n) -> p h n", h=H),
                                          Zo[:, :, c * P:(c + 1) * P], ALU.mult), "hT", c)
            def logits_out(l, i):
                take(dve, "lg", l, i)
                n = ROWS[i]
                give(dve, v.tensor_copy(LG[0:n, i], slot_flat("lg", l, i)[0:n, 0:36]), "lg", l, i)

            def sum_parts(out, fresh, *job):
                o = slot(*job)
                for q in range(4):
                    part = o[32 * q:32 * q + NS]
                    if q == 0 and fresh:
                        ins = v.tensor_copy(out, part)
                    else:
                        ins = v.tensor_tensor(out, out, part, ALU.add)
                    if q < 3:
                        step(ins)
                give(dve, ins, *job)

            def mixed(i):
                take(dve, "wo", i)
                n = ROWS[i]
                if i == TILES:
                    sum_parts(X[0:n, i, :].rearrange("p (b n) -> p b n", b=2), False, "wo", i)
                else:
                    give(dve, v.tensor_tensor(X[0:n, i, :], X[0:n, i, :], slot_flat("wo", i)[0:n], ALU.add), "wo", i)
                dve.sem_inc(sem("x_tile"), 1)
                if i >= 2:
                    logits_out(0, i - 2)
            step(v.memset(LG, 0.0))
            dve.wait_ge(sem("kb_in"), 32)
            dve.wait_ge(sem("c0_in"), 16)
            tt(CS, CS, spread(DB, P), ALU.mult)
            kb4 = KB.rearrange("p (n h) k -> p n h k", h=H)
            tt(kb4, kb4, spread(vs.rearrange("p h n -> p n h"), P), ALU.mult)
            tt(CS, CS, KB, ALU.add)
            dve.sem_inc(sem("kb_used"), 1)
            dve.wait_ge(sem("s5_in"), 96)
            lr2, li2 = GTMP[:, 0, 0:2].rearrange("p l c -> p (l c)"), GTMP[:, 0, 2:4].rearrange("p l c -> p (l c)")
            tt(lr2, lr, lr, ALU.mult)
            tt(li2, li_, li_, ALU.mult)
            tt(lr2, lr2, li2, ALU.add)
            step(v.reciprocal(den_, lr2))
            dve.sem_inc(sem("s5_den"), 1)
            mixed(0)
            mixed(1)
            dve.wait_ge(sem("kb_in"), 48)
            tt(KB, KB, CS, ALU.mult)
            step(v.tensor_reduce(rs, KB, AX, ALU.add))
            tt(MIX[:, H:2 * H, SEQ:NT], rs.rearrange("p (n h) -> p h n", h=H), Zo[:, :, SEQ:NT], ALU.mult)
            dve.sem_inc(sem("mix_samples"), 1)
            for i in range(2, 5):
                mixed(i)
            dve.wait_ge(sem("stored"), 16 * 8)
            dve.wait_ge(sem("s5_ready"), 1)
            dve.sem_inc(sem("x_mixed"), 1)

            def router(l):
                norm_recip(dve, step, 2 * l + 1)
                dve.sem_inc(sem("rstd_ready"), 1)
                for i in (3, 4):
                    logits_out(l, i)
                tt(LG, LG, spread(rstd, 36), ALU.mult)
                tt(LG, LG, spread_mid(BR[l], 5), ALU.add)
                gl, el = LG[:, :, 0:4], LG[:, :, 4:36]

                def first_of(values, top, rev, out):
                    n = values.shape[-1]
                    step(v.tensor_reduce(top, values, AX, ALU.max))
                    tt(out, values, spread(top, n), ALU.is_equal)
                    tt(out, out, spread_mid(rev, 5), ALU.mult)
                    step(v.tensor_reduce(etop, out, AX, ALU.max))
                    tt(out, out, spread(etop, n), ALU.is_equal)

                first_of(gl, gmax, const("revg"), og)
                tt(gexp, gl, spread(gmax, 4), ALU.subtract)
                dve.sem_inc(sem("dg_ready"), 1)
                ts(gneg, og, BIG, -BIG, ALU.mult, ALU.add)
                tt(me.rearrange("p t (g k) -> p t g k", g=4), el.rearrange("p t (g k) -> p t g k", g=4),
                   spread(gneg, 8), ALU.add)
                first_of(me, m1, const("reve"), oh[0])
                stt(me, oh[0], -2 * BIG, me, ALU.mult, ALU.add)
                first_of(me, m2, const("reve"), oh[1])
                tt(dexp, m2, m1, ALU.subtract)
                dve.sem_inc(sem("d12_ready"), 1)
                for j in range(2):
                    tt(oh[j], oh[j], spread(const("valid"), E), ALU.mult)
                tt(OH, oh[0], oh[1], ALU.add)
                step(v.memset(PRE[:, 0], 0.0))
                for i in range(1, 5):
                    tt(PRE[:, i], PRE[:, i - 1], OH[:, i - 1], ALU.add)
                tt(both, PRE[:, 4], OH[:, 4], ALU.add)
                dve.sem_inc(sem("chosen"), 1)
                dve.wait_ge(sem("gexp_ready"), l + 1)
                step(v.tensor_reduce(gsum, gexp, AX, ALU.add))
                step(v.reciprocal(gw, gsum))
                dve.wait_ge(sem("dexp_ready"), l + 1)
                ts(dsum, dexp, 1.0, None, ALU.add)
                step(v.reciprocal(dsum, dsum))
                tt(pw_[0], dsum, gw, ALU.mult)
                tt(pw_[1], pw_[0], dexp, ALU.mult)
                take(dve, "pos", l)
                o = slot("pos", l)
                step(v.tensor_copy(POS, o[:, 0, 0:5 * E].rearrange("p (t e) -> p t e", t=5)))
                step(v.tensor_reduce(cntmax, o[:, 1, 0:E], AX, ALU.max))
                give(dve, v.tensor_copy(most[:, l:l + 1], cntmax), "pos", l)
                dve.sem_inc(sem("most_ready"), 1)
                for j in range(2):
                    tt(hit, oh[j], POS, ALU.mult)
                    step(v.tensor_reduce(RK[:, j], hit, AX, ALU.add))
                    tt(hit, oh[j], spread_mid(const("eio"), 5), ALU.mult)
                    step(v.tensor_reduce(EID[:, j], hit, AX, ALU.add))
                    tt(oh[j], oh[j], spread(const("tokid"), E), ALU.mult)
                ts(EID, EID, float(CAP), None, ALU.mult)

            def experts(l):
                def turns(r):
                    n = 19

                    def lstep(ins, k):
                        ins.then_inc(sem(f"list_steps_{l}"), 1)
                        dve.wait_ge(sem(f"list_steps_{l}"), n * r + k)

                    for q in range(10):
                        v.tensor_scalar(OHR[:, q], const("iota"), RK.rearrange("p j t -> p (j t)")[:, q:q + 1], None,
                                        ALU.is_equal).then_inc(sem(f"list_steps_{l}"), 1)
                    dve.wait_ge(sem(f"list_steps_{l}"), n * r + 10)
                    dve.sem_inc(sem(f"spots_{l}"), 1)
                    lstep(v.tensor_scalar(QR, RK, 0.0, None, ALU.is_ge), 11)
                    lstep(v.scalar_tensor_tensor(QR, RK, float(CAP), QR, ALU.is_lt, ALU.mult), 12)
                    lstep(v.tensor_scalar(QR, QR, -1e5, 1e5, ALU.mult, ALU.add), 13)
                    lstep(v.tensor_tensor(QR, QR, EID, ALU.add), 14)
                    lstep(v.tensor_tensor(idx_back[:, :], QR.rearrange("p j t -> p (j t)"),
                                          RK.rearrange("p j t -> p (j t)"), ALU.add), 15)
                    lstep(v.tensor_scalar(RK, RK, -float(CAP), None, ALU.add), 16)
                    dve.wait_ge(sem(f"list_done_{l}"), r + 1)
                    lstep(v.tensor_scalar(both, ps[:, 0, 0:E], 0.0, 4096.0, ALU.is_equal, ALU.mult), 17)
                    lstep(v.scalar_tensor_tensor(both, ps[:, 0, 0:E], 2.0, both, ALU.mult, ALU.add), 18)
                    lstep(v.tensor_scalar(idx_list[:, :], both, const("half"), None, ALU.add), 19)
                    dve.sem_inc(sem(f"list_read_{l}"), 1)
                    with dve.Fori(0, E // 2) as k:
                        t = k + 16 * r
                        for s in range(2):
                            dve.wait_ge(sem(f"silu_{l}"), 2 * t + s + 1)
                            v.tensor_tensor(ACTB[s], SIL[s], ps[:, 2 + s, P:2 * P], ALU.mult
                                            ).then_inc(sem(f"act_ready_{l}"), 1)
                        for s in range(2):
                            dve.wait_ge(sem(f"at_done_{l}"), 2 * t + s + 1)
                            v.tensor_copy(AT[s], ps[:, 4 + s, 0:P]).then_inc(sem(f"at_ready_{l}"), 1)
                        for s in range(2):
                            dve.wait_ge(sem(f"down_done_{l}"), 2 * t + s + 3)
                            dve.wait_ge(sem(f"y_out_{l}_{s}"), 16 * t + 16)
                            v.tensor_copy(YE[s], ps[:, 6 + s, :]).then_inc(sem(f"y_ready_{l}"), 1)
                    for q in range(10):
                        i, j, m = q // 2, q % 2, ROWS[q // 2]
                        dve.wait_ge(sem(f"yg_in_{l}_{i}"), 32 * r + 32)
                        v.scalar_tensor_tensor(X[0:m, i, :], YG[l][0:m, q if l else 2 * (i % 2) + j], pw_[j][0:m, i:i + 1], X[0:m, i, :],
                                               ALU.mult, ALU.add).then_inc(sem(f"combined_{l}"), 1)
                        dve.wait_ge(sem(f"combined_{l}"), 10 * r + q + 1)
                    dve.sem_inc(sem("round_marks"), 1)
                turns(0)
                n = dve.value_load(most[0:1, l:l + 1], min_val=0, max_val=NT)
                with dve.If(n > CAP):
                    with dve.Fori(1, ROUNDS) as r:
                        with dve.If(n > r * CAP):
                            turns(r)
                for i in range(5):
                    dve.sem_inc(sem("x_tile"), 1)
                dve.sem_inc(sem("x_moe"), 1)

            router(0)
            experts(0)

            step(v.memset(XK[:, 0:L // 2], 0.0))
            dve.sem_inc(sem("xk_cleared"), 1)
            make_bd(dve, step, v, 1)
            norm_scale(dve, step, 2, H2)
            take(dve, "k")
            give(dve, v.tensor_copy(KS.rearrange("p a b -> p (a b)"), slot_flat("k")), "k")
            tt(SKIP, spread_mid(const("diag"), KC), spread(DSK, CW), ALU.mult)
            tt(KS[:, :, 0:CW], KS[:, :, 0:CW], SKIP, ALU.add)
            dve.sem_inc(sem("taps_ready"), 1)
            dve.wait_ge(sem("xk_in"), 96)
            recut(dve, step, v.tensor_copy, 0)
            ring.wait_full(dve, "u", 7)
            dve.wait_ge(sem("phases_ready"), 1)
            phases(tt, NCH // 2)
            step(v.tensor_copy(R8, spread(mag8, NCH)))
            step(v.memset(R8[:, :, 0:1], 0.0))
            dve.wait_ge(sem("phases_ready"), 2)
            for q in range(8):
                take(dve, "zs", q)
                z = slot("zs", q)[:, :, 0:4 * SC].rearrange("p r (j n) -> p r j n", j=4)
                zr, zi = z[:, 0, :, NS:SC], z[:, 1, :, NS:SC]
                rr, ri, tc, ts_ = (b[:, 4 * q:4 * q + 4] for b in (RR, RI, TC, TS))
                tm = TMQ
                tt(rr, zr, tc, ALU.mult)
                tt(tm, zi, ts_, ALU.mult)
                tt(rr, rr, tm, ALU.add)
                tt(ri, zi, tc, ALU.mult)
                tt(tm, zr, ts_, ALU.mult)
                tt(ri, ri, tm, ALU.subtract)
                sr, si = SHR[:, 4 * q:4 * q + 4], SHI[:, 4 * q:4 * q + 4]
                tt(sr, sr, z[:, 0, :, 0:NS], ALU.add)
                give(dve, v.tensor_tensor(si, si, z[:, 1, :, 0:NS], ALU.add), "zs", q)
            for b in (RR, RI):
                f = b.rearrange("p r k -> p (r k)")
                step(v.tensor_tensor_scan(f, R8.rearrange("p r k -> p (r k)"), f, 0.0, ALU.mult, ALU.add))
            n = NCH - 1
            for half in (slice(0, PAIRS // 2), slice(PAIRS // 2, PAIRS)):
                for o, h0, x, y, op in ((HR, H0R, RR, RI, ALU.subtract), (HI, H0I, RI, RR, ALU.add)):
                    o, x, y, tc, ts_, tm = (b[:, half] for b in (o, x, y, TC, TS, TMP))
                    step(v.memset(o[:, :, 0:1], 0.0))
                    tt(o[:, :, 1:NCH], x[:, :, 0:n], tc[:, :, 0:n], ALU.mult)
                    tt(tm[:, :, 0:n], y[:, :, 0:n], ts_[:, :, 0:n], ALU.mult)
                    tt(o[:, :, 1:NCH], o[:, :, 1:NCH], tm[:, :, 0:n], op)
                    step(v.tensor_copy(o[:, :, NCH:SC], h0.rearrange("p (r n) -> p r n", n=NS)[:, half]))
                dve.sem_inc(sem("states_in"), 1)
            for q, (x, y, op) in enumerate(((RR, RI, ALU.subtract), (RI, RR, ALU.add))):
                last = TMQ[:, 0, 0:PAIRS]
                tt(HEND[:, q], x[:, :, n], TC[:, :, n], ALU.mult)
                tt(last, y[:, :, n], TS[:, :, n], ALU.mult)
                tt(HEND[:, q], HEND[:, q], last, op)
            dve.sem_inc(sem("states_in"), 1)
            for q in range(0, 8, 2):
                take(dve, "y", q)
                step(v.tensor_copy(*y_views(q, 0)))
                give(dve, v.tensor_copy(*y_views(q, 1)), "y", q)
            step(v.memset(LG, 0.0))
            for ch in range(2):
                for i in range(5):
                    q = 5 * ch + i
                    n = ROWS[i]
                    take(dve, "gl", ch, i)
                    if i == TILES:
                        if ch:
                            dve.wait_ge(sem("sig_used"), 5)
                        sum_parts(SUM, True, "gl", ch, i)
                        dve.sem_inc(sem("summed"), 1)
                        dve.wait_ge(sem("sig_ready"), q + 1)
                        tt(GT[q % 2][0:n], SUM[:, 0], SIG[q % 2][0:n], ALU.mult)
                    else:
                        dve.wait_ge(sem("sig_ready"), q + 1)
                        ins = v.tensor_tensor(GT[q % 2][0:n], slot("gl", ch, i)[0:n, 0, :], SIG[q % 2][0:n], ALU.mult)
                        give(dve, ins, "gl", ch, i)
                    dve.sem_inc(sem("sig_used"), 1)
                    xs = X[0:n, i, 512 * ch:512 * ch + 512]
                    tt(xs, xs, GT[q % 2][0:n], ALU.add)
                    if ch:
                        dve.sem_inc(sem("x_tile"), 1)
                        if i >= 2:
                            logits_out(1, i - 2)
            dve.wait_ge(sem("stored"), 16 * 11)
            dve.sem_inc(sem("x_mixed"), 1)
            router(1)
            experts(1)
            norm_scale(dve, step, 4, HC)

        @block.gpsimd
        def _(pool):
            g_ = nc.gpsimd
            chain = [0]

            def step(ins):
                chain[0] += 1
                ins.then_inc(sem("pool_steps"), 1)
                pool.wait_ge(sem("pool_steps"), chain[0])

            step(g_.memset(KZ, 0.0))
            pool.sem_inc(sem("kz_cleared"), 1)
            ring.wait_emptied(pool, "z", 3)
            ring.wait_full(pool, "ws")
            for g in range(4):
                src = UE[:, g]
                for q in range(g + 1):
                    d = 2 ** q
                    dst = TU[q % 2]
                    step(g_.tensor_tensor(dst[:, 2 * d - 1:528], src[:, 2 * d - 1:528], src[:, d - 1:528 - d], ALU.add))
                    src = dst
                other = TU[(g + 1) % 2]
                step(g_.tensor_scalar(other[:, CW:528], src[:, CW:528], 2.0 ** -(g + 1), None, ALU.mult))
                ramp = const("ramp")[:, CW * g:CW * g + CW]
                step(g_.tensor_tensor(other[:, CW:2 * CW], src[:, CW:2 * CW], ramp, ALU.mult))
                step(g_.tensor_tensor(DT[:, g, 0:SEQ], other[:, CW:528], UE[:, g, CW:528], ALU.subtract))
                if g == 0:
                    pool.wait_ge(sem("ws_done"), 1)
                pool.sem_inc(sem("pool_mixed"), 1)

            def tt(out, a, b, op):
                step(g_.tensor_tensor(out, a, b, op))

            def ts(out, a, s1, s2, op0, op1=ALU.bypass):
                step(g_.tensor_scalar(out, a, s1, s2, op0, op1))

            pool.wait_ge(sem("s5_dt"), 1)
            tt(a_, lr, ls, ALU.mult)
            tt(th, li_, ls, ALU.mult)
            magic = 1.5 * 2.0 ** 23
            ts(nn, th, 1.0 / (2 * pi), magic, ALU.mult, ALU.add)
            ts(nn, nn, -magic, None, ALU.add)
            c1 = 6.28125
            c2 = float(np.float32(round((2 * pi - c1) * 2 ** 21) / 2 ** 21))
            for c in (c1, c2, 2 * pi - c1 - c2):
                ts(t1, nn, -c, None, ALU.mult)
                tt(th, th, t1, ALU.add)
            ts(th, th, 3.1415925, -3.1415925, ALU.min, ALU.max)
            pool.sem_inc(sem("s5_ath"), 1)
            pool.wait_ge(sem("s5_sin"), 1)
            tt(cs, shalf, shalf, ALU.mult)
            ts(cs, cs, -2.0, 1.0, ALU.mult, ALU.add)
            tt(lbr, a_, cs, ALU.mult)
            tt(lbi, a_, th, ALU.mult)
            ts(nn, lbr, -1.0, None, ALU.add)
            cmul(tt, qr_, qi_, nn, lbi, lr, li_, t1, t2, sign=-1)
            pool.wait_ge(sem("s5_den"), 1)
            tt(qr_, qr_, den_, ALU.mult)
            tt(qi_, qi_, den_, ALU.mult)
            cmul(tt, BBR, BBI, spread(qr_, CW), spread(qi_, CW), BIN[0], BIN[1], BTMP[0], BTMP[1])
            step(g_.tensor_copy(ur, cs))
            step(g_.tensor_copy(ui, th))
            for _ in range(3):
                cmul(tt, qr_, qi_, ur, ui, ur, ui, t1, t2)
                step(g_.tensor_copy(ur, qr_))
                step(g_.tensor_copy(ui, qi_))
            tt(t1, ur, ur, ALU.mult)
            tt(t2, ui, ui, ALU.mult)
            tt(t1, t1, t2, ALU.add)
            ts(t1, t1, -0.5, 1.5, ALU.mult, ALU.add)
            tt(cs, ur, t1, ALU.mult)
            tt(th, ui, t1, ALU.mult)
            for k in range(5):
                cmul(tt, *UNIT[k + 1], *UNIT[k], *UNIT[k], t1, t2)
            step(g_.memset(PWR[:, :, 0], 1.0))
            step(g_.memset(PWI[:, :, 0], 0.0))
            for j in range(1, L + 1):
                cmul(tt, PWR[:, :, j], PWI[:, :, j], PWR[:, :, j - 1], PWI[:, :, j - 1], lbr, lbi, t1, t2)
            for j in range(L):
                step(g_.tensor_copy(BACKR[:, :, j], PWR[:, :, L - 1 - j]))
                step(g_.tensor_copy(BACKI[:, :, j], PWI[:, :, L - 1 - j]))
            pool.sem_inc(sem("s5_ready"), 1)

            def weigh(l):
                pool.wait_ge(sem("norm_in"), 16 * (2 * l + 2))
                for i in range(5):
                    pool.wait_ge(sem("h_scaled"), 5 * l + i + 1)
                    g_.tensor_tensor(HB[:, i], HB[:, i], GB, ALU.mult).then_inc(sem(f"h_{2 * l + 1}"), 1)

            def experts(l):
                for s in range(2):
                    step(g_.memset(XG[s], 0.0))
                pool.wait_ge(sem(f"h_out_{l}"), 80)
                if l == 0:
                    pool.wait_ge(sem("s5_in"), 128)
                    step(g_.tensor_scalar(CIN[1], CIN[1], -1.0, None, ALU.mult))

                def matrices(k, t):
                    done = [0]

                    def mul_add(out, a, b, c, d, op, tmp):
                        for o, x, y, f in ((out, a, b, ALU.mult), (tmp, c, d, ALU.mult), (out, out, tmp, op)):
                            done[0] += 1
                            g_.tensor_tensor(o, x, y, f).then_inc(sem("matrix_steps"), 1)
                            pool.wait_ge(sem("matrix_steps"), 12 * t + done[0])
                            pool.sem_inc(sem("turn_marks"), 1)

                    two = bass.ds(2 * k, 2)

                    def by_step(a, n):
                        return a[:, two].unsqueeze(2).broadcast_to((P, 2, n, CW))

                    pr_, pi_ = spread(PWR[:, two], CW), spread(PWI[:, two], CW)
                    cr_, nci = by_step(CIN[0], L + 1), by_step(CIN[1], L + 1)
                    mul_add(GR[:, two], pr_, cr_, pi_, nci, ALU.add, GTMP)
                    mul_add(GI[:, two], pr_, nci, pi_, cr_, ALU.subtract, GTMP)
                    pr_, pi_ = spread(BACKR[:, two], CW), spread(BACKI[:, two], CW)
                    br_, bi_ = by_step(BBR, L), by_step(BBI, L)
                    pool.wait_ge(sem("m_turned"), t + 1)
                    pool.sem_inc(sem("turn_marks"), 1)
                    mul_add(VR, pr_, br_, pi_, bi_, ALU.subtract, GTMP[:, :, 0:L])
                    mul_add(VI, pr_, bi_, pi_, br_, ALU.add, GTMP[:, :, 0:L])
                    pool.sem_inc(sem("v_ready"), 1)

                def turns(r):
                    if l and isinstance(r, int):
                        ring.wait_full(pool, "pos", l)
                        step(g_.memset(YG[l], 0.0))
                    pool.wait_ge(sem(f"list_read_{l}"), r + 1)
                    pool.sem_inc(sem("round_marks"), 1)
                    with pool.Fori(0, E // 2) as k:
                        t = k + 16 * r
                        pool.wait_ge(sem(f"xt_done_{l}"), 2 * t + 2)
                        g_.tensor_copy(idx_now[:, :], idx_list[:, bass.ds(2 * k, 2)]).then_inc(sem(f"idx_{l}"), 1)
                        pool.wait_ge(sem(f"idx_{l}"), t + 1)
                        pool.sem_inc(sem("turn_marks"), 1)
                        for s in range(2):
                            g_.indirect_dma_start(out=XG[s], out_offset=None, in_=hd_halves,
                                                  in_offset=bass.IndirectOffsetOnAxis(ap=idx_now[:, s:s + 1], axis=0),
                                                  bounds_check=2 * NT - 1, oob_is_err=False
                                                  ).then_inc(sem(f"xg_in_{l}_{s}"), 16)
                        if l == 0:
                            matrices(k, t)
                    if l == 0:
                        pool.wait_ge(sem("m_turned"), 16 * r + 17)
                    pool.sem_inc(sem("turn_marks"), 1)
                    def clear(i):
                        at = 2 * (i % 2)
                        if i >= 2:
                            pool.wait_ge(sem(f"combined_{l}"), 10 * r + 2 * i - 2)
                            pool.sem_inc(sem("turn_marks"), 1)
                        g_.memset(YG[l][:, at:at + 2], 0.0).then_inc(sem(f"yg_cleared_{l}"), 1)
                        pool.wait_ge(sem(f"yg_cleared_{l}"), 5 * r + i + 1)
                        pool.sem_inc(sem("turn_marks"), 1)

                    if l and not isinstance(r, int):
                        g_.memset(YG[l], 0.0).then_inc(sem(f"yg_cleared_{l}"), 1)
                        pool.wait_ge(sem(f"yg_cleared_{l}"), r)
                        pool.sem_inc(sem("turn_marks"), 1)
                    if l == 0:
                        clear(0)
                        clear(1)
                    pool.wait_ge(sem(f"y_all_out_{l}"), r + 1)
                    pool.sem_inc(sem("round_marks"), 1)
                    for i in range(5):
                        m = ROWS[i]
                        if l == 0 and i >= 2:
                            clear(i)
                        for j in range(2):
                            g_.indirect_dma_start(out=YG[l][0:m, 2 * i + j if l else 2 * (i % 2) + j], out_offset=None,
                                                  in_=yd_rows,
                                                  in_offset=bass.IndirectOffsetOnAxis(
                                                      ap=idx_back[0:m, 5 * j + i:5 * j + i + 1], axis=0),
                                                  bounds_check=E * CAP - 1, oob_is_err=False
                                                  ).then_inc(sem(f"yg_in_{l}_{i}"), 16)
                turns(0)
                n = pool.value_load(most[0:1, l:l + 1], min_val=0, max_val=NT)
                with pool.If(n > CAP):
                    with pool.Fori(1, ROUNDS) as r:
                        with pool.If(n > r * CAP):
                            turns(r)

            weigh(0)
            experts(0)
            pool.wait_ge(sem("x_moe"), 1)
            step(g_.memset(XK[:, L // 2:L], 0.0))
            pool.sem_inc(sem("xk_cleared"), 1)
            make_bd(pool, step, g_, 0)
            step(g_.memset(TC[:, :, 0:1], 1.0))
            step(g_.memset(TS[:, :, 0:1], 0.0))
            for k in range(5):
                phases(tt, 2 ** k)
            pool.sem_inc(sem("phases_ready"), 1)
            pool.wait_ge(sem("s5_in"), 160)
            for o, x, y, op in ((SHR, H0R, H0I, ALU.subtract), (SHI, H0I, H0R, ALU.add)):
                x, y = (z.rearrange("p (r n) -> p r n", n=NS) for z in (x, y))
                tt(o, x, spread(lbr, NS), ALU.mult)
                tt(SHT, y, spread(lbi, NS), ALU.mult)
                tt(o, o, SHT, op)
            pool.sem_inc(sem("phases_ready"), 1)
            weigh(1)
            experts(1)


_SHAPES = dict(hd=(NT, D), yd=(E, CAP, D), sdk=(NS, 512), sdq=(NS, 512), sdd=(NS, H), kp=(D, KROW))
_OUT = dict(y=(NT, D), pool_s=(NS, 14, 512), pool_p=(P, H, 15), pool_us=(P, H, NS), n_s=(NS, 512), m_s=(NS, H),
            c_s=(P, NS * H, P), cn_p=(P, H, 129), m_p=(H, 1), s5_p=(P, 2, PAIRS), s5_sr=(P, PAIRS, NS),
            s5_si=(P, PAIRS, NS))


def kernel(**inputs):
    import concourse.bacc as bacc
    from concourse.bass_utils import run_bass_kernel_spmd

    n = {k: np.asarray(a) for k, a in inputs.items()}

    def kmajor(w):
        return w.reshape(KC, P, -1).transpose(1, 0, 2)

    def rep(a):
        return np.broadcast_to(a, (P,) + a.shape)

    def groups(a):
        a = a.reshape((PAIRS, P) + a.shape[2:])
        return a.swapaxes(0, 1)

    w = n["w_in_ab"][0]
    cols = [w[:, 0:512], w[:, 1024:1536], w[:, 512:1024], w[:, 1536:2048], w[:, 2048:2560]]
    w_in = np.stack([kmajor(c[:, 256 * b:256 * b + 256]) for c in cols for b in range(2)])
    gate, up = n["moe_w_gate"], n["moe_w_up"]
    gu = np.concatenate([gate[..., 0:P], up[..., 0:P], gate[..., P:], up[..., P:]], axis=-1)
    gu = gu.reshape(2, E, KC, P, 512).transpose(0, 1, 3, 2, 4)
    down = n["moe_w_down"].reshape(2, E, 2, P, D).transpose(0, 1, 3, 2, 4)
    glu = n["w_glu"][0]
    arrays = dict(
        const=constants(), x_prompt=n["x_prompt"][0], x_sample=n["x_sample"][:, 0],
        norms=np.stack([rep(a) for a in (n["norm_mix"][0], n["norm_ffn"][0], n["norm_mix"][1], n["norm_ffn"][1],
                                         n["norm_final"])]),
        w_gate8=kmajor(w[:, 2560:2568]), b_gates=n["b_gates"][0].reshape(2, H).T, m0=n["state_mlstm_m"][0],
        pool_scale=n["pool_scale"][0].reshape(H, P).T,
        norm_ffn=n["norm_ffn"].reshape(2, KC, P).transpose(2, 0, 1),
        w_router=np.stack([kmajor(np.concatenate([n["moe_w_group"][l], n["moe_w_expert"][l]], -1)) for l in range(2)]),
        b_router=np.stack([rep(np.concatenate([n["moe_b_group"][l], n["moe_b_expert"][l]])) for l in range(2)]),
        pool_w=n["pool_w"][0].transpose(1, 0, 2), pool_rows=n["state_pool"][0].reshape(120, 512),
        pool_buf=n["state_pool"][0][:, 1:], n0=n["state_mlstm_n"][0].reshape(NS, 512), w_in=w_in,
        w_out=kmajor(n["w_out_ab"][0]), c0=n["state_mlstm_c"][0].reshape(NS * H, P, P).transpose(1, 0, 2),
        w_gu=gu, w_down=down,
        s5_cb=np.stack([groups(a) for a in (n["s5_c_re"][0].swapaxes(1, 2), n["s5_c_im"][0].swapaxes(1, 2),
                                            n["s5_b_re"][0], n["s5_b_im"][0])]),
        s5_ls=groups(np.broadcast_to(n["s5_log_step"][0][:, None], (GU, 64))),
        s5_lr=groups(n["s5_lam_re"][0]), s5_li=groups(n["s5_lam_im"][0]), s5_d=n["s5_d"][0].reshape(KC, P).T,
        s5_h0r=groups(n["state_s5_re"][0].transpose(1, 2, 0)).reshape(P, -1),
        s5_h0i=groups(n["state_s5_im"][0].transpose(1, 2, 0)).reshape(P, -1),
        w_glu=np.stack([kmajor(np.concatenate([glu[:, 512 * c:512 * c + 512], glu[:, D + 512 * c:D + 512 * c + 512]], -1))
                        for c in range(2)]),
    )
    nc = bacc.Bacc("TRN2", target_bir_lowering=False, num_devices=1)
    T, feed = {}, {}
    for k, a in arrays.items():
        feed[f"in_{k}"] = a = np.ascontiguousarray(a)
        T[k] = nc.dram_tensor(f"in_{k}", a.shape, mybir.dt.from_np(a.dtype), kind="ExternalInput").ap()
    for k, s in _OUT.items():
        T[k] = nc.dram_tensor(f"out_{k}", s, F32, kind="ExternalOutput").ap()
    for k, s in _SHAPES.items():
        T[k] = nc.dram_tensor(f"scratch_{k}", s, F32, kind="Internal").ap()
    bass_hybrid_step(nc, T)
    r = run_bass_kernel_spmd(nc, [feed], core_ids=[0]).results[0]
    o = {k: np.asarray(r[f"out_{k}"]) for k in _OUT}

    def ungroup(a):
        a = a.swapaxes(0, 1)
        return a.reshape((GU, 64) + a.shape[2:])

    us = o["pool_us"].transpose(2, 1, 0).reshape(NS, 1, 512)
    cn = o["cn_p"].transpose(1, 2, 0)
    return (o["y"][None, :SEQ], o["y"][SEQ:, None],
            o["pool_p"].transpose(2, 1, 0).reshape(1, 1, 15, 512), cn[None, None, :, :P], cn[None, None, :, P],
            o["m_p"][:, 0][None, None], ungroup(o["s5_p"][:, 0])[None, None], ungroup(o["s5_p"][:, 1])[None, None],
            np.concatenate([o["pool_s"], us], axis=1)[None],
            o["c_s"].transpose(1, 0, 2).reshape(1, NS, H, P, P), o["n_s"].reshape(1, NS, H, P), o["m_s"][None],
            ungroup(o["s5_sr"]).transpose(2, 0, 1)[None], ungroup(o["s5_si"]).transpose(2, 0, 1)[None])
```
